# Optimizing a Trainium2 kernel written in Bass

```python
import jax, jax.numpy as jnp
from jax import lax
import numpy as np
import math

D_MODEL = 1024
BATCH = 1
SEQ = 512
DEPTH = 2

N_MIXERS = 2
N_POOL_LAYERS = (DEPTH + N_MIXERS - 1) // N_MIXERS
N_MLA_LAYERS = DEPTH // N_MIXERS
EXPAND = 2
POOL_WIDTH = EXPAND * D_MODEL
POOL_WINDOWS = (2, 4, 8, 16)
N_POOL_GROUPS = len(POOL_WINDOWS)
POOL_GROUP = POOL_WIDTH // N_POOL_GROUPS
N_HEADS = 16
QK_NOPE_DIM = 128
QK_ROPE_DIM = 64
QK_HEAD_DIM = QK_NOPE_DIM + QK_ROPE_DIM
V_HEAD_DIM = 128
Q_LORA_RANK = 384
KV_LORA_RANK = 256
MLA_WIDTH = N_HEADS * V_HEAD_DIM
MLA_IN_WIDTH = Q_LORA_RANK + KV_LORA_RANK + QK_ROPE_DIM + MLA_WIDTH
ROPE_THETA = 10000.0
Q_BLOCK = 128
EPS = 1e-6


def rmsnorm(x, g):
    xf = x.astype(jnp.float32)
    inv = lax.rsqrt(jnp.mean(xf * xf, axis=-1, keepdims=True) + EPS)
    return (xf * inv).astype(x.dtype) * g

def causal_window_mean(u, w):
    S = u.shape[1]
    cs = jnp.cumsum(u.astype(jnp.float32), axis=1)
    shifted = jnp.pad(cs, ((0, 0), (w, 0), (0, 0)))[:, :S]
    count = jnp.minimum(jnp.arange(1, S + 1), w).astype(jnp.float32)
    return ((cs - shifted) / count[None, :, None]).astype(u.dtype)

def pool_layer(x, norm_g, w_in, w_group, scale, w_out):
    B, S, _ = x.shape
    h = rmsnorm(x, norm_g)
    uz = h @ w_in
    u, z = uz[..., :POOL_WIDTH], uz[..., POOL_WIDTH:]
    ug = u.reshape(B, S, N_POOL_GROUPS, POOL_GROUP)
    pooled = jnp.stack([causal_window_mean(ug[:, :, g], w)
                        for g, w in enumerate(POOL_WINDOWS)], axis=2) - ug
    mixed = jnp.einsum('bsgc,gcd->bsgd', pooled, w_group).reshape(B, S, POOL_WIDTH) * scale
    y = mixed * jax.nn.silu(z)
    return x + y @ w_out

def rope_tables(positions, dtype):
    inv_freq = 1.0 / (ROPE_THETA ** (jnp.arange(0, QK_ROPE_DIM, 2, dtype=jnp.float32) / QK_ROPE_DIM))
    ang = positions.astype(jnp.float32)[..., None] * inv_freq
    return jnp.cos(ang).astype(dtype), jnp.sin(ang).astype(dtype)

def apply_rope(t, cos, sin):
    half = QK_ROPE_DIM // 2
    t1, t2 = t[..., :half], t[..., half:]
    return jnp.concatenate([t1 * cos - t2 * sin, t2 * cos + t1 * sin], axis=-1)

def causal_mla_attention(q_nope, q_rope, k_nope, k_rope, v):
    B, S, H, _ = q_nope.shape
    nb = S // Q_BLOCK
    scale = QK_HEAD_DIM ** -0.5
    key_pos = jnp.arange(S)

    def to_blocks(t):
        return t.reshape(B, nb, Q_BLOCK, *t.shape[2:]).swapaxes(0, 1)

    def one_block(args):
        qn, qr, start = args
        s = (jnp.einsum('bqhd,bkhd->bhqk', qn, k_nope)
             + jnp.einsum('bqhr,bkr->bhqk', qr, k_rope)).astype(jnp.float32) * scale
        q_pos = start + jnp.arange(Q_BLOCK)
        mask = q_pos[:, None] >= key_pos[None, :]
        s = jnp.where(mask, s, jnp.finfo(jnp.float32).min)
        p = jax.nn.softmax(s, axis=-1).astype(v.dtype)
        return jnp.einsum('bhqk,bkhd->bqhd', p, v)

    starts = jnp.arange(nb, dtype=jnp.int32) * Q_BLOCK
    out = lax.map(one_block, (to_blocks(q_nope), to_blocks(q_rope), starts))
    return out.swapaxes(0, 1).reshape(B, S, H, V_HEAD_DIM)

def mla_layer(x, cos, sin, norm_g, w_in, q_norm_g, w_q_b, kv_norm_g, w_kv_b, w_out):
    B, S, _ = x.shape
    h = rmsnorm(x, norm_g)
    proj = h @ w_in
    o1 = Q_LORA_RANK
    o2 = o1 + KV_LORA_RANK
    o3 = o2 + QK_ROPE_DIM
    q_lat, kv_lat, k_rope, z = proj[..., :o1], proj[..., o1:o2], proj[..., o2:o3], proj[..., o3:]
    q = (rmsnorm(q_lat, q_norm_g) @ w_q_b).reshape(B, S, N_HEADS, QK_HEAD_DIM)
    q_nope, q_rope = q[..., :QK_NOPE_DIM], q[..., QK_NOPE_DIM:]
    kv = (rmsnorm(kv_lat, kv_norm_g) @ w_kv_b).reshape(B, S, N_HEADS, QK_NOPE_DIM + V_HEAD_DIM)
    k_nope, v = kv[..., :QK_NOPE_DIM], kv[..., QK_NOPE_DIM:]
    q_rope = apply_rope(q_rope, cos[:, :, None, :], sin[:, :, None, :])
    k_rope = apply_rope(k_rope, cos, sin)
    o = causal_mla_attention(q_nope, q_rope, k_nope, k_rope, v)
    y = o.reshape(B, S, MLA_WIDTH) * jax.nn.silu(z)
    return x + y @ w_out

def first_inputs(seed: int = 0) -> dict:
    key = jax.random.key(seed)
    ks = jax.random.split(key, 16)
    nrm = jax.random.normal
    Lp, Lm = N_POOL_LAYERS, N_MLA_LAYERS
    x = nrm(ks[0], (BATCH, SEQ, D_MODEL), jnp.float32)
    positions = jnp.broadcast_to(jnp.arange(SEQ, dtype=jnp.int32)[None, :], (BATCH, SEQ))
    return {
        "x": x,
        "positions": positions,
        "pool_norm": 1.0 + 0.02 * nrm(ks[1], (Lp, D_MODEL), jnp.float32),
        "pool_w_in": nrm(ks[2], (Lp, D_MODEL, 2 * POOL_WIDTH), jnp.float32) * D_MODEL ** -0.5,
        "pool_w_group": nrm(ks[3], (Lp, N_POOL_GROUPS, POOL_GROUP, POOL_GROUP), jnp.float32) * POOL_GROUP ** -0.5,
        "pool_scale": 1.0 + 0.02 * nrm(ks[4], (Lp, POOL_WIDTH), jnp.float32),
        "pool_w_out": nrm(ks[5], (Lp, POOL_WIDTH, D_MODEL), jnp.float32) * POOL_WIDTH ** -0.5,
        "mla_norm": 1.0 + 0.02 * nrm(ks[6], (Lm, D_MODEL), jnp.float32),
        "mla_w_in": nrm(ks[7], (Lm, D_MODEL, MLA_IN_WIDTH), jnp.float32) * D_MODEL ** -0.5,
        "mla_q_norm": 1.0 + 0.02 * nrm(ks[8], (Lm, Q_LORA_RANK), jnp.float32),
        "mla_w_q_b": nrm(ks[9], (Lm, Q_LORA_RANK, N_HEADS * QK_HEAD_DIM), jnp.float32) * Q_LORA_RANK ** -0.5,
        "mla_kv_norm": 1.0 + 0.02 * nrm(ks[10], (Lm, KV_LORA_RANK), jnp.float32),
        "mla_w_kv_b": nrm(ks[11], (Lm, KV_LORA_RANK, N_HEADS * (QK_NOPE_DIM + V_HEAD_DIM)), jnp.float32) * KV_LORA_RANK ** -0.5,
        "mla_w_out": nrm(ks[12], (Lm, MLA_WIDTH, D_MODEL), jnp.float32) * MLA_WIDTH ** -0.5,
        "final_norm": 1.0 + 0.02 * nrm(ks[13], (D_MODEL,), jnp.float32),
    }

def first_block(x, positions, pool_norm, pool_w_in, pool_w_group, pool_scale, pool_w_out,
              mla_norm, mla_w_in, mla_q_norm, mla_w_q_b, mla_kv_norm, mla_w_kv_b, mla_w_out,
              final_norm):
    cos, sin = rope_tables(positions, x.dtype)
    for i in range(DEPTH):
        j = i // N_MIXERS
        if i % N_MIXERS == 0:
            x = pool_layer(x, pool_norm[j], pool_w_in[j], pool_w_group[j], pool_scale[j], pool_w_out[j])
        else:
            x = mla_layer(x, cos, sin, mla_norm[j], mla_w_in[j], mla_q_norm[j], mla_w_q_b[j],
                          mla_kv_norm[j], mla_w_kv_b[j], mla_w_out[j])
    return rmsnorm(x, final_norm)


DEPTH_2 = 1

ATT_PATTERNS = ((128, 1), (512, 4), (2048, 16))
ATT_GROUPS = len(ATT_PATTERNS)
ATT_HEADS = 8
ATT_HEAD_DIM = 64
ATT_WIDTH = ATT_HEADS * ATT_HEAD_DIM
ATT_BLOCK = 128
RWKV_WIDTH = D_MODEL
RWKV_HEAD_DIM = 64
RWKV_HEADS = RWKV_WIDTH // RWKV_HEAD_DIM
DECAY_LORA = 64
AAA_LORA = 64
GATE_LORA = 160
D_FF = 2816
CONV_WIDTH = 3
N_BRANCHES = 2
ATT_IN = ATT_GROUPS * 3 * ATT_WIDTH
RWKV_IN = 3 * RWKV_WIDTH + DECAY_LORA + AAA_LORA + GATE_LORA
GATE_IN = N_BRANCHES * D_MODEL
N_IN = ATT_IN + RWKV_IN + GATE_IN
RMS_EPS = 1e-6
GN_EPS = 64e-5


def rms_norm(x, w):
    xf = x.astype(jnp.float32)
    y = xf * lax.rsqrt(jnp.mean(xf * xf, axis=-1, keepdims=True) + RMS_EPS)
    return (y * w).astype(x.dtype)

def dilated_window_attention(q, k, v, window, dilation):
    b, s, h, e = q.shape
    back = window // dilation
    sub_len = -(-s // dilation)
    n_blk = -(-sub_len // ATT_BLOCK)
    s_pad = n_blk * ATT_BLOCK * dilation

    def to_blocks(t):
        t = jnp.pad(t, ((0, 0), (0, s_pad - s), (0, 0), (0, 0)))
        return t.reshape(b, n_blk, ATT_BLOCK, dilation, h, e)

    def with_prev(t):
        prev = jnp.concatenate([jnp.zeros_like(t[:, :1]), t[:, :-1]], axis=1)
        return jnp.concatenate([prev, t], axis=2)

    qb = to_blocks(q)
    kc = with_prev(to_blocks(k))
    vc = with_prev(to_blocks(v))
    scores = jnp.einsum('bnqrhe,bnkrhe->bnrhqk', qb, kc).astype(jnp.float32) * (e ** -0.5)
    qi = jnp.arange(ATT_BLOCK)[:, None]
    kj = jnp.arange(2 * ATT_BLOCK)[None, :]
    dist = qi + ATT_BLOCK - kj
    kpos = jnp.arange(n_blk)[:, None] * ATT_BLOCK + kj - ATT_BLOCK
    valid = ((dist >= 0) & (dist <= back))[None] & (kpos >= 0)[:, None, :]
    scores = jnp.where(valid[None, :, None, None], scores, -jnp.inf)
    m = jnp.max(scores, axis=-1, keepdims=True)
    p = jnp.exp(scores - m)
    den = jnp.sum(p, axis=-1)
    num = jnp.einsum('bnrhqk,bnkrhe->bnqrhe', p, vc.astype(jnp.float32))
    den_q = jnp.transpose(den, (0, 1, 4, 2, 3))
    out = (num / den_q[..., None]).reshape(b, s_pad, h, e)[:, :s]
    lse = (jnp.transpose(m[..., 0], (0, 1, 4, 2, 3)) + jnp.log(den_q)).reshape(b, s_pad, h)[:, :s]
    return out, lse

def attention_mixer(z):
    b, s, _ = z.shape
    qkv = z.reshape(b, s, ATT_GROUPS, 3, ATT_HEADS, ATT_HEAD_DIM)
    outs, lses = [], []
    for g, (window, dilation) in enumerate(ATT_PATTERNS):
        o, l = dilated_window_attention(qkv[:, :, g, 0], qkv[:, :, g, 1], qkv[:, :, g, 2], window, dilation)
        outs.append(o)
        lses.append(l)
    wts = jax.nn.softmax(jnp.stack(lses), axis=0)
    out = jnp.sum(wts[..., None] * jnp.stack(outs), axis=0)
    return out.reshape(b, s, ATT_WIDTH).astype(z.dtype)

def rwkv7_mixer(z, mu, w0, w2, a0, a2, g2, k_k, k_a, r_k, lnx_w, lnx_b):
    f32 = jnp.float32
    b, s, _ = z.shape
    z_prev = jnp.pad(z, ((0, 0), (1, 0), (0, 0)))[:, :s]
    z = z + (z_prev - z) * mu
    c = RWKV_WIDTH
    r, k, v, w_low, a_low, g_low = jnp.split(
        z, [c, 2 * c, 3 * c, 3 * c + DECAY_LORA, 3 * c + DECAY_LORA + AAA_LORA], axis=-1)
    w_log = -jax.nn.softplus(-(w0 + jnp.tanh(w_low) @ w2).astype(f32)) - 0.5
    decay = jnp.exp(-jnp.exp(w_log))
    a = jax.nn.sigmoid((a0 + a_low @ a2).astype(f32))
    g = jax.nn.sigmoid(g_low) @ g2
    k_mod = k.astype(f32) * (1.0 + (a - 1.0) * k_a)

    def heads(t):
        return t.astype(f32).reshape(b, s, RWKV_HEADS, RWKV_HEAD_DIM)

    kk = heads(k * k_k)
    kk = kk / jnp.maximum(jnp.sqrt(jnp.sum(kk * kk, axis=-1, keepdims=True)), 1e-12)
    r_h, k_h, v_h, w_h, a_h = heads(r), heads(k_mod), heads(v), heads(decay), heads(a)

    def step(state, inp):
        r_t, w_t, k_t, v_t, aa_t, bb_t = inp
        sa = jnp.einsum('bhvk,bhk->bhv', state, aa_t)
        state = state * w_t[:, :, None, :] + sa[..., None] * bb_t[:, :, None, :] + v_t[..., None] * k_t[:, :, None, :]
        return state, jnp.einsum('bhvk,bhk->bhv', state, r_t)

    tm = lambda t: jnp.swapaxes(t, 0, 1)
    state0 = jnp.zeros((b, RWKV_HEADS, RWKV_HEAD_DIM, RWKV_HEAD_DIM), f32)
    _, y = lax.scan(step, state0, (tm(r_h), tm(w_h), tm(k_h), tm(v_h), tm(-kk), tm(kk * a_h)))
    y = tm(y)
    mean = jnp.mean(y, axis=-1, keepdims=True)
    var = jnp.mean(jnp.square(y - mean), axis=-1, keepdims=True)
    y = ((y - mean) * lax.rsqrt(var + GN_EPS)).reshape(b, s, c) * lnx_w + lnx_b
    bonus = (jnp.sum(r_h * k_h * r_k, axis=-1, keepdims=True) * v_h).reshape(b, s, c)
    return ((y + bonus) * g).astype(z.dtype)

def conv_ffn(h, w_up, conv_w, conv_b, w_down):
    s = h.shape[1]
    u = h @ w_up
    up = jnp.pad(u, ((0, 0), (CONV_WIDTH - 1, 0), (0, 0)))
    u = conv_b + sum(conv_w[j] * up[:, j:j + s] for j in range(CONV_WIDTH))
    gate, val = jnp.split(u, 2, axis=-1)
    return (jax.nn.silu(gate) * val) @ w_down

def second_inputs(seed: int = 0) -> dict:
    key = jax.random.key(seed)
    ks = iter(jax.random.split(key, 32))
    f32 = jnp.float32
    L, D, C = DEPTH_2, D_MODEL, RWKV_WIDTH

    def nrm(shape, scale):
        return jax.random.normal(next(ks), shape, f32) * scale

    ramp = (jnp.arange(C, dtype=f32) / (C - 1)) ** 0.85
    inputs = {}
    inputs['x'] = nrm((BATCH, SEQ, D), 1.0)
    inputs['c'] = nrm((BATCH, D), 1.0)
    inputs['w_ada'] = nrm((L, D, 6 * D), 0.3 * D ** -0.5)
    inputs['b_ada'] = nrm((L, 6 * D), 0.02)
    inputs['norm1_w'] = 1.0 + nrm((L, D), 0.05)
    inputs['w_in'] = nrm((L, D, N_IN), D ** -0.5)
    inputs['b_gate'] = nrm((L, GATE_IN), 0.1)
    inputs['mu_shift'] = jax.random.uniform(next(ks), (L, RWKV_IN), f32)
    inputs['w0'] = -6.5 + 5.0 * ramp + nrm((L, C), 0.1)
    inputs['w2'] = nrm((L, DECAY_LORA, C), 0.1 * DECAY_LORA ** -0.5)
    inputs['a0'] = nrm((L, C), 0.1)
    inputs['a2'] = nrm((L, AAA_LORA, C), AAA_LORA ** -0.5)
    inputs['g2'] = nrm((L, GATE_LORA, C), GATE_LORA ** -0.5)
    inputs['k_k'] = 0.85 + nrm((L, C), 0.05)
    inputs['k_a'] = 1.0 + nrm((L, C), 0.05)
    inputs['r_k'] = nrm((L, RWKV_HEADS, RWKV_HEAD_DIM), 0.1)
    inputs['lnx_w'] = 1.0 + nrm((L, C), 0.05)
    inputs['lnx_b'] = nrm((L, C), 0.02)
    inputs['w_att_out'] = nrm((L, ATT_WIDTH, D), ATT_WIDTH ** -0.5)
    inputs['w_rwkv_out'] = nrm((L, C, D), C ** -0.5)
    inputs['w_o'] = nrm((L, D, D), D ** -0.5)
    inputs['norm2_w'] = 1.0 + nrm((L, D), 0.05)
    inputs['w_up'] = nrm((L, D, 2 * D_FF), D ** -0.5)
    inputs['conv_w'] = nrm((L, CONV_WIDTH, 2 * D_FF), CONV_WIDTH ** -0.5)
    inputs['conv_b'] = nrm((L, 2 * D_FF), 0.02)
    inputs['w_down'] = nrm((L, D_FF, D), D_FF ** -0.5)
    inputs['norm_f_w'] = 1.0 + nrm((D,), 0.05)
    return inputs

def second_block(x, c, w_ada, b_ada, norm1_w, w_in, b_gate, mu_shift, w0, w2, a0, a2, g2, k_k, k_a, r_k,
              lnx_w, lnx_b, w_att_out, w_rwkv_out, w_o, norm2_w, w_up, conv_w, conv_b, w_down, norm_f_w):
    for l in range(DEPTH_2):
        ada = (c @ w_ada[l] + b_ada[l])[:, None, :]
        sh1, sc1, gt1, sh2, sc2, gt2 = jnp.split(ada, 6, axis=-1)
        h = rms_norm(x, norm1_w[l]) * (1.0 + sc1) + sh1
        proj = h @ w_in[l]
        att_in, rwkv_in, gate_in = jnp.split(proj, [ATT_IN, ATT_IN + RWKV_IN], axis=-1)
        y_att = attention_mixer(att_in) @ w_att_out[l]
        y_rwkv = rwkv7_mixer(rwkv_in, mu_shift[l], w0[l], w2[l], a0[l], a2[l], g2[l], k_k[l], k_a[l],
                             r_k[l], lnx_w[l], lnx_b[l]) @ w_rwkv_out[l]
        g_att, g_rwkv = jnp.split(jax.nn.sigmoid(gate_in + b_gate[l]), N_BRANCHES, axis=-1)
        x = x + gt1 * ((g_att * y_att + g_rwkv * y_rwkv) @ w_o[l])
        h = rms_norm(x, norm2_w[l]) * (1.0 + sc2) + sh2
        x = x + gt2 * conv_ffn(h, w_up[l], conv_w[l], conv_b[l], w_down[l])
    return rms_norm(x, norm_f_w)


def setup_inputs(seed=0):
    out = dict(first_inputs(seed))
    for name, value in second_inputs(seed + 1).items():
        if name != "x":
            out[name + "_2"] = value
    return out


def reference(
    x, positions, pool_norm, pool_w_in, pool_w_group, pool_scale, pool_w_out, mla_norm,
    mla_w_in, mla_q_norm, mla_w_q_b, mla_kv_norm, mla_w_kv_b, mla_w_out, final_norm, c_2,
    w_ada_2, b_ada_2, norm1_w_2, w_in_2, b_gate_2, mu_shift_2, w0_2, w2_2, a0_2, a2_2, g2_2,
    k_k_2, k_a_2, r_k_2, lnx_w_2, lnx_b_2, w_att_out_2, w_rwkv_out_2, w_o_2, norm2_w_2, w_up_2,
    conv_w_2, conv_b_2, w_down_2, norm_f_w_2,
):
    x = first_block(
        x, positions, pool_norm, pool_w_in, pool_w_group, pool_scale, pool_w_out, mla_norm,
        mla_w_in, mla_q_norm, mla_w_q_b, mla_kv_norm, mla_w_kv_b, mla_w_out, final_norm,
    )
    return second_block(
        x, c_2, w_ada_2, b_ada_2, norm1_w_2, w_in_2, b_gate_2, mu_shift_2, w0_2, w2_2, a0_2,
        a2_2, g2_2, k_k_2, k_a_2, r_k_2, lnx_w_2, lnx_b_2, w_att_out_2, w_rwkv_out_2, w_o_2,
        norm2_w_2, w_up_2, conv_w_2, conv_b_2, w_down_2, norm_f_w_2,
    )


_drawn_inputs = setup_inputs


def setup_inputs(seed=0):
    import zlib

    import numpy as np

    out = dict(_drawn_inputs(seed))
    spreads = {}
    factors = {'pool_norm': 3.812,
     'pool_scale': 6.007,
     'mla_norm': 8.0,
     'mla_q_norm': 8.0,
     'mla_kv_norm': 8.0,
     'b_ada_2': 2.833,
     'norm1_w_2': 6.232,
     'b_gate_2': 8.0,
     'w2_2': 173.986,
     'a0_2': 8.0,
     'k_k_2': 200.0,
     'k_a_2': 8.0,
     'lnx_w_2': 200.0,
     'lnx_b_2': 200.0,
     'norm2_w_2': 29.568,
     'conv_b_2': 64.0,
     'w0_2': 7.651,
     'w_att_out_2': 2.76}
    for name, (base, spread) in spreads.items():
        noise = np.random.default_rng([zlib.crc32(name.encode()), seed]).standard_normal(out[name].shape)
        drawn = base * np.exp(spread * noise) if base else spread * noise
        out[name] = __import__('jax').numpy.asarray(drawn.astype(out[name].dtype))
    for name, factor in factors.items():
        out[name] = (out[name] * factor).astype(out[name].dtype)
    return out
```

```python
from contextlib import ExitStack, nullcontext

import numpy as np

import concourse.bass as bass
from concourse import mybir

P = 128
S = 512
D = 1024
DT = D // P
EPS = 1e-6
POOL_WINDOWS = (2, 4, 8, 16)
PAD = 16
HEADS = 16
NOPE, ROPE, VD = 128, 64, 128
QK = NOPE + ROPE
Q_RANK, KV_RANK = 384, 256
ROPE_THETA = 10000.0
QK_SCALE = QK ** -0.5
ATT_GROUPS = 3
ATT_HEADS, ATT_DIM = 8, 64
ATT_WIDTH = ATT_HEADS * ATT_DIM
ATT_IN = ATT_GROUPS * 3 * ATT_WIDTH
CH = 64
PAIRS = D // P
RWKV_IN = 3 * D + 64 + 64 + 160
GATE0 = ATT_IN + RWKV_IN
GN_EPS = 64e-5
D_FF = 2816
FT = D_FF // P
DOWN_K = (8, 8, 6)
SCAN_SCALE = 2.0 ** -20
BIG = 1e30
ROUND = 1.5 * 2.0 ** 23
TWO_PI = (6.28125, 0.00193500518798828125, 3.0199159795074593e-07)
PI_IN = 3.14159250259399414

F32 = mybir.dt.float32
F32R = mybir.dt.float32r
BF16 = mybir.dt.bfloat16
I32 = mybir.dt.int32
ALU = mybir.AluOpType
ACT = mybir.ActivationFunctionType
AX = mybir.AxisListType
ds = bass.ds

VEC_ROWS = [("pool_norm", 8), ("pool_scale", 16), ("mla_norm", 8), ("mla_q_norm", 3), ("mla_kv_norm", 2),
            ("final_norm", 8), ("c_2", 8), ("b_ada_2", 48), ("norm1_w_2", 8), ("b_gate_2", 16),
            ("mu_shift_2", 27), ("w0_2", 8), ("a0_2", 8), ("k_k_2", 8), ("k_a_2", 8), ("r_k_2", 8),
            ("lnx_w_2", 8), ("lnx_b_2", 8), ("norm2_w_2", 8), ("conv_w_2", 132), ("conv_b_2", 44),
            ("norm_f_w_2", 8)]
VEC0 = {}
for _name, _rows in VEC_ROWS:
    VEC0[_name] = sum(r for n, r in VEC_ROWS[:len(VEC0)])
VEC_ALL = sum(r for _, r in VEC_ROWS)
VEC_TILES = -(-VEC_ALL // P)

STREAM = [("pool", 4, 6), ("pool_out", 2, 4), ("lat", 1, 4), ("mz", 4, 2), ("heads", 8, 2), ("mla_out", 2, 4),
          ("att", 9, 2), ("lora", 1, 2), ("rkv", PAIRS, 2), ("mix", 4, 4), ("wo", 2, 2), ("up", 11, 2),
          ("down", 2, 6)]
STRIP0 = {}
for _name, _n, _m in STREAM:
    STRIP0[_name] = sum(n * m for _, n, m in STREAM[:len(STRIP0)])
FILLS = {"pool": (12,) * 4, "pool_out": (2,) * 4, "lat": (2, 1, 2, 1), "mz": (4,) * 4, "heads": (16,) * 4,
         "mla_out": (2,) * 4, "att": (9,) * 4, "lora": (1, 0, 1, 1), "rkv": (8, 8, 8, 0), "mix": (8,) * 4,
         "wo": (2,) * 4, "up": (11,) * 4, "down": (2,) * 4}
FILL0 = {}
for _name, _n, _m in STREAM:
    FILL0[_name] = tuple(sum(FILLS[p][b] for p, _, _ in STREAM[:len(FILL0)]) for b in range(4))
RAW_CREDIT = 2
SPLIT_CREDIT = 4


def loaded_value(ph, i, j, m):
    before = STRIP0[ph] // 2 + j // 2 + 1
    if ph == "rkv" and j == 0:
        return (i * 2 + (before + 1)) * 16
    if j % 2 == 0 and STRIP0[ph] > STRIP0["rkv"]:
        before += PAIRS
    return (i * (m // 2) + before) * 16


def split_value(s):
    return RAW_CREDIT + s + 1


def done_value(s, half):
    return SPLIT_CREDIT + 2 * s + half + 1


def att_units(g):
    units = []
    for h in range(ATT_HEADS):
        if g == 0:
            units += [(h, [(0, 0), (1, 0), (1, 1)]), (h, [(2, 1), (2, 2), (3, 2), (3, 3)])]
        else:
            units.append((h, [(b, b) for b in range(4)]))
    return units


def att_rows(blocks):
    rows = []
    for n, (qb, kb) in enumerate(blocks):
        if rows and rows[-1][0] == qb:
            rows[-1] = (qb, rows[-1][1], rows[-1][2] + 1, rows[-1][3])
        else:
            rows.append((qb, kb, 1, n * P))
    return rows


def gram_list():
    return [(h, l, r) for l, r in (("b", "a"), ("a", "b")) for h in range(2)] + \
           [(h, l, r) for h in range(2) for l, r in (("k", "a"), ("b", "r"), ("k", "r"))]


INVERSE = [
    {"mm": [("DA", "D", "act", "N2"), ("D", "DA", "dve", "A2")]},
    {"mm": [("A2", "N2", "act", "N4"), ("N2", "A2", "act", "A4")]},
    {"mm": [("N4", "A4", "act", "A8"), ("A2", "U", "dve", "+U")]},
    {"mm": [("A4", "U", "dve", "+U")], "E": 16},
    {"mm": [("A8", "U", "dve", "+U")]},
    {"mm": [("U", "I", "act", "W"), ("E", "U", "act", "Z")]},
    {"mm": [("W", "Z", "dve", "+U"), ("Z", "W", "dve", "+W")], "E": 32},
    {"mm": [("E", "U", "act", "Z")]},
    {"mm": [("W", "Z", "dve", "+U"), ("Z", "W", "dve", "+W")], "E": 64},
    {"mm": [("E", "U", "act", "Z")]},
    {"mm": [("W", "Z", "dve", "+U")]},
]
INV_ACT = [sum(x[2] == "act" for st in INVERSE[:k] for x in st["mm"]) for k in range(len(INVERSE) + 1)]
INV_DVE = [1 + sum(x[2] == "dve" for st in INVERSE[:k] for x in st["mm"]) + sum("E" in st for st in INVERSE[:k])
           for k in range(len(INVERSE) + 1)]


def build(nc, a, out):
    with ExitStack() as ctx:
        def sb(name, shape, dt=F32, stack=None):
            return (stack or ctx).enter_context(nc.sbuf_tensor(name, shape, dt))

        sems = {}

        def sem(name):
            if name not in sems:
                sems[name] = ctx.enter_context(nc.semaphore(name))
            return sems[name]

        bank = [ctx.enter_context(nc.psum_tensor(f"bank{b}", [P, S], F32)) for b in range(8)]
        scratch = nc.dram_tensor("stat_scratch", [4, S * ATT_HEADS], F32, kind="Internal").ap()

        raw = [sb(f"raw{b}", [P, 2048]) for b in range(2)]
        whi = [sb(f"whi{b}", [P, 2048], F32R) for b in range(2)]
        wlo = [sb(f"wlo{b}", [P, 2048], F32R) for b in range(2)]
        xT = sb("xT", [P, DT * S])
        hbuf = sb("hbuf", [P, 2 * DT * S], F32R)
        sq = sb("sq", [P, 2 * S])
        hf = sb("hf", [P, 2 * S])
        inv = sb("inv", [P, S])
        vec = sb("vec", [P, VEC_ALL])
        ident = sb("ident", [P, P])
        ones = sb("ones", [P, P])
        same = {n: sb(f"same{n}", [P, P]) for n in (16, 32, 64)}
        upper1 = sb("upper1", [P, P])
        upper0 = sb("upper0", [P, P])
        lower1 = sb("lower1", [P, P])
        up16 = sb("up16", [P, P])
        low16 = sb("low16", [P, P])
        step_mask = {n: sb(f"step{n}", [P, P]) for n in (16, 32, 64)}
        ident_b = sb("ident_b", [P, P], BF16)
        neg_band = sb("neg_band", [P, 2 * P], BF16)
        neg_dil = sb("neg_dil", [P, P], BF16)
        ada = sb("ada", [P, 48])
        gain1 = sb("gain1", [P, DT])
        gain2 = sb("gain2", [P, DT])
        spare = sb("spare", [P, 1])
        eps_c = sb("eps_c", [P, 1])
        gneps_c = sb("gneps_c", [P, 1])
        one_minus_ka = sb("one_minus_ka", [P, DT])
        neg_causal = neg_band[:, P:2 * P]

        def tile(buf, i):
            return buf[:, i * S:(i + 1) * S]

        def dtile(buf, i):
            return buf[:, ds(i * S, S)]

        def col(name, i):
            return vec[:, VEC0[name] + i:VEC0[name] + i + 1]

        def dcol(name, i):
            return vec[:, ds(VEC0[name] + i, 1)]

        with ExitStack() as st:
            vecrow = sb("vecrow", [P, VEC_TILES * P], F32, st)
            xin = sb("xin", [P, 4 * D], F32, st)
            res4 = sb("res4", [P, 4], F32, st)
            tmp_mask = sb("tmp_mask", [P, P], F32, st)
        with ExitStack() as st:
            y1H = sb("y1H", [P, 16 * S], F32R, st)
            y1L = sb("y1L", [P, 16 * S], F32R, st)
            poolH = sb("poolH", [P, 4 * S], F32R, st)
            poolL = sb("poolL", [P, 4 * S], F32R, st)
            zp = sb("zp", [P, 4 * S], F32, st)
            upad = [sb(f"upad{b}", [P, PAD + S], F32, st) for b in range(2)]
            cinv = sb("cinv", [P, 4 * PAD], F32, st)
        with ExitStack() as st:
            zm = sb("zm", [P, 16 * S], F32, st)
            latH = sb("latH", [P, 5 * S], F32R, st)
            latL = sb("latL", [P, 5 * S], F32R, st)
            krope = sb("krope", [P, S], F32, st)
            cosT = sb("cosT", [P, S], F32, st)
            sinT = sb("sinT", [P, S], F32, st)
            with ExitStack() as st2:
                lat = sb("lat", [P, 5 * S], F32, st2)
                posi = sb("posi", [P, S], I32, st2)
                ang = sb("ang", [P, 3 * S], F32, st2)
                invf = sb("invf", [P, 1], F32, st2)
            with ExitStack() as st2:
                kT = sb("kT", [P, 2 * S], F32, st2)
                vN = hf
                qT = sb("qT", [P, 2 * S], F32, st2)
                qrope = sb("qrope", [P, S], F32, st2)
                prob = [sb(f"prob{b}", [P, S], F32, st2) for b in range(2)]
                probT = sb("probT", [P, 4 * S], F32, st2)
                adaw = sb("adaw", [P, DT * 256], F32, st2)
                adaacc = sb("adaacc", [P, 3 * 256], F32, st2)
                stat = sb("stat", [P, 8], F32, st2)
            with ExitStack() as st2:
                y2L = sb("y2L", [P, 16 * S], F32R, st2)
        y2H = hbuf
        with ExitStack() as st:
            at = sb("at", [P, 4 * S], F32, st)
            with ExitStack() as st2:
                aq = sb("aq", [P, 4 * S], F32, st2)
                ak = sb("ak", [P, 4 * S], F32, st2)
                av = sb("av", [P, 4 * ATT_HEADS * P], F32, st2)
                num = [sb(f"num{g}", [P, 4 * S], F32, st2) for g in range(3)]
                ap_ = [sb(f"ap{b}", [P, S], F32, st2) for b in range(2)]
                apT = [sb(f"apT{b}", [P, S], F32, st2) for b in range(2)]
                spread = [ap_[0], ap_[1], apT[0]]
                nmax = sb("nmax", [P, 3 * 32], F32, st2)
                den = sb("den", [P, 3 * 32], F32, st2)
                stq = sb("stq", [P, 2 * 32], F32, st2)
                fac = sb("fac", [P, 3 * 32], F32, st2)
                fac0 = sb("fac0", [P, 32], F32, st2)
                zden = sb("zden", [P, 32], F32, st2)
            with ExitStack() as st2:
                yr = sb("yr", [P, PAIRS * S], F32, st2)
                with ExitStack() as st3:
                    wlow = sb("wlow", [P, S], F32, st3)
                    glow = sb("glow", [P, 2 * S], F32, st3)
                    lw2 = sb("lw2", [P, P], F32, st3)
                    lg2 = sb("lg2", [P, 2 * P], F32, st3)
                    rmask = sb("rmask", [P, S], F32, st3)
                    pcol = sb("pcol", [P, 16], F32, st3)
                    aT = sb("aT", [P, S], F32, st3)
                    rT = sb("rT", [P, S], F32, st3)
                    bT = sb("bT", [P, S], F32, st3)
                    kkT = sb("kkT", [P, S], F32, st3)
                    vT = sb("vT", [P, S], F32, st3)
                    bonus = sb("bonus", [P, S], F32, st3)
                    vpad = sb("vpad", [P, 4 * 256], F32, st3)
                    bN = sb("bN", [P, S], F32, st3)
                    kN = sb("kN", [P, S], F32, st3)
                    Gak = [sb(f"Gak{h}", [P, S], F32, st3) for h in range(2)]
                    Gqb = [sb(f"Gqb{h}", [P, S], F32, st3) for h in range(2)]
                    Gqk = [sb(f"Gqk{h}", [P, S], F32, st3) for h in range(2)]
                    sapad = sb("sapad", [P, 256], F32, st3)
                    rhs = sb("rhs", [P, P], F32, st3)
                    state = sb("state", [P, P], F32, st3)
                    fade = sb("fade", [P, 4], F32, st3)
                    with ExitStack() as st4:
                        zsh = [sb(f"zsh{b}", [P, 1 + S], F32, st4) for b in range(3)]
                        Rr = sb("Rr", [P, S], F32, st4)
                        Kr = sb("Kr", [P, S], F32, st4)
                        lwd = sb("lwd", [P, S], F32, st4)
                        csum = sb("csum", [P, S], F32, st4)
                        cc = sb("cc", [P, S], F32, st4)
                        epos = sb("epos", [P, S], F32, st4)
                        aa = sb("aa", [P, S], F32, st4)
                        kk = sb("kk", [P, S], F32, st4)
                    with ExitStack() as st4:
                        IA, IN4, IA4, IA8, IE = [[sb(f"{n}_{h}", [P, S], F32, st4) for h in range(2)]
                                                 for n in ("IA", "IN4", "IA4", "IA8", "IE")]
                    IW = [tile(sq, h) for h in range(2)]
                    IU = [tile(hf, h) for h in range(2)]
        with ExitStack() as st:
            sb("under_at_and_yr", [P, (4 + PAIRS) * S], F32, st)
            atH = sb("atH", [P, 4 * S], F32R, st)
            atL = sb("atL", [P, 4 * S], F32R, st)
            rH = sb("rH", [P, PAIRS * S], F32R, st)
            rL = sb("rL", [P, PAIRS * S], F32R, st)
            mixL = sb("mixL", [P, DT * S], F32R, st)
        with ExitStack() as st:
            mixH = sb("mixH", [P, DT * S], F32R, st)
        with ExitStack() as st:
            fH = sb("fH", [P, FT * S], F32R, st)
            fL = sb("fL", [P, FT * S], F32R, st)
            cpad = [sb(f"cpad{b}", [P, 2 + S], F32, st) for b in range(2)]
        with ExitStack() as st:
            yout = [sb(f"yout{b}", [P, D], F32, st) for b in range(2)]
        V, A, G, M = nc.vector, nc.scalar, nc.gpsimd, nc.tensor
        products_done, raw_split = sem("products_done"), sem("raw_split")
        raw_loaded = [sem(f"raw_loaded{b}") for b in range(2)]
        evac = [sem(f"bank_taken{b}") for b in range(4)]
        hH = [hbuf[:, d * S:(d + 1) * S] for d in range(DT)]
        hL = [hbuf[:, (DT + d) * S:(DT + d + 1) * S] for d in range(DT)]
        f32 = lambda r: r.bitcast(F32)
        fill = lambda ph, b: FILL0[ph][b]

        def out_tile_taken(ph, t):
            b = (t // 2 % 2) * 2 + t % 2
            return evac[b], fill(ph, b) + t // 4 + 1

        w_in1 = a["pool_w_in"].rearrange("l (k p) n -> p (l k) n", p=P)
        w_grp = a["pool_w_group"].rearrange("l g (k p) n -> p (l g k) n", p=P)
        w_out1 = a["pool_w_out"].rearrange("l (k p) n -> p (l k) n", p=P)
        w_mla = a["mla_w_in"].rearrange("l (k p) n -> p (l k) n", p=P)
        w_q = a["mla_w_q_b"].rearrange("l (k p) n -> p (l k) n", p=P)
        w_kv = a["mla_w_kv_b"].rearrange("l (k p) n -> p (l k) n", p=P)
        w_out2 = a["mla_w_out"].rearrange("l (k p) n -> p (l k) n", p=P)
        w_ada = a["w_ada_2"].rearrange("l (k p) n -> p (l k) n", p=P)
        w_in2 = a["w_in_2"].rearrange("l (k p) n -> p (l k) n", p=P)
        w_ao = a["w_att_out_2"].rearrange("l (k p) n -> p (l k) n", p=P)
        w_ro = a["w_rwkv_out_2"].rearrange("l (k p) n -> p (l k) n", p=P)
        w_wo = a["w_o_2"].rearrange("l (k p) n -> p (l k) n", p=P)
        w_up = a["w_up_2"].rearrange("l (k p) n -> p (l k) n", p=P)
        w_dn = a["w_down_2"].rearrange("l (k p) n -> p (l k) n", p=P)
        LAT = ((0, 256), (256, 256), (512, 128), (640, 64))
        MZ0 = Q_RANK + KV_RANK + ROPE
        LORA0 = ATT_IN + 3 * D
        LORA = ((LORA0, 128), (LORA0 + 128, 160))

        def strip_source(ph, i, j):
            if ph == "pool":
                if j < 4:
                    return w_in1[:, :, ds(i * 512 + (j // 2) * 2 * D + (j % 2) * 256, 256)], 8, 256
                return w_grp[:, ds(i * 4, 4), (j - 4) * 256:(j - 3) * 256], 4, 256
            if ph in ("pool_out", "mla_out"):
                w = w_out1 if ph == "pool_out" else w_out2
                return w[:, (j % 2) * 8:(j % 2) * 8 + 8, ds(i * 512 + (j // 2) * 256, 256)], 8, 256
            if ph == "lat":
                return w_mla[:, :, LAT[j][0]:LAT[j][0] + LAT[j][1]], 8, LAT[j][1]
            if ph == "mz":
                return w_mla[:, :, ds(MZ0 + i * 512 + j * 256, 256)], 8, 256
            if ph == "heads":
                if j == 0:
                    return w_kv[:, :, ds(i * 512, 512)], 2, 512
                return w_q[:, :, ds(i * 2 * QK, 2 * QK)], 3, 2 * QK
            if ph == "att":
                return w_in2[:, :, ds(i * 512 + j * 256, 256)], 8, 256
            if ph == "lora":
                return w_in2[:, :, LORA[j][0]:LORA[j][0] + LORA[j][1]], 8, LORA[j][1]
            if ph == "rkv":
                if j == 0:
                    return None, 8, 256
                return w_in2[:, :, ds(i * P + (ATT_IN + 2 * D), P)], 8, P
            if ph == "mix":
                if j < 2:
                    return w_in2[:, :, ds(i * 256 + (GATE0 + j * D), 256)], 8, 256
                return (w_ao if j == 2 else w_ro)[:, :, ds(i * 256, 256)], (4 if j == 2 else 8), 256
            if ph == "wo":
                return w_wo[:, :, ds(i * 512 + j * 256, 256)], 8, 256
            if ph == "up":
                return w_up[:, :, ds(i * 256 + j * D_FF, 256)], 8, 256
            k0 = sum(DOWN_K[:j % 3])
            return w_dn[:, k0:k0 + DOWN_K[j % 3], ds(i * 512 + (j // 3) * 256, 256)], DOWN_K[j % 3], 256

        vec_src = {"conv_w_2": "l j (r c) -> (l j r) c", "r_k_2": "l (r h) e -> (l r) (h e)",
                   "final_norm": "(r c) -> r c", "norm_f_w_2": "(r c) -> r c"}
        vec_dmas = []
        for name, rows in VEC_ROWS:
            full = a[name]
            if name == "mu_shift_2":
                vec_dmas.append((VEC0[name] + 26, 1, 32, full[0:1, 26 * P:RWKV_IN]))
                full, rows = full[:, 0:26 * P], 26
            view = full.rearrange(vec_src[name], h=2) if name == "r_k_2" else \
                full.rearrange(vec_src.get(name, "l (r c) -> (l r) c"), c=P)
            r = 0
            while r < rows:
                n = min(rows - r, P - (VEC0[name] + r) % P)
                vec_dmas.append((VEC0[name] + r, n, P, view[r:r + n, :]))
                r += n
        VEC_DMAS = len(vec_dmas)

        block = ctx.enter_context(nc.Block())

        def phase_loop(eng, n):
            return eng.Fori(0, n) if n > 1 else nullcontext(0)

        @block.sync
        def _(sp):
            sp.dma_start(xin[:, :].rearrange("p (t d) -> p t d", t=4),
                         a["x"].rearrange("b (t p) d -> p (b t) d", p=P)).then_inc(sem("x_loaded"), 16)
            for ph, n, m in STREAM:
                if ph == "heads":
                    sp.wait_ge(sem("n_kv.lo"), 2)
                    sp.wait_ge(sem("krope"), 1)
                def load_strips(i):
                    for j in range(m):
                        s = STRIP0[ph] + i * m + j
                        par = j % 2
                        src, K, W = strip_source(ph, i, j)
                        sp.wait_ge(raw_split, s + 1)
                        dst = raw[par][:, 0:K * W].rearrange("p (k n) -> p k n", k=K)
                        if ph == "rkv" and j == 0:
                            for t in range(2):
                                sp.dma_start(dst[:, :, t * P:(t + 1) * P],
                                             w_in2[:, :, ds(i * P + (ATT_IN + t * D), P)])\
                                    .then_inc(raw_loaded[par], 16)
                            continue
                        sp.dma_start(dst, src).then_inc(raw_loaded[par], 16)

                if ph == "mix":
                    for i in range(n):
                        load_strips(i)
                    continue
                with phase_loop(sp, n) as i:
                    load_strips(i)
                    if ph == "heads":
                        for q in range(3):
                            sp.wait_ge(sem("ada.acc"), i * 3 + q + 1)
                            sp.dma_start(adaw[:, :].rearrange("p (k n) -> p k n", k=DT),
                                         w_ada[:, :, ds(i * 768 + q * 256, 256)]).then_inc(sem("ada.ld"), 16)
            for t in range(4):
                sp.wait_ge(sem("fin.out"), 2 * t + 2)
                sp.dma_start(out[0, t * P:(t + 1) * P, :], yout[t % 2][:, :]).then_inc(sem(f"out_stored{t % 2}"), 16)
            for b in range(2):
                sp.wait_ge(sem(f"out_stored{b}"), 32)

        @block.gpsimd
        def _(pool):
            G.memset(vecrow[:, :], 0.0).then_inc(sem("vecrow_zero"), 1)
            G.memset(ones[:, :], 1.0)
            G.memset(ident[:, :], 0.0)
            G.memset(upad[0][:, 0:PAD], 0.0)
            G.memset(upad[1][:, 0:PAD], 0.0)
            G.memset(eps_c[:, :], EPS)
            G.memset(gneps_c[:, :], GN_EPS)
            for n in (16, 32, 64):
                G.memset(same[n][:, :], 1.0)
            G.iota(cinv[:, :].rearrange("p (g t) -> p g t", g=4), [[0, 4], [1, PAD]], base=1, channel_multiplier=0,
                   allow_small_or_imprecise_dtypes=True)
            pool.drain()
            G.affine_select(out=ident[:, :], in_=ident[:, :], compare_op=ALU.not_equal, fill=1.0, base=0,
                            pattern=[[-1, P]], channel_multiplier=1)
            G.affine_select(out=upper0[:, :], in_=ones[:, :], compare_op=ALU.is_ge, fill=0.0, base=0,
                            pattern=[[1, P]], channel_multiplier=-1)
            G.affine_select(out=upper1[:, :], in_=ones[:, :], compare_op=ALU.is_gt, fill=0.0, base=0,
                            pattern=[[1, P]], channel_multiplier=-1)
            G.affine_select(out=lower1[:, :], in_=ones[:, :], compare_op=ALU.is_gt, fill=0.0, base=0,
                            pattern=[[-1, P]], channel_multiplier=1)
            for n in (16, 32, 64):
                v = same[n][:, :].rearrange("p (b c) -> p b c", c=n)
                G.affine_select(out=v, in_=v, compare_op=ALU.is_ge, fill=0.0, base=0,
                                pattern=[[-n, P // n], [0, n]], channel_multiplier=1)
                pool.drain()
                G.affine_select(out=v, in_=v, compare_op=ALU.is_ge, fill=0.0, base=n - 1,
                                pattern=[[n, P // n], [0, n]], channel_multiplier=-1)
            pool.drain()
            G.memset(res4[0:1, 0:1], 0.0).then_inc(raw_split, RAW_CREDIT)
            pool.drain()
            G.memset(res4[0:1, 0:1], 0.0).then_inc(products_done, SPLIT_CREDIT)
            for name, credit in (("ada.acc", 1), ("ada.col", 1), ("rk.g", 1), ("rk.y", 1), ("mx.lo2", 1),
                                 ("up.conv", 2)):
                pool.drain()
                G.memset(res4[0:1, 0:1], 0.0).then_inc(sem(name), credit)
            pool.drain()
            G.memset(res4[0:1, 0:1], 0.0).then_inc(sem("consts"), 1)
            for ph, n, m in STREAM:
                with phase_loop(pool, n) as i:
                    for j in range(m):
                        s = STRIP0[ph] + i * m + j
                        par = j % 2
                        _, K, W = strip_source(ph, i, j)
                        pool.wait_ge(raw_loaded[par], loaded_value(ph, i, j, m))
                        pool.wait_ge(products_done, done_value(s, 1) - 4)
                        if n > 1:
                            G.tensor_tensor(spare[0:1, 0:1], ones[0:1, 0:1], ones[0:1, 0:1], ALU.mult)
                        r, h, l = raw[par][:, 0:K * W], whi[par][:, 0:K * W], wlo[par][:, 0:K * W]
                        if ph == "heads" and j == 1:
                            n = K * 2 * NOPE
                            r = r.rearrange("p (x c) -> p x c", c=QK)
                            parts = [(r[:, :, lo:hi], *[w[:, o:o + 2 * K * (hi - lo)]
                                                        .rearrange("p (x c) -> p x c", c=hi - lo) for w in (h, l)])
                                     for lo, hi, o in ((0, NOPE, 0), (NOPE, QK, n))]
                            for r_, h_, _ in parts:
                                G.tensor_scalar(h_, r_, 1.0, 1.0, ALU.mult, ALU.mult)
                            pool.drain()
                            for r_, h_, l_ in parts:
                                last = G.tensor_tensor(l_, r_, f32(h_), ALU.subtract)
                            last.then_inc(raw_split, 1)
                            continue
                        G.tensor_scalar(h, r, 1.0, 1.0, ALU.mult, ALU.mult)
                        pool.drain()
                        G.tensor_tensor(l, r, f32(h), ALU.subtract).then_inc(raw_split, 1)

        def act_norm(act, name, srcs, width, src_ready, outs):
            n = len(srcs)
            for d in range(n):
                src_ready(act, d)
                if d >= 2:
                    act.wait_ge(sem(name + ".sum"), d - 1)
                A.activation(tile(sq, d % 2), srcs[d], ACT.Square).then_inc(sem(name + ".sq"), 1)
            act.wait_ge(sem(name + ".sum"), n)
            A.activation(inv[:, :], bank[7][:, :], ACT.Sqrt, scale=1.0 / width, bias=eps_c[:, 0:1])\
                .then_inc(sem(name + ".rms"), 1)
            if outs:
                for d in range(n):
                    act.wait_ge(sem(name + ".hf"), d + 1)
                    A.copy(outs[d][0], tile(hf, d % 2)).then_inc(sem(name + ".hi"), 1)

        def pe_norm(pe, name, n):
            for d in range(n):
                pe.wait_ge(sem(name + ".sq"), d + 1)
                M.matmul(bank[7][:, :], ones[:, :], tile(sq, d % 2), start=(d == 0), stop=(d == n - 1))\
                    .then_inc(sem(name + ".sum"), 1)

        def dve_norm(dve, name, srcs, gains, outs, shifts=None):
            n = len(srcs)
            dve.wait_ge(sem(name + ".rms"), 1)
            V.reciprocal(inv[:, :], inv[:, :])
            dve.drain()
            if not outs:
                for d in range(n):
                    V.scalar_tensor_tensor(srcs[d], srcs[d], gains[d], inv[:, :], ALU.mult, ALU.mult)\
                        .then_inc(sem(name + ".hf"), 1)
                return

            def normed(d):
                if d >= 2:
                    dve.wait_ge(sem(name + ".hi"), d - 1)
                if shifts is None:
                    V.scalar_tensor_tensor(tile(hf, d % 2), srcs[d], gains[d], inv[:, :], ALU.mult, ALU.mult)\
                        .then_inc(sem(name + ".hf"), 1)
                else:
                    V.scalar_tensor_tensor(tile(hf, d % 2), srcs[d], gains[d], inv[:, :], ALU.mult, ALU.mult)
                    dve.drain()
                    V.tensor_scalar(tile(hf, d % 2), tile(hf, d % 2), shifts[d], None, ALU.add)\
                        .then_inc(sem(name + ".hf"), 1)

            normed(0)
            for d in range(n):
                if d + 1 < n:
                    normed(d + 1)
                dve.drain()
                dve.wait_ge(sem(name + ".hi"), d + 1)
                V.tensor_tensor(outs[d][1], tile(hf, d % 2), f32(outs[d][0]), ALU.subtract)\
                    .then_inc(sem(name + ".lo"), 1)
                dve.drain()

        xt = [tile(xT, d) for d in range(DT)]
        h_out = [(hH[d], hL[d]) for d in range(DT)]
        lat_t = [tile(lat, d) for d in range(5)]
        lat_out = [(tile(latH, d), tile(latL, d)) for d in range(5)]
        cols = lambda name, n: [col(name, d) for d in range(n)]

        @block.tensor
        def _(pe):
            def product(dst, slot, W, c0, cw, acts, first=True, last=True, ready=None, half_at=None):
                n = len(acts)
                for k in range(n):
                    wh = whi[slot][:, k * W + c0:k * W + c0 + cw]
                    wl = wlo[slot][:, k * W + c0:k * W + c0 + cw]
                    if ready is not None:
                        pe.wait_ge(ready[0], ready[1] + k)
                    M.matmul(dst, wh, acts[k][0], start=(first and k == 0), stop=False)
                    M.matmul(dst, wh, acts[k][1], start=False, stop=False)
                    mm = M.matmul(dst, wl, acts[k][0], start=False, stop=(last and k == n - 1))
                    if half_at is not None and k + 1 == half_at:
                        mm.then_inc(products_done, 1)
                return mm

            def strip_ready(s):
                pe.wait_ge(raw_split, split_value(s))

            def bank_free(ph, b, n):
                if isinstance(n, int) and fill(ph, b) + n == 0:
                    return
                pe.wait_ge(evac[b], fill(ph, b) + n)

            def two_tiles(ph, s, par, n, acts, ready=None):
                strip_ready(s)
                for j in range(2):
                    b = par * 2 + j
                    bank_free(ph, b, n)
                    product(bank[b][:, :], par, 256, j * P, P, acts, ready=ready if j == 0 else None)\
                        .then_inc(products_done, 1)

            def out_product(ph, acts, ready):
                pe.wait_ge(ready, 16)
                with pe.Fori(0, 2) as i:
                    for nn in range(2):
                        for half in range(2):
                            strip_ready(STRIP0[ph] + i * 4 + nn * 2 + half)
                            for j in range(2):
                                b = nn * 2 + j
                                if half == 0:
                                    bank_free(ph, b, i)
                                product(bank[b][:, :], half, 256, j * P, P, acts[half * 8:half * 8 + 8],
                                        first=(half == 0), last=(half == 1)).then_inc(products_done, 1)

            pe.wait_ge(sem("consts"), 1)
            pe.wait_ge(sem("vec_loaded"), 16 * VEC_DMAS)
            for t in range(VEC_TILES):
                mm = M.transpose(bank[4][:, t * P:(t + 1) * P], vecrow[:, t * P:(t + 1) * P], ident[:, :])
            mm.then_inc(sem("vec.t"), 1)
            pe.wait_ge(sem("x_loaded"), 16)
            for d in range(DT):
                if d >= 2:
                    pe.wait_ge(sem("xt.taken"), d - 1)
                for t in range(4):
                    mm = M.transpose(bank[5 + d % 2][:, t * P:(t + 1) * P],
                                     xin[:, t * D + d * P:t * D + (d + 1) * P], ident[:, :])
                mm.then_inc(sem("xt.t"), 1)

            pe_norm(pe, "n_pool", DT)
            pool_acts = [(tile(poolH, k), tile(poolL, k)) for k in range(4)]
            for g in range(4):
                s0 = STRIP0["pool"] + g * 6
                for j in range(4):
                    two_tiles("pool", s0 + j, j % 2, 3 * g + j // 2, h_out,
                              ready=(sem("n_pool.lo"), 1) if g == 0 and j == 0 else None)
                for j in range(2):
                    two_tiles("pool", s0 + 4 + j, j, 3 * g + 2, pool_acts,
                              ready=(sem("pool.lo"), 4 * g + 1) if j == 0 else None)
            out_product("pool_out", [(tile(y1H, k), tile(y1L, k)) for k in range(16)], sem("pool.ylo"))

            pe_norm(pe, "n_mla", DT)
            for j in range(4):
                s, par, w = STRIP0["lat"] + j, j % 2, LAT[j][1]
                ready = (sem("n_mla.lo"), 1) if j == 0 else None
                if w == 256:
                    two_tiles("lat", s, par, 0, h_out, ready=ready)
                    continue
                strip_ready(s)
                bank_free("lat", par * 2, 1)
                product(bank[par * 2][0:w, :], par, w, 0, w, h_out, half_at=1).then_inc(products_done, 1)
            with pe.Fori(0, 4) as i:
                for j in range(2):
                    two_tiles("mz", STRIP0["mz"] + i * 2 + j, j, i, h_out)
            pe_norm(pe, "n_q", 3)
            pe_norm(pe, "n_kv", 2)
            pe.wait_ge(sem("n_q.lo"), 3)
            pe.wait_ge(sem("n_kv.lo"), 2)
            pe.wait_ge(sem("krope"), 1)
            kv_acts, q_acts = lat_out[3:5], lat_out[0:3]
            with pe.Fori(0, 8) as i:
                sk = STRIP0["heads"] + i * 2
                strip_ready(sk)
                for h in range(2):
                    bank_free("heads", h, i * 2)
                    mm = product(bank[h][:, :], 0, 512, h * 256, P, kv_acts)
                mm.then_inc(products_done, 1)
                for b in (2, 3):
                    bank_free("heads", b, i * 2)
                    for t in range(2):
                        blk = (b - 2) * 2 + t
                        dst = bank[b][:, t * 256:(t + 1) * 256]
                        for k in range(2):
                            wv = [w[0][:, k * 512:(k + 1) * 512].rearrange("p (h c) -> p h c", h=2)[:, :, P:2 * P]
                                  for w in (whi, wlo)]
                            ah, al = [x[:, blk * P:(blk + 1) * P] for x in kv_acts[k]]
                            M.matmul(dst, ah, wv[0], start=(k == 0), stop=False)
                            M.matmul(dst, ah, wv[1], start=False, stop=False)
                            mm = M.matmul(dst, al, wv[0], start=False, stop=(k == 1))
                mm.then_inc(products_done, 1)
                strip_ready(sk + 1)
                for h in range(2):
                    bank_free("heads", h, i * 2 + 1)
                    mm = product(bank[h][:, :], 1, 2 * NOPE, h * NOPE, P, q_acts)
                mm.then_inc(products_done, 1)
                bank_free("heads", 2, i * 2 + 1)
                for k in range(3):
                    r0 = 3 * 2 * NOPE + k * 2 * ROPE
                    wr = [w[1][:, r0:r0 + 2 * ROPE] for w in (whi, wlo)]
                    M.matmul(bank[2][:, :], wr[0], q_acts[k][0], start=(k == 0), stop=False)
                    M.matmul(bank[2][:, :], wr[0], q_acts[k][1], start=False, stop=False)
                    mm = M.matmul(bank[2][:, :], wr[1], q_acts[k][0], start=False, stop=(k == 2))
                mm.then_inc(products_done, 1)
                pe.wait_ge(evac[0], fill("heads", 0) + i * 2 + 2)
                pe.wait_ge(evac[1], fill("heads", 1) + i * 2 + 2)
                pe.wait_ge(evac[2], fill("heads", 2) + i * 2 + 2)
                pe.wait_ge(evac[3], fill("heads", 3) + i * 2 + 1)
                pe.wait_ge(sem("qrope"), i + 1)

                def scores(u):
                    h, qb = u // 4, u % 4
                    w = (qb + 1) * P
                    if u >= 2:
                        pe.wait_ge(sem("m.exp"), i * 8 + u - 1)
                    dst = bank[4 + u % 2]
                    M.matmul(dst[:, 0:w], qT[:, h * S + qb * P:h * S + (qb + 1) * P], kT[:, h * S:h * S + w],
                             start=True, stop=False)
                    M.matmul(dst[:, 0:w], qrope[h * 64:h * 64 + 64, qb * P:(qb + 1) * P],
                             krope[h * 64:h * 64 + 64, 0:w], start=False, stop=True)
                    M.matmul(dst[:, qb * P:w], ident_b[:, :], neg_causal, start=False, stop=True, skip_group_check=True)\
                        .then_inc(sem("m.s"), 1)

                def turned(u):
                    h, qb = u // 4, u % 4
                    pe.wait_ge(sem("m.p"), i * 8 + u + 1)
                    if u >= 1:
                        pe.wait_ge(sem("m.te"), i * 8 + u)
                    for kb in range(qb + 1):
                        mm = M.transpose(bank[6][:, kb * P:(kb + 1) * P], prob[u % 2][:, kb * P:(kb + 1) * P],
                                         ident[:, :])
                    mm.then_inc(sem("m.t"), 1)

                def values(h):
                    pe.wait_ge(sem("m.te"), i * 8 + 4 * h + 4)
                    if h == 1:
                        pe.wait_ge(sem("m.y"), i * 2 + 1)
                    for kb in range(4):
                        mm = M.matmul(bank[7][:, kb * P:S], vN[:, kb * 256 + h * VD:kb * 256 + (h + 1) * VD],
                                      probT[:, kb * S + kb * P:(kb + 1) * S], start=(kb == 0), stop=(kb == 3))
                    mm.then_inc(sem("m.o"), 1)

                scores(0)
                for u in range(1, 8):
                    scores(u)
                    turned(u - 1)
                    if u == 4:
                        values(0)
                turned(7)
                values(1)
                pe.wait_ge(sem("ada.acc"), i * 3 + 4)
                bank_free("heads", 3, i * 2 + 1)
                for t in range(6):
                    mm = M.matmul(bank[3][:, t:t + 1], adaacc[:, t * P:(t + 1) * P], ones[:, 0:1],
                                  start=True, stop=True)
                mm.then_inc(sem("ada.col"), 1)
            out_product("mla_out", [(y2H[:, k * S:(k + 1) * S], tile(y2L, k)) for k in range(16)], sem("m.lo"))

            pe_norm(pe, "n_fin", DT)
            pe_norm(pe, "n_1", DT)
            units_before = 0
            for g in range(3):
                sg = STRIP0["att"] + g * 6
                for kind in range(2):
                    for j in range(2):
                        two_tiles("att", sg + kind * 2 + j, j, 3 * g + kind, h_out,
                                  ready=(sem("n_1.lo"), 1) if g == 0 and kind == 0 and j == 0 else None)
                for j in range(2):
                    strip_ready(sg + 4 + j)
                    for hv in range(2):
                        b = j * 2 + hv
                        bank_free("att", b, 3 * g + 2)
                        for t in range(2):
                            blk = hv * 2 + t
                            dst = bank[b][:, t * 256:(t + 1) * 256]
                            for k in range(DT):
                                if g == 0:
                                    ah, al = [x[:, blk * P:(blk + 1) * P] for x in h_out[k]]
                                else:
                                    ah, al = [x[:, blk:S:4] for x in h_out[k]]
                                wh, wl = whi[j][:, k * 256:(k + 1) * 256], wlo[j][:, k * 256:(k + 1) * 256]
                                M.matmul(dst, ah, wh, start=(k == 0), stop=False)
                                M.matmul(dst, ah, wl, start=False, stop=False)
                                mm = M.matmul(dst, al, wh, start=False, stop=(k == DT - 1))
                        mm.then_inc(products_done, 1)
                for b in range(4):
                    pe.wait_ge(evac[b], fill("att", b) + 3 * g + 3)
                pe.wait_ge(sem("att.vz"), 1)
                units = att_units(g)

                def scores(u):
                    h, blocks = units[u]
                    U = units_before + u
                    if U >= 2:
                        pe.wait_ge(sem("att.exp"), U - 1)
                    dst, rows = bank[4 + U % 2], slice((h % 2) * 64, (h % 2) * 64 + 64)
                    for qb, kb0, nk, c0 in att_rows(blocks):
                        w = nk * P
                        mask = neg_dil[:, :] if g == 2 else neg_band[:, (2 - nk) * P:2 * P]
                        base = (h // 2) * S
                        M.matmul(dst[:, c0:c0 + w], aq[rows, base + qb * P:base + (qb + 1) * P],
                                 ak[rows, base + kb0 * P:base + kb0 * P + w], start=True, stop=False)
                        mm = M.matmul(dst[:, c0:c0 + w], ident_b[:, :], mask, start=False, stop=True)
                    mm.then_inc(sem("att.s"), 1)

                def turned(u):
                    U = units_before + u
                    pe.wait_ge(sem("att.exp"), U + 1)
                    if U >= 1:
                        pe.wait_ge(sem("att.te"), U)
                    for n in range(len(units[u][1])):
                        mm = M.transpose(bank[6][:, n * P:(n + 1) * P], ap_[U % 2][:, n * P:(n + 1) * P],
                                         ident[:, :])
                    mm.then_inc(sem("att.t"), 1)

                def values(u):
                    h, blocks = units[u]
                    U = units_before + u
                    first = h % 2 == 0 and (u == 0 or units[u - 1][0] != h)
                    pe.wait_ge(sem("att.te"), U + 1)
                    if first and 4 * g + h // 2 > 0:
                        pe.wait_ge(sem("att.num"), 4 * g + h // 2)
                    for n, (qb, kb) in enumerate(blocks):
                        v0 = (kb * ATT_HEADS + h) * P
                        mm = M.matmul(bank[7][:, qb * P:(qb + 1) * P], av[:, v0:v0 + P],
                                      apT[U % 2][:, n * P:(n + 1) * P], start=(first and n == 0), stop=True,
                                      skip_group_check=True)
                    mm.then_inc(sem("att.pv"), 1)

                for u in range(len(units) + 2):
                    if u < len(units):
                        scores(u)
                    if 1 <= u <= len(units):
                        turned(u - 1)
                    if u >= 2:
                        values(u - 2)
                units_before += len(units)
            for pr in range(4):
                pe.wait_ge(sem("cmb.f"), (pr + 1) * 3)
                if pr >= 1:
                    pe.wait_ge(sem("cmb.used"), pr)
                for g in range(3):
                    for blk in range(4):
                        cs = slice(blk * P, (blk + 1) * P)
                        mm = M.transpose(bank[4 + g][:, cs], spread[g][:, cs], ident[:, :])
                mm.then_inc(sem("cmb.pe"), 1)

            strip_ready(STRIP0["lora"])
            bank_free("lora", 0, 0)
            product(bank[0][:, :], 0, P, 0, P, h_out, half_at=1).then_inc(products_done, 1)
            strip_ready(STRIP0["lora"] + 1)
            bank_free("lora", 2, 0)
            product(bank[2][:, :], 1, 160, 0, P, h_out).then_inc(products_done, 1)
            bank_free("lora", 3, 0)
            product(bank[3][0:32, :], 1, 160, P, 32, h_out).then_inc(products_done, 1)
            pe.wait_ge(sem("lora.act"), 2)
            pe.wait_ge(sem("rk.zero"), 1)
            with pe.Fori(0, PAIRS) as p:
                s0 = STRIP0["rkv"] + p * 2
                two_tiles("rkv", s0, 0, p, h_out)
                strip_ready(s0 + 1)
                bank_free("rkv", 2, p)
                product(bank[2][:, :], 1, P, 0, P, h_out, half_at=1).then_inc(products_done, 1)
                pe.wait_ge(sem("lw.ld"), (p + 1) * 64)
                pe.wait_ge(sem("rk.y"), p + 1)
                M.matmul(bank[4][:, :], lw2[0:64, :], wlow[0:64, :], start=True, stop=True)
                M.matmul(bank[5][:, :], lw2[64:128, :], wlow[64:128, :], start=True, stop=True)\
                    .then_inc(sem("rk.lora"), 1)
                pe.wait_ge(sem("rk.sq"), p + 1)
                M.matmul(bank[6][:, :], same[64][:, :], tile(sq, 0), start=True, stop=True)\
                    .then_inc(sem("rk.ss"), 1)
                pe.wait_ge(sem("rk.sig"), p + 1)
                pe.wait_ge(sem("rk.v"), p + 1)
                for c in range(4):
                    mm = M.transpose(bank[4][:, c * P:(c + 1) * P], vT[:, c * P:(c + 1) * P], ident[:, :])
                mm.then_inc(sem("rk.tv"), 1)
                pe.wait_ge(sem("rk.ab"), p + 1)
                for c in range(4):
                    mm = M.transpose(bank[5][:, c * P:(c + 1) * P], bT[:, c * P:(c + 1) * P], ident[:, :])
                mm.then_inc(sem("rk.tb"), 1)
                pe.wait_ge(sem("rk.nr"), p + 1)
                pe.wait_ge(sem("rk.kr"), p + 1)
                for c in range(4):
                    mm = M.transpose(bank[6][:, c * P:(c + 1) * P], kkT[:, c * P:(c + 1) * P], ident[:, :])
                mm.then_inc(sem("rk.tk"), 1)
                pe.wait_ge(sem("rk.bon"), p + 1)
                M.matmul(bank[7][:, :], same[64][:, :], tile(hf, 0), start=True, stop=True)\
                    .then_inc(sem("rk.bs"), 1)
                for q, (h, left, right) in enumerate(gram_list()):
                    if q == 0:
                        pe.wait_ge(sem("rk.te"), p * 3 + 3)
                    if q == 3:
                        pe.wait_ge(sem("rk.bonus"), p + 1)
                    if q >= 4:
                        pe.wait_ge(sem("rk.ge"), p * 10 + q - 3)
                    L, R = {"a": aT, "b": bT, "k": kkT, "r": rT}[left], {"a": aT, "b": bT, "k": kkT, "r": rT}[right]
                    rows = slice(h * 64, h * 64 + 64)
                    for c in range(4):
                        mm = M.matmul(bank[4 + q % 4][:, c * P:(c + 1) * P], L[rows, c * P:(c + 1) * P],
                                      R[rows, c * P:(c + 1) * P], start=True, stop=True)
                    mm.then_inc(sem("rk.gram"), 1)
                pe.wait_ge(sem("rk.ge"), p * 10 + 10)
                for k, step in enumerate(INVERSE):
                    for h in range(2):
                        tiles = {"D": IN4, "N4": IN4, "Z": IN4, "DA": IA4, "A4": IA4, "N2": IA8, "A8": IA8,
                                 "A2": IE, "E": IE, "U": IU, "W": IW}
                        if INV_ACT[k]:
                            pe.wait_ge(sem(f"inv{h}.act"), p * INV_ACT[-1] + INV_ACT[k])
                        pe.wait_ge(sem(f"inv{h}.dve"), p * INV_DVE[-1] + INV_DVE[k])
                        for which, (left, right, _, _) in enumerate(step["mm"]):
                            for c in range(4):
                                cs = slice(c * P, (c + 1) * P)
                                dst = bank[4 + 2 * h + which][:, cs]
                                if right == "I":
                                    mm = M.transpose(dst, tiles[left][h][:, cs], ident[:, :])
                                else:
                                    mm = M.matmul(dst, tiles[left][h][:, cs], tiles[right][h][:, cs],
                                                  start=True, stop=True)
                        mm.then_inc(sem(f"inv{h}.pe"), 1)
                for h in range(2):
                    pe.wait_ge(sem(f"inv{h}.dve"), p * INV_DVE[-1] + INV_DVE[-1])
                for c in range(4):
                    cs = slice(c * P, (c + 1) * P)
                    if c > 0:
                        pe.wait_ge(sem("sq.st"), p * 3 + c)
                        M.matmul(bank[4][:, 0:P], aT[:, cs], state[:, :], start=True, stop=True)
                    for h in range(2):
                        mm = M.matmul(bank[4][:, h * 64:h * 64 + 64], Gak[h][:, cs],
                                      vpad[:, c * 256 + h * 192:c * 256 + h * 192 + 64],
                                      start=(c == 0), stop=True, skip_group_check=True)
                    mm.then_inc(sem("sq.r"), 1)
                    if c > 0:
                        M.matmul(bank[7][:, cs], state[:, :], rT[:, cs], start=False, stop=True,
                                 skip_group_check=True)
                    for h in range(2):
                        M.matmul(bank[7][:, cs], vpad[:, c * 256 + h * P:c * 256 + (h + 1) * P], Gqk[h][:, cs],
                                 start=(c == 0 and h == 0), stop=True, skip_group_check=True)
                    pe.wait_ge(sem("sq.re"), p * 4 + c + 1)
                    for h in range(2):
                        mm = M.matmul(bank[5][:, h * 64:h * 64 + 64], IU[h][:, cs], rhs[:, h * 64:h * 64 + 64],
                                      start=True, stop=True)
                    mm.then_inc(sem("sq.sa"), 1)
                    pe.wait_ge(sem("sq.se"), p * 4 + c + 1)
                    if c < 3:
                        M.matmul(bank[6][:, 0:64], bN[:, cs], sapad[:, 0:64], start=True, stop=True,
                                 skip_group_check=True)
                        M.matmul(bank[6][:, 64:P], bN[:, cs], sapad[:, 192:256], start=False, stop=True,
                                 skip_group_check=True)
                        for h in range(2):
                            mm = M.matmul(bank[6][:, h * 64:h * 64 + 64], kN[:, cs],
                                          vpad[:, c * 256 + h * 192:c * 256 + h * 192 + 64],
                                          start=False, stop=True, skip_group_check=True)
                        if c > 0:
                            mm = M.matmul(bank[6][:, 0:P], ident[:, :], state[:, :], start=False, stop=True,
                                          skip_group_check=True)
                        mm.then_inc(sem("sq.s"), 1)
                    for h in range(2):
                        mm = M.matmul(bank[7][:, cs], sapad[:, h * P:(h + 1) * P], Gqb[h][:, cs], start=False,
                                      stop=True, skip_group_check=True)
                mm.then_inc(sem("sq.y"), 1)
                M.matmul(bank[6][:, :], lg2[:, 0:P], tile(glow, 0), start=True, stop=False)
                M.matmul(bank[6][:, :], lg2[0:32, P:2 * P], glow[0:32, S:2 * S], start=False, stop=True)\
                    .then_inc(sem("rk.g"), 1)
                pe.wait_ge(sem("gn.y"), p + 1)
                M.matmul(bank[4][:, :], same[64][:, :], aT[:, :], start=True, stop=True).then_inc(sem("gn.m"), 1)
                pe.wait_ge(sem("gn.q"), p + 1)
                M.matmul(bank[5][:, :], same[64][:, :], bT[:, :], start=True, stop=True).then_inc(sem("gn.v"), 1)

            at_acts = [(tile(atH, k), tile(atL, k)) for k in range(4)]
            r_acts = [(tile(rH, k), tile(rL, k)) for k in range(PAIRS)]
            mix_acts = [(tile(mixH, k), tile(mixL, k)) for k in range(DT)]
            with pe.Fori(0, 4) as i:
                s0 = STRIP0["mix"] + i * 4
                two_tiles("mix", s0, 0, i * 2, h_out)
                two_tiles("mix", s0 + 1, 1, i * 2, h_out)
                pe.wait_ge(sem("mx.lo"), 12)
                two_tiles("mix", s0 + 2, 0, i * 2 + 1, at_acts)
                two_tiles("mix", s0 + 3, 1, i * 2 + 1, r_acts)
            pe.wait_ge(sem("mx.lo2"), 1 + DT)
            with pe.Fori(0, 2) as i:
                for j in range(2):
                    two_tiles("wo", STRIP0["wo"] + i * 2 + j, j, i, mix_acts)

            pe_norm(pe, "n_2", DT)
            pe.wait_ge(sem("n_2.lo"), DT)
            with pe.Fori(0, 11) as i:
                for j in range(2):
                    two_tiles("up", STRIP0["up"] + i * 2 + j, j, i, h_out)
            pe.wait_ge(sem("up.lo"), FT)
            with pe.Fori(0, 2) as i:
                for nn in range(2):
                    for kk_ in range(3):
                        j6 = nn * 3 + kk_
                        k0 = sum(DOWN_K[:kk_])
                        acts = [(tile(fH, k), tile(fL, k)) for k in range(k0, k0 + DOWN_K[kk_])]
                        strip_ready(STRIP0["down"] + i * 6 + j6)
                        for j in range(2):
                            b = nn * 2 + j
                            if kk_ == 0:
                                bank_free("down", b, i)
                            product(bank[b][:, :], j6 % 2, 256, j * P, P, acts, first=(kk_ == 0),
                                    last=(kk_ == 2)).then_inc(products_done, 1)
            pe_norm(pe, "n_out", DT)
            pe.wait_ge(sem("n_out.hf"), DT)
            for q in range(8):
                t, half = q // 2, q % 2
                if q >= 2:
                    pe.wait_ge(sem("fin.out"), q - 1)
                for d in range(4):
                    mm = M.transpose(bank[4 + q % 2][:, d * P:(d + 1) * P],
                                     xT[:, (half * 4 + d) * S + t * P:(half * 4 + d) * S + (t + 1) * P], ident[:, :])
                mm.then_inc(sem("fin.t"), 1)

        @block.scalar
        def _(act):
            act.wait_ge(sem("vecrow_zero"), 1)
            for row, n, w, src in vec_dmas:
                c0 = row // P * P
                act.dma_start(vecrow[row % P:row % P + n, c0:c0 + w], src).then_inc(sem("vec_loaded"), 16)
            for d in range(DT):
                act.wait_ge(sem("xt.t"), d + 1)
                A.copy(xt[d], bank[5 + d % 2][:, :]).then_inc(sem("xt.taken"), 1)

            def product_ready(s, half):
                act.wait_ge(products_done, done_value(s, half))

            act.drain()
            act_norm(act, "n_pool", xt, D, lambda e, d: e.wait_ge(sem("xt.taken"), d + 1), h_out)
            for g in range(4):
                s0 = STRIP0["pool"] + 6 * g
                for t in range(4):
                    n = 4 * g + t
                    if n >= 2:
                        act.wait_ge(sem("pool.win"), n - 1)
                    product_ready(s0 + t // 2, t % 2)
                    A.copy(upad[n % 2][:, PAD:PAD + S], bank[t][:, :]).then_inc(evac[t], 1)
                for t in range(4):
                    if g >= 1:
                        act.wait_ge(evac[t], 3 * g)
                    product_ready(s0 + 2 + t // 2, t % 2)
                    A.activation(tile(zp, t), bank[t][:, :], ACT.Silu).then_inc(evac[t], 1)

            act_norm(act, "n_mla", xt, D, lambda e, d: e.wait_ge(*out_tile_taken("pool_out", d)), h_out)
            act.wait_ge(sem("n_mla.lo"), DT)
            act.dma_start(posi[:, :], a["positions"][0:1, :].partition_broadcast(P)).then_inc(sem("pos_loaded"), 16)
            act.dma_start(invf[:, :], a["inv_freq"]).then_inc(sem("pos_loaded"), 16)
            s0 = STRIP0["lat"]
            for t, (s, half, b) in enumerate(((0, 0, 0), (0, 1, 1), (1, 0, 2), (1, 1, 3), (2, 1, 0))):
                product_ready(s0 + s, half)
                A.copy(lat_t[t], bank[b][:, :]).then_inc(evac[b], 1)
            act.wait_ge(sem("trig.r"), 1)
            A.activation(sinT[:, :], tile(ang, 0), ACT.Sin).then_inc(sem("trig.s"), 1)
            A.activation(tile(ang, 1), tile(ang, 0), ACT.Sin, scale=0.5).then_inc(sem("trig.s"), 1)
            with act.Fori(0, 4) as i:
                for j in range(2):
                    for half in range(2):
                        product_ready(STRIP0["mz"] + i * 2 + j, half)
                        A.activation(dtile(zm, i * 4 + j * 2 + half), bank[j * 2 + half][:, :], ACT.Silu)\
                            .then_inc(evac[j * 2 + half], 1)
            act.drain()
            act_norm(act, "n_q", lat_t[0:3], Q_RANK, lambda e, d: None, lat_out[0:3])
            act.drain()
            act_norm(act, "n_kv", lat_t[3:5], KV_RANK, lambda e, d: None, lat_out[3:5])
            act.wait_ge(sem("n_kv.lo"), 2)
            act.wait_ge(sem("krope"), 1)
            with act.Fori(0, 8) as i:
                sk = STRIP0["heads"] + i * 2
                product_ready(sk, 0)
                for h in range(2):
                    A.activation(tile(kT, h), bank[h][:, :], ACT.Copy, scale=QK_SCALE).then_inc(evac[h], 1)
                product_ready(sk, 1)
                for b in (2, 3):
                    A.copy(vN[:, (b - 2) * 512:(b - 1) * 512], bank[b][:, :]).then_inc(evac[b], 1)
                product_ready(sk + 1, 0)
                for h in range(2):
                    A.copy(tile(qT, h), bank[h][:, :]).then_inc(evac[h], 1)

                def exponentials(u):
                    w = (u % 4 + 1) * P
                    act.wait_ge(sem("m.max"), i * 8 + u + 1)
                    if u >= 2:
                        act.wait_ge(sem("m.t"), i * 8 + u - 1)
                    A.activation(prob[u % 2][:, 0:w], bank[4 + u % 2][:, 0:w], ACT.Exp, bias=stat[:, u % 2:u % 2 + 1],
                                 accum_out=stat[:, 2 + u % 2:3 + u % 2]).then_inc(sem("m.exp"), 1)

                def take_turned(u):
                    qb = u % 4
                    act.wait_ge(sem("m.t"), i * 8 + u + 1)
                    A.copy(probT[:, :].rearrange("p (k q) -> p k q", k=4)[:, 0:qb + 1, qb * P:(qb + 1) * P],
                           bank[6][:, 0:(qb + 1) * P].rearrange("p (k q) -> p k q", q=P)).then_inc(sem("m.te"), 1)

                exponentials(0)
                for u in range(1, 8):
                    exponentials(u)
                    take_turned(u - 1)
                take_turned(7)
                act.wait_ge(sem("ada.col"), i + 2)
                A.copy(ada[:, ds(i * 6, 6)], bank[3][:, 0:6]).then_inc(evac[3], 1)
            act.wait_ge(sem("m.y"), HEADS)
            with act.Fori(0, 16) as i:
                A.copy(dtile(y2H, i), dtile(zm, i)).then_inc(sem("m.hi"), 1)

            act_norm(act, "n_fin", xt, D, lambda e, d: e.wait_ge(*out_tile_taken("mla_out", d)), None)
            act_norm(act, "n_1", xt, D, lambda e, d: e.wait_ge(sem("n_fin.hf"), d + 1), h_out)
            act.wait_ge(sem("n_1.lo"), DT)
            units_before = 0
            for g in range(3):
                sg = STRIP0["att"] + g * 6
                for kind, dst in ((0, aq), (1, ak)):
                    for t in range(4):
                        product_ready(sg + kind * 2 + t // 2, t % 2)
                        o, x = tile(dst, t), bank[t][:, :]
                        if g:
                            o, x = o.rearrange("p (b q) -> p b q", b=4), x.rearrange("p (q b) -> p b q", b=4)
                        A.activation(o, x, ACT.Copy, scale=ATT_DIM ** -0.5 if kind == 0 else 1.0)\
                            .then_inc(evac[t], 1)
                if g == 0:
                    act.wait_ge(sem("att.vz"), 1)
                av6 = av[:, :].rearrange("p (k r par c e) -> p k r par c e", k=4, r=4, par=2, c=2)
                for j in range(2):
                    for hv in range(2):
                        b = j * 2 + hv
                        product_ready(sg + 4 + j, hv)
                        x = bank[b][:, :].rearrange("p (k r par e) -> p k r par e", k=2, r=2, par=2)
                        for par in range(2):
                            cp = A.copy(av6[:, 2 * hv:2 * hv + 2, 2 * j:2 * j + 2, par, par, :], x[:, :, :, par, :])
                        cp.then_inc(evac[b], 1)
                units = att_units(g)

                def take_pair(u):
                    h = units[u][0]
                    act.wait_ge(sem("att.pv"), units_before + u + 1)
                    A.copy(tile(num[g], h // 2), bank[7][:, :]).then_inc(sem("att.num"), 1)

                def pair_ends(u):
                    return units[u][0] % 2 == 1 and (u + 1 == len(units) or units[u + 1][0] != units[u][0])

                for u in range(len(units) + 2):
                    if u < len(units):
                        h, blocks = units[u]
                        U = units_before + u
                        act.wait_ge(sem("att.max"), U + 1)
                        if U >= 2:
                            act.wait_ge(sem("att.t"), U - 1)
                        for qb, kb0, nk, c0 in att_rows(blocks):
                            n = g * 32 + qb * ATT_HEADS + h
                            ex = A.activation(ap_[U % 2][:, c0:c0 + nk * P], bank[4 + U % 2][:, c0:c0 + nk * P],
                                              ACT.Exp, bias=nmax[:, n:n + 1], accum_out=den[:, n:n + 1])
                        ex.then_inc(sem("att.exp"), 1)
                    if u >= 2 and pair_ends(u - 2):
                        take_pair(u - 2)
                units_before += len(units)
            act.wait_ge(sem("att.exp"), units_before)
            act.wait_ge(sem("att.max"), units_before)
            nat = "(B p h) -> p B h"
            for n, x in enumerate((nmax, den)):
                act.dma_start(scratch[n].rearrange(nat, p=P, h=ATT_HEADS),
                              x[:, 0:32].rearrange("p (B h) -> p B h", h=ATT_HEADS)).then_inc(sem("st.out"), 16)
            act.wait_ge(sem("st.out"), 32)
            for n in range(2):
                act.dma_start(stq[:, n * 32:n * 32 + 32], scratch[n].rearrange("(q c) -> q c", q=P))\
                    .then_inc(sem("st.in"), 16)
            act.wait_ge(sem("st.d"), 1)
            A.activation(fac[:, :], fac[:, :], ACT.Exp).then_inc(sem("st.e"), 1)
            act.wait_ge(sem("st.f"), 1)
            act.dma_start(scratch[2].rearrange("(q c) -> q c", q=P), fac[:, 0:32]).then_inc(sem("st.out"), 16)
            act.wait_ge(sem("st.out"), 48)
            act.dma_start(fac0[:, :].rearrange("p (B h) -> p B h", h=ATT_HEADS),
                          scratch[2].rearrange(nat, p=P, h=ATT_HEADS)).then_inc(sem("st.f0"), 16)
            act.wait_ge(sem("st.f0"), 16)
            act.wait_ge(sem("att.pv"), units_before)
            for pr in range(4):
                if pr >= 1:
                    act.wait_ge(sem("cmb.pe"), pr)
                for g in range(3):
                    f = (fac0 if g == 0 else fac[:, 32 * g:32 * g + 32])[:, :]
                    f = f.rearrange("p (k h) -> p k h", k=4)[:, :, 2 * pr:2 * pr + 2]
                    A.copy(spread[g][:, :].rearrange("p (k h e) -> p k h e", k=4, h=2),
                           f.unsqueeze(3).to_broadcast([P, 4, 2, 64])).then_inc(sem("cmb.f"), 1)

            act.wait_ge(sem("att.at"), 4)
            s0 = STRIP0["lora"]
            for z, s, half, b, rows in ((0, 0, 1, 0, P), (1, 1, 0, 2, P), (2, 1, 1, 3, 32)):
                product_ready(s0 + s, half)
                A.copy(zsh[z][0:rows, 1:S + 1], bank[b][0:rows, :]).then_inc(evac[b], 1)
            act.wait_ge(sem("lora.z"), 3)
            A.activation(wlow[0:64, :], wlow[0:64, :], ACT.Tanh).then_inc(sem("lora.act"), 1)
            A.activation(tile(glow, 0), tile(glow, 0), ACT.Sigmoid)
            A.activation(glow[0:32, S:2 * S], glow[0:32, S:2 * S], ACT.Sigmoid).then_inc(sem("lora.act"), 1)
            with act.Fori(0, PAIRS) as p:
                s0 = STRIP0["rkv"] + p * 2
                act.wait_ge(sem("rk.g"), p + 1)
                for dst, src in ((lw2[0:64, :], a["w2_2"][0, :, ds(p * P, P)]),
                                 (lw2[64:128, :], a["a2_2"][0, :, ds(p * P, P)]),
                                 (lg2[:, 0:P], a["g2_2"][0, 0:P, ds(p * P, P)]),
                                 (lg2[0:32, P:2 * P], a["g2_2"][0, P:160, ds(p * P, P)])):
                    act.dma_start(dst, src).then_inc(sem("lw.ld"), 16)
                for z, (s, half) in enumerate(((0, 0), (0, 1), (1, 1))):
                    product_ready(s0 + s, half)
                    A.copy(zsh[z][:, 1:S + 1], bank[z][:, :]).then_inc(evac[z], 1)
                act.wait_ge(sem("rk.kk"), p + 1)
                A.activation(tile(sq, 0), kk[:, :], ACT.Square).then_inc(sem("rk.sq"), 1)
                act.wait_ge(sem("rk.lora"), p + 1)
                A.activation(lwd[:, :], bank[4][:, :], ACT.Sigmoid, bias=pcol[:, 3:4])
                A.activation(aa[:, :], bank[5][:, :], ACT.Sigmoid, bias=pcol[:, 4:5]).then_inc(sem("rk.sig"), 1)
                act.wait_ge(sem("rk.ss"), p + 1)
                A.activation(tile(sq, 1), bank[6][:, :], ACT.Sqrt).then_inc(sem("rk.nr"), 1)
                act.wait_ge(sem("rk.tv"), p + 1)
                vp = vpad[:, :].rearrange("p (c x) -> p c x", c=4)
                vb = bank[4][:, :].rearrange("p (c h e) -> p c h e", c=4, h=2)
                A.copy(vp[:, :, 0:64], vb[:, :, 0, :])
                A.copy(vp[:, :, 192:256], vb[:, :, 1, :]).then_inc(sem("rk.te"), 1)
                act.wait_ge(sem("rk.lp"), p + 1)
                A.activation(epos[:, :], cc[:, :], ACT.Exp)
                A.activation(fade[:, 0:3], fade[:, 0:3], ACT.Exp)
                A.activation(lwd[:, :], lwd[:, :], ACT.Exp)
                act.drain()
                A.activation(cc[:, :], cc[:, :], ACT.Exp, scale=-1.0).then_inc(sem("rk.ex"), 1)
                act.wait_ge(sem("rk.tb"), p + 1)
                A.copy(bN[:, :], bank[5][:, :]).then_inc(sem("rk.te"), 1)
                act.wait_ge(sem("rk.tk"), p + 1)
                A.copy(kN[:, :], bank[6][:, :]).then_inc(sem("rk.te"), 1)
                goes = {"N2": IA8, "N4": IN4, "A4": IA4, "A8": IA8, "W": IW, "Z": IN4}
                for k, step in enumerate(INVERSE):
                    for h in range(2):
                        for which, (_, _, by, to) in enumerate(step["mm"]):
                            if by == "act":
                                act.wait_ge(sem(f"inv{h}.pe"), p * len(INVERSE) + k + 1)
                                A.copy(goes[to][h][:, :], bank[4 + 2 * h + which][:, :]).then_inc(sem(f"inv{h}.act"), 1)
                for c in range(4):
                    act.wait_ge(sem("sq.r"), p * 4 + c + 1)
                    A.copy(rhs[:, :], bank[4][:, 0:P]).then_inc(sem("sq.re"), 1)
                    act.wait_ge(sem("sq.sa"), p * 4 + c + 1)
                    A.copy(sapad[:, 0:64], bank[5][:, 0:64])
                    A.copy(sapad[:, 192:256], bank[5][:, 64:P]).then_inc(sem("sq.se"), 1)
                act.wait_ge(sem("sq.y"), p + 1)
                A.activation(aT[:, :], bank[7][:, :], ACT.Copy, scale=SCAN_SCALE ** -2).then_inc(sem("gn.y"), 1)
                act.wait_ge(sem("gn.c"), p + 1)
                A.activation(bT[:, :], rT[:, :], ACT.Square).then_inc(sem("gn.q"), 1)
                act.wait_ge(sem("gn.v"), p + 1)
                A.activation(kkT[:, :], bank[5][:, :], ACT.Sqrt, scale=1.0 / 64, bias=gneps_c[:, 0:1])\
                    .then_inc(sem("gn.s"), 1)

            act.wait_ge(sem("rk.y"), 1 + PAIRS)
            act.wait_ge(sem("n_1.lo"), DT)
            for k in range(12):
                src, dst = (tile(at, k), tile(atH, k)) if k < 4 else (tile(yr, k - 4), tile(rH, k - 4))
                A.copy(dst, src).then_inc(sem("mx.hi"), 1)
            with act.Fori(0, 4) as i:
                s0 = STRIP0["mix"] + i * 4
                for j, buf in enumerate((sq, hf)):
                    for half in range(2):
                        act.wait_ge(sem("mx.lo2"), i * 2 + 1)
                        product_ready(s0 + j, half)
                        A.activation(tile(buf, half), bank[2 * j + half][:, :], ACT.Sigmoid,
                                     bias=dcol("b_gate_2", i * 2 + (j * DT + half))).then_inc(evac[2 * j + half], 1)

            act_norm(act, "n_2", xt, D, lambda e, d: e.wait_ge(*out_tile_taken("wo", d)), h_out)
            act.wait_ge(sem("n_2.lo"), DT)
            act.wait_ge(sem("up.zero"), 1)
            with act.Fori(0, 11) as i:
                s0 = STRIP0["up"] + i * 2
                for t in range(4):
                    act.wait_ge(sem("up.conv"), i * 4 + t + 1)
                    product_ready(s0 + t // 2, t % 2)
                    A.copy(cpad[t % 2][:, 2:2 + S], bank[t][:, :]).then_inc(evac[t], 1)
                    if t >= 2:
                        act.wait_ge(sem("up.conv"), i * 4 + t + 1)
                        A.activation(tile(sq, t - 2), tile(sq, t - 2), ACT.Silu).then_inc(sem("up.silu"), 1)
            act_norm(act, "n_out", xt, D, lambda e, d: e.wait_ge(*out_tile_taken("down", d)), None)
            for q in range(8):
                t, half = q // 2, q % 2
                act.wait_ge(sem("fin.t"), q + 1)
                if t >= 2:
                    act.wait_ge(sem(f"out_stored{t % 2}"), 16)
                A.copy(yout[t % 2][:, half * S:(half + 1) * S], bank[4 + q % 2][:, :]).then_inc(sem("fin.out"), 1)

        @block.vector
        def _(dve):
            def product_ready(s, half):
                dve.wait_ge(products_done, done_value(s, half))

            def split(hi, lo, x):
                V.tensor_copy(hi, x)
                dve.drain()
                return V.tensor_tensor(lo, x, f32(hi), ALU.subtract)

            dve.wait_ge(sem("consts"), 1)
            V.tensor_tensor(up16[:, :], upper1[:, :], same[16][:, :], ALU.mult)
            V.tensor_tensor(low16[:, :], lower1[:, :], same[16][:, :], ALU.mult)
            for n, wide in ((16, same[32]), (32, same[64]), (64, ones)):
                V.tensor_tensor(step_mask[n][:, :], wide[:, :], same[n][:, :], ALU.subtract)
            V.tensor_reduce(res4[:, :], ident[:, :].rearrange("p (k r) -> p r k", r=4), AX.X, ALU.add)
            V.tensor_tensor(tmp_mask[:, :], lower1[:, :], ident[:, :], ALU.add)
            V.tensor_copy(ident_b[:, :], ident[:, :])
            V.tensor_scalar(neg_band[:, P:2 * P], upper1[:, :], -BIG, None, ALU.mult)
            V.tensor_scalar(neg_band[:, 0:P], lower1[:, :], -BIG, None, ALU.mult)
            for g, w in enumerate(POOL_WINDOWS):
                V.tensor_scalar(cinv[:, g * PAD:(g + 1) * PAD], cinv[:, g * PAD:(g + 1) * PAD], float(w), None, ALU.min)
            dve.drain()
            V.reciprocal(cinv[:, :], cinv[:, :])
            for n in (16, 32, 64):
                V.tensor_tensor(step_mask[n][:, :], step_mask[n][:, :], lower1[:, :], ALU.mult)
            m4 = tmp_mask[:, :].rearrange("p (k r) -> p k r", r=4)
            V.tensor_tensor(m4, m4, res4[:, :].unsqueeze(1).to_broadcast([P, 32, 4]), ALU.mult)
            dve.drain()
            V.tensor_scalar(neg_dil[:, :], tmp_mask[:, :], BIG, -BIG, ALU.mult, ALU.add).then_inc(sem("masks"), 1)
            dve.wait_ge(sem("vec.t"), 1)
            V.tensor_copy(vec[:, :], bank[4][:, 0:VEC_ALL]).then_inc(sem("vec.ready"), 1)
            dve.drain()
            V.tensor_scalar(one_minus_ka[:, :], vec[:, VEC0["k_a_2"]:VEC0["k_a_2"] + DT], -1.0, 1.0, ALU.mult, ALU.add)

            dve_norm(dve, "n_pool", xt, cols("pool_norm", DT), h_out)
            dve.drain()
            W_ = PAD + S
            tmp = [sq[:, 0:W_], hf[:, 0:W_]]
            for g, w in enumerate(POOL_WINDOWS):
                s0 = STRIP0["pool"] + 6 * g
                for t in range(4):
                    u = upad[t % 2]
                    dve.wait_ge(evac[t], 3 * g + 1)
                    cur = u[:, :]
                    for l in range(g + 1):
                        sh, nxt = 1 << l, tmp[l % 2]
                        V.tensor_tensor(nxt[:, 2 * sh - 1:W_], cur[:, 2 * sh - 1:W_], cur[:, sh - 1:W_ - sh], ALU.add)
                        dve.drain()
                        cur = nxt
                    mean = tmp[(g + 1) % 2][:, PAD:W_]
                    V.scalar_tensor_tensor(mean, cur[:, PAD:W_], 1.0 / w, u[:, PAD:W_], ALU.mult, ALU.subtract)
                    V.tensor_tensor(inv[:, 0:PAD], cur[:, PAD:2 * PAD], cinv[:, g * PAD:(g + 1) * PAD], ALU.mult)
                    dve.drain()
                    V.tensor_tensor(mean[:, 0:PAD], inv[:, 0:PAD], u[:, PAD:2 * PAD], ALU.subtract)\
                        .then_inc(sem("pool.win"), 1)
                    dve.drain()
                    if g >= 1 and t == 0:
                        product_ready(s0 - 1, 1)
                    split(tile(poolH, t), tile(poolL, t), mean).then_inc(sem("pool.lo"), 1)
                    dve.drain()
                for t in range(4):
                    product_ready(s0 + 4 + t // 2, t % 2)
                    dve.wait_ge(evac[t], 3 * g + 2)
                    y = tmp[t % 2][:, 0:S]
                    V.scalar_tensor_tensor(y, bank[t][:, :], col("pool_scale", 4 * g + t), tile(zp, t),
                                           ALU.mult, ALU.mult).then_inc(evac[t], 1)
                    dve.drain()
                    split(tile(y1H, 4 * g + t), tile(y1L, 4 * g + t), y).then_inc(sem("pool.ylo"), 1)
                    dve.drain()

            def residual(ph):
                with dve.Fori(0, 2) as i:
                    for nn in range(2):
                        for j in range(2):
                            product_ready(STRIP0[ph] + i * 4 + nn * 2 + 1, j)
                            x = dtile(xT, i * 4 + nn * 2 + j)
                            V.tensor_tensor(x, bank[nn * 2 + j][:, :], x, ALU.add).then_inc(evac[nn * 2 + j], 1)

            residual("pool_out")

            dve.drain()
            dve_norm(dve, "n_mla", xt, cols("mla_norm", DT), h_out)
            dve.wait_ge(sem("pos_loaded"), 32)
            a0_, a1_, a2_ = [tile(ang, n) for n in range(3)]
            V.tensor_copy(a0_, posi[:, :])
            dve.drain()
            V.tensor_scalar(a0_, a0_, invf[:, 0:1], None, ALU.mult)
            dve.drain()
            V.tensor_scalar(a1_, a0_, 1.0 / (2.0 * np.pi), ROUND, ALU.mult, ALU.add)
            dve.drain()
            V.tensor_scalar(a1_, a1_, ROUND, None, ALU.subtract)
            for part in TWO_PI:
                dve.drain()
                V.scalar_tensor_tensor(a0_, a1_, -part, a0_, ALU.mult, ALU.add)
            dve.drain()
            V.tensor_scalar(a0_, a0_, PI_IN, -PI_IN, ALU.min, ALU.max).then_inc(sem("trig.r"), 1)
            dve.wait_ge(sem("trig.s"), 2)
            V.tensor_tensor(cosT[:, :], a1_, a1_, ALU.mult)
            V.tensor_scalar(sinT[0:32, :], sinT[0:32, :], -1.0, None, ALU.mult)
            V.tensor_scalar(sinT[64:96, :], sinT[64:96, :], -1.0, None, ALU.mult)
            dve.drain()
            V.tensor_scalar(cosT[:, :], cosT[:, :], -2.0, 1.0, ALU.mult, ALU.add)
            dve.drain()

            def rotate(x, t, turned, rows):
                V.tensor_tensor(t, x[0:rows, :], cosT[0:rows, :], ALU.mult)
                for q in range(0, rows, 32):
                    o = q ^ 32
                    last = V.tensor_tensor(turned[q:q + 32, :], x[o:o + 32, :], sinT[q:q + 32, :], ALU.mult)
                return last

            product_ready(STRIP0["lat"] + 3, 1)
            rotate(bank[2], a2_[0:64, :], a1_, 64).then_inc(evac[2], 1)
            dve.drain()
            V.tensor_tensor(a2_[0:64, :], a2_[0:64, :], a1_[0:64, :], ALU.add)
            dve.drain()
            V.tensor_scalar(krope[0:64, :], a2_[0:64, :], QK_SCALE, None, ALU.mult)
            V.tensor_scalar(krope[64:128, :], a2_[0:64, :], QK_SCALE, None, ALU.mult).then_inc(sem("krope"), 1)
            dve.drain()
            dve_norm(dve, "n_q", lat_t[0:3], cols("mla_q_norm", 3), lat_out[0:3])
            dve.drain()
            dve_norm(dve, "n_kv", lat_t[3:5], cols("mla_kv_norm", 2), lat_out[3:5])
            dve.drain()
            with dve.Fori(0, 8) as i:
                def ada_strip(q):
                    dve.wait_ge(sem("ada.ld"), (i * 3 + q + 1) * 16)
                    acc = adaacc[:, q * 256:(q + 1) * 256]
                    for k in range(DT):
                        w = adaw[:, k * 256:(k + 1) * 256]
                        if k == 0:
                            V.tensor_scalar(acc, w, col("c_2", k), None, ALU.mult)
                        else:
                            last = V.scalar_tensor_tensor(acc, w, col("c_2", k), acc, ALU.mult, ALU.add)
                        if k < DT - 1:
                            dve.drain()
                    last.then_inc(sem("ada.acc"), 1)

                dve.wait_ge(sem("ada.col"), i + 1)
                ada_strip(0)
                dve.drain()
                product_ready(STRIP0["heads"] + i * 2 + 1, 1)
                rotate(bank[2], tile(sq, 0), tile(sq, 1), P).then_inc(evac[2], 1)
                dve.drain()
                V.tensor_tensor(qrope[:, :], tile(sq, 0), tile(sq, 1), ALU.add).then_inc(sem("qrope"), 1)

                def maximum(u):
                    w = (u % 4 + 1) * P
                    dve.wait_ge(sem("m.s"), i * 8 + u + 1)
                    V.tensor_reduce(stat[:, u % 2:u % 2 + 1], bank[4 + u % 2][:, 0:w], AX.X, ALU.max, negate=True)\
                        .then_inc(sem("m.max"), 1)

                def divide(u):
                    w = (u % 4 + 1) * P
                    dve.wait_ge(sem("m.exp"), i * 8 + u + 1)
                    V.reciprocal(stat[:, 4 + u % 2:5 + u % 2], stat[:, 2 + u % 2:3 + u % 2])
                    dve.drain()
                    V.tensor_scalar(prob[u % 2][:, 0:w], prob[u % 2][:, 0:w], stat[:, 4 + u % 2:5 + u % 2], None,
                                    ALU.mult).then_inc(sem("m.p"), 1)

                def gated(h):
                    dve.wait_ge(sem("m.o"), i * 2 + h + 1)
                    z = dtile(zm, i * 2 + h)
                    V.tensor_tensor(z, bank[7][:, :], z, ALU.mult).then_inc(sem("m.y"), 1)

                maximum(0)
                for u in range(1, 8):
                    maximum(u)
                    divide(u - 1)
                    if u == 5:
                        gated(0)
                        dve.drain()
                        ada_strip(1)
                divide(7)
                gated(1)
                dve.drain()
                ada_strip(2)
            dve.drain()
            with dve.Fori(0, 16) as i:
                dve.wait_ge(sem("m.hi"), i + 1)
                V.tensor_tensor(dtile(y2L, i), dtile(zm, i), f32(dtile(y2H, i)), ALU.subtract).then_inc(sem("m.lo"), 1)
            residual("mla_out")

            dve.wait_ge(evac[3], fill("heads", 3) + 16)
            V.tensor_tensor(ada[:, :], ada[:, :], vec[:, VEC0["b_ada_2"]:VEC0["b_ada_2"] + 48], ALU.add)
            dve.drain()
            for gain, name, c0 in ((gain1, "norm1_w_2", DT), (gain2, "norm2_w_2", 4 * DT)):
                V.scalar_tensor_tensor(gain[:, :], ada[:, c0:c0 + DT], 1.0, vec[:, VEC0[name]:VEC0[name] + DT],
                                       ALU.add, ALU.mult)
            dve.drain()
            dve_norm(dve, "n_fin", xt, cols("final_norm", DT), None)
            dve.drain()
            dve_norm(dve, "n_1", xt, [gain1[:, d:d + 1] for d in range(DT)], h_out,
                     [ada[:, d:d + 1] for d in range(DT)])
            dve.drain()
            V.memset(av[:, :], 0.0).then_inc(sem("att.vz"), 1)
            units_before = 0
            for g in range(3):
                units = att_units(g)

                def maxima(u):
                    h, blocks = units[u]
                    U = units_before + u
                    dve.wait_ge(sem("att.s"), U + 1)
                    rows = att_rows(blocks)
                    runs = [rows[:1], rows[1:]] if rows[0][2] != rows[-1][2] else [rows]
                    for run in runs:
                        qb, _, nk, c0 = run[0]
                        n = len(run)
                        x = bank[4 + U % 2][:, c0:c0 + n * nk * P].rearrange("p (n w) -> p n w", n=n)
                        m0 = g * 32 + qb * ATT_HEADS + h
                        last = V.tensor_reduce(nmax[:, m0:m0 + (n - 1) * ATT_HEADS + 1:ATT_HEADS], x, AX.X, ALU.max,
                                               negate=True)
                    last.then_inc(sem("att.max"), 1)

                def take_turned(u):
                    U = units_before + u
                    w = len(units[u][1]) * P
                    dve.wait_ge(sem("att.t"), U + 1)
                    if U >= 2:
                        dve.wait_ge(sem("att.pv"), U - 1)
                    V.tensor_copy(apT[U % 2][:, 0:w], bank[6][:, 0:w]).then_inc(sem("att.te"), 1)

                for u in range(len(units) + 1):
                    if u < len(units):
                        maxima(u)
                    if u >= 1:
                        take_turned(u - 1)
                units_before += len(units)
            dve.wait_ge(sem("st.in"), 32)
            negs = [stq[:, 0:32], nmax[:, 32:64], nmax[:, 64:96]]
            dens = [stq[:, 32:64], den[:, 32:64], den[:, 64:96]]
            facs = [fac[:, 32 * g:32 * g + 32] for g in range(3)]
            V.tensor_tensor(zden[:, :], negs[0], negs[1], ALU.min)
            dve.drain()
            V.tensor_tensor(zden[:, :], zden[:, :], negs[2], ALU.min)
            dve.drain()
            for g in range(3):
                last = V.tensor_tensor(facs[g], zden[:, :], negs[g], ALU.subtract)
            last.then_inc(sem("st.d"), 1)
            dve.wait_ge(sem("st.e"), 1)
            for g in range(3):
                V.tensor_tensor(dens[g], dens[g], facs[g], ALU.mult)
            dve.drain()
            V.tensor_tensor(zden[:, :], dens[0], dens[1], ALU.add)
            dve.drain()
            V.tensor_tensor(zden[:, :], zden[:, :], dens[2], ALU.add)
            dve.drain()
            V.reciprocal(zden[:, :], zden[:, :])
            dve.drain()
            for g in range(3):
                last = V.tensor_tensor(facs[g], facs[g], zden[:, :], ALU.mult)
            last.then_inc(sem("st.f"), 1)
            dve.wait_ge(sem("att.num"), 12)
            for pr in range(4):
                dve.wait_ge(sem("cmb.pe"), pr + 1)
                n_ = [tile(num[g], pr) for g in range(3)]
                for g in range(3):
                    last = V.tensor_tensor(n_[g], n_[g], bank[4 + g][:, :], ALU.mult)
                last.then_inc(sem("cmb.used"), 1)
                dve.drain()
                V.tensor_tensor(n_[1], n_[1], n_[2], ALU.add)
                dve.drain()
                V.tensor_tensor(tile(at, pr).rearrange("p (q b) -> p b q", b=4), n_[1].rearrange("p (b q) -> p b q", b=4),
                                n_[0].rearrange("p (q b) -> p b q", b=4), ALU.add).then_inc(sem("att.at"), 1)
            dve.drain()

            def shifted(z, mu, out_, rows=P):
                V.tensor_tensor(sq[0:rows, 0:S], z[0:rows, 0:S], z[0:rows, 1:S + 1], ALU.subtract)
                dve.drain()
                return V.scalar_tensor_tensor(out_, sq[0:rows, 0:S], mu, z[0:rows, 1:S + 1], ALU.mult, ALU.add)

            mu = VEC0["mu_shift_2"]
            dve.wait_ge(sem("cmb.pe"), 4)
            for z in range(3):
                V.memset(zsh[z][:, 0:1], 0.0)
            V.memset(vpad[:, :], 0.0)
            V.memset(sapad[:, :], 0.0)
            V.memset(state[:, :], 0.0)
            V.memset(rmask[:, :], 1.0)
            dve.drain()
            V.memset(rmask[:, 0:S:P], 0.0).then_inc(sem("rk.zero"), 1)
            dve.drain()
            for n, (z, b, out_, rows) in enumerate(((0, 0, wlow[:, :], P), (1, 2, tile(glow, 0), P),
                                                    (2, 3, glow[0:32, S:2 * S], 32))):
                dve.wait_ge(evac[b], fill("lora", b) + 1)
                shifted(zsh[z], vec[0:rows, mu + 24 + n:mu + 25 + n], out_, rows).then_inc(sem("lora.z"), 1)
                dve.drain()
            with dve.Fori(0, PAIRS) as p:
                for z in range(3):
                    V.memset(zsh[z][:, 0:1], 0.0)
                V.tensor_copy(pcol[:, 0:3], vec[:, mu:mu + 24].rearrange("p (j r) -> p j r", j=3)[:, :, ds(p, 1)])
                w0 = VEC0["w0_2"]
                V.tensor_copy(pcol[:, 3:10], vec[:, w0:w0 + 56].rearrange("p (j r) -> p j r", j=7)[:, :, ds(p, 1)])
                V.tensor_copy(pcol[:, 10:11], one_minus_ka[:, ds(p, 1)])
                dve.drain()
                kk_c, ka_c, rk_c, lw_c, lb_c, oka_c = [pcol[:, n:n + 1] for n in (5, 6, 7, 8, 9, 10)]
                for z, out_ in enumerate((Rr, Kr, vT)):
                    dve.wait_ge(evac[z], p + (fill("rkv", z) + 1))
                    last = shifted(zsh[z], pcol[:, z:z + 1], out_[:, :])
                    if z == 2:
                        last.then_inc(sem("rk.v"), 1)
                    dve.drain()
                V.tensor_scalar(kk[:, :], Kr[:, :], kk_c, None, ALU.mult).then_inc(sem("rk.kk"), 1)
                dve.wait_ge(sem("rk.sig"), p + 1)
                V.tensor_scalar(lwd[:, :], lwd[:, :], -float(np.exp(-0.5)), None, ALU.mult)
                dve.drain()
                V.tensor_tensor_scan(csum[:, :], rmask[:, :], lwd[:, :], 0.0, ALU.mult, ALU.add)
                dve.drain()
                c4 = csum[:, :].rearrange("p (c t) -> p c t", c=4)
                V.tensor_tensor(cc[:, :].rearrange("p (c t) -> p c t", c=4), c4,
                                c4[:, :, CH - 1:CH].to_broadcast([P, 4, P]), ALU.subtract)
                dve.drain()
                V.tensor_tensor(fade[:, 0:3], cc[:, P - 1:3 * P:P], csum[:, P + CH - 1:S:P], ALU.add)
                V.tensor_tensor(lwd[:, :], cc[:, :], lwd[:, :], ALU.subtract).then_inc(sem("rk.lp"), 1)
                dve.wait_ge(sem("rk.nr"), p + 1)
                V.tensor_scalar(tile(sq, 1), tile(sq, 1), 1e-12, None, ALU.max)
                dve.drain()
                V.reciprocal(tile(sq, 1), tile(sq, 1))
                dve.drain()
                V.tensor_tensor(kk[:, :], kk[:, :], tile(sq, 1), ALU.mult)
                dve.drain()
                dve.wait_ge(sem("rk.ex"), p + 1)
                V.scalar_tensor_tensor(aT[:, :], kk[:, :], -1.0, lwd[:, :], ALU.mult, ALU.mult)
                V.tensor_tensor(bT[:, :], kk[:, :], aa[:, :], ALU.mult)
                dve.drain()
                V.tensor_tensor(bT[:, :], bT[:, :], cc[:, :], ALU.mult).then_inc(sem("rk.ab"), 1)
                V.tensor_scalar(aa[:, :], aa[:, :], ka_c, oka_c, ALU.mult, ALU.add)
                dve.drain()
                V.tensor_tensor(Kr[:, :], Kr[:, :], aa[:, :], ALU.mult)
                dve.drain()
                V.scalar_tensor_tensor(kkT[:, :], Kr[:, :], SCAN_SCALE, cc[:, :], ALU.mult, ALU.mult)
                V.scalar_tensor_tensor(rT[:, :], Rr[:, :], SCAN_SCALE, epos[:, :], ALU.mult, ALU.mult)\
                    .then_inc(sem("rk.kr"), 1)
                V.scalar_tensor_tensor(tile(hf, 0), Kr[:, :], rk_c, Rr[:, :], ALU.mult, ALU.mult)\
                    .then_inc(sem("rk.bon"), 1)
                dve.wait_ge(sem("rk.bs"), p + 1)
                V.tensor_tensor(bonus[:, :], bank[7][:, :], vT[:, :], ALU.mult).then_inc(sem("rk.bonus"), 1)
                dve.drain()

                def masked(dst, x, mask):
                    m = mask[:, :].unsqueeze(1).to_broadcast([P, 4, P])
                    return V.tensor_tensor(dst[:, :].rearrange("p (c t) -> p c t", c=4),
                                           x.rearrange("p (c t) -> p c t", c=4), m, ALU.mult)

                for q, (h, left, right) in enumerate(gram_list()):
                    dve.wait_ge(sem("rk.gram"), p * 10 + q + 1)
                    x = bank[4 + q % 4][:, :]
                    if (left, right) == ("b", "a"):
                        last = masked(IN4[h], x, up16)
                    elif (left, right) == ("a", "b"):
                        masked(IA[h], x, lower1)
                        last = masked(IA4[h], x, low16)
                    elif right == "a":
                        last = masked(Gak[h], x, upper1)
                    else:
                        last = masked(Gqb[h] if left == "b" else Gqk[h], x, upper0)
                    last.then_inc(sem("rk.ge"), 1)
                dve.drain()
                for h in range(2):
                    V.tensor_tensor(IU[h].rearrange("p (c t) -> p c t", c=4),
                                    IN4[h][:, :].rearrange("p (c t) -> p c t", c=4),
                                    ident[:, :].unsqueeze(1).to_broadcast([P, 4, P]), ALU.add)\
                        .then_inc(sem(f"inv{h}.dve"), 1)
                for k, step in enumerate(INVERSE):
                    for h in range(2):
                        waited = False
                        for which, (_, _, by, to) in enumerate(step["mm"]):
                            if by != "dve":
                                continue
                            if not waited:
                                dve.drain()
                                dve.wait_ge(sem(f"inv{h}.pe"), p * len(INVERSE) + k + 1)
                                waited = True
                            x = bank[4 + 2 * h + which][:, :]
                            if to == "A2":
                                last = V.tensor_copy(IE[h][:, :], x)
                            else:
                                dst = IU[h] if to == "+U" else IW[h]
                                last = V.tensor_tensor(dst, x, dst, ALU.add)
                            last.then_inc(sem(f"inv{h}.dve"), 1)
                        if "E" in step:
                            masked(IE[h], IA[h][:, :], step_mask[step["E"]]).then_inc(sem(f"inv{h}.dve"), 1)
                for c in range(3):
                    dve.wait_ge(sem("sq.s"), p * 3 + c + 1)
                    V.tensor_scalar(state[0:64, 0:64], bank[6][0:64, 0:64], fade[0:64, c:c + 1], None, ALU.mult)
                    V.tensor_scalar(state[64:P, 64:P], bank[6][64:P, 64:P], fade[64:P, c:c + 1], None, ALU.mult)\
                        .then_inc(sem("sq.st"), 1)
                dve.wait_ge(sem("gn.m"), p + 1)
                V.scalar_tensor_tensor(rT[:, :], bank[4][:, :], -1.0 / 64, aT[:, :], ALU.mult, ALU.add)\
                    .then_inc(sem("gn.c"), 1)
                dve.wait_ge(sem("gn.s"), p + 1)
                V.reciprocal(kkT[:, :], kkT[:, :])
                dve.drain()
                V.scalar_tensor_tensor(aT[:, :], rT[:, :], lw_c, kkT[:, :], ALU.mult, ALU.mult)
                dve.drain()
                V.scalar_tensor_tensor(aT[:, :], aT[:, :], lb_c, bonus[:, :], ALU.add, ALU.add)
                dve.drain()
                dve.wait_ge(sem("rk.g"), p + 2)
                V.tensor_tensor(dtile(yr, p), aT[:, :], bank[6][:, :], ALU.mult).then_inc(sem("rk.y"), 1)
                dve.drain()

            for k in range(12):
                src, hi, lo = (tile(at, k), tile(atH, k), tile(atL, k)) if k < 4 else \
                    (tile(yr, k - 4), tile(rH, k - 4), tile(rL, k - 4))
                dve.wait_ge(sem("mx.hi"), k + 1)
                V.tensor_tensor(lo, src, f32(hi), ALU.subtract).then_inc(sem("mx.lo"), 1)
            dve.drain()
            with dve.Fori(0, 4) as i:
                s0 = STRIP0["mix"] + i * 4
                for half in range(2):
                    dve.wait_ge(evac[half], fill("mix", half) + i * 2 + 1)
                    product_ready(s0 + 2, half)
                    V.tensor_tensor(tile(sq, half), bank[half][:, :], tile(sq, half), ALU.mult).then_inc(evac[half], 1)
                for half in range(2):
                    b = 2 + half
                    dve.wait_ge(evac[b], fill("mix", b) + i * 2 + 1)
                    product_ready(s0 + 3, half)
                    V.tensor_tensor(tile(hf, half), bank[b][:, :], tile(hf, half), ALU.mult).then_inc(evac[b], 1)
                    dve.drain()
                    V.tensor_tensor(tile(sq, half), tile(sq, half), tile(hf, half), ALU.add)
                    dve.drain()
                    split(dtile(mixH, i * 2 + half), dtile(mixL, i * 2 + half), tile(sq, half))\
                        .then_inc(sem("mx.lo2"), 1)

            with dve.Fori(0, 2) as i:
                for j in range(2):
                    for half in range(2):
                        product_ready(STRIP0["wo"] + i * 2 + j, half)
                        b, t = j * 2 + half, i * 4 + (j * 2 + half)
                        V.scalar_tensor_tensor(dtile(xT, t), bank[b][:, :], ada[:, ds(t + 2 * DT, 1)], dtile(xT, t),
                                               ALU.mult, ALU.add).then_inc(evac[b], 1)

            dve.drain()
            dve_norm(dve, "n_2", xt, [gain2[:, d:d + 1] for d in range(DT)], h_out,
                     [ada[:, 3 * DT + d:3 * DT + d + 1] for d in range(DT)])
            for b in range(2):
                last = V.memset(cpad[b][:, 0:2], 0.0)
            last.then_inc(sem("up.zero"), 1)
            dve.drain()
            cw, cb = VEC0["conv_w_2"], VEC0["conv_b_2"]
            with dve.Fori(0, 11) as i:
                for t in range(4):
                    n = i * 2 + (FT if t >= 2 else 0) + t % 2
                    u, acc = cpad[t % 2], tile(sq if t < 2 else hf, t % 2)
                    wt = [vec[:, ds(n + (cw + 2 * FT * j), 1)] for j in range(3)]
                    dve.wait_ge(evac[t], fill("up", t) + i + 1)
                    V.tensor_scalar(acc, u[:, 0:S], wt[0], vec[:, ds(n + cb, 1)], ALU.mult, ALU.add)
                    dve.drain()
                    V.scalar_tensor_tensor(acc, u[:, 1:S + 1], wt[1], acc, ALU.mult, ALU.add)
                    dve.drain()
                    V.scalar_tensor_tensor(acc, u[:, 2:S + 2], wt[2], acc, ALU.mult, ALU.add)\
                        .then_inc(sem("up.conv"), 1)
                    if t >= 2:
                        j = t - 2
                        dve.drain()
                        dve.wait_ge(sem("up.silu"), i * 2 + j + 1)
                        V.tensor_tensor(acc, acc, tile(sq, j), ALU.mult)
                        dve.drain()
                        split(dtile(fH, i * 2 + j), dtile(fL, i * 2 + j), acc).then_inc(sem("up.lo"), 1)
                dve.drain()
            with dve.Fori(0, 2) as i:
                for nn in range(2):
                    for half in range(2):
                        product_ready(STRIP0["down"] + i * 6 + nn * 3 + 2, half)
                        b, t = nn * 2 + half, i * 4 + (nn * 2 + half)
                        V.scalar_tensor_tensor(dtile(xT, t), bank[b][:, :], ada[:, ds(t + 5 * DT, 1)], dtile(xT, t),
                                               ALU.mult, ALU.add).then_inc(evac[b], 1)
            dve.drain()
            dve_norm(dve, "n_out", xt, cols("norm_f_w_2", DT), None)


_INS = ["x", "positions", "pool_norm", "pool_w_in", "pool_w_group", "pool_scale", "pool_w_out", "mla_norm", "mla_w_in",
        "mla_q_norm", "mla_w_q_b", "mla_kv_norm", "mla_w_kv_b", "mla_w_out", "final_norm", "c_2", "w_ada_2", "b_ada_2",
        "norm1_w_2", "w_in_2", "b_gate_2", "mu_shift_2", "w0_2", "w2_2", "a0_2", "a2_2", "g2_2", "k_k_2", "k_a_2",
        "r_k_2", "lnx_w_2", "lnx_b_2", "w_att_out_2", "w_rwkv_out_2", "w_o_2", "norm2_w_2", "w_up_2", "conv_w_2",
        "conv_b_2", "w_down_2", "norm_f_w_2"]


def kernel(**inputs):
    import numpy as _np
    import concourse.bacc as _bacc
    from concourse import mybir as _mybir
    from concourse.bass_utils import run_bass_kernel_spmd as _run

    nc = _bacc.Bacc("TRN2", target_bir_lowering=False, num_devices=1)
    arrays = {name: _np.ascontiguousarray(inputs[name]) for name in _INS}
    freq = 1.0 / (_np.float32(ROPE_THETA) ** (_np.arange(0, ROPE, 2, dtype=_np.float32) / _np.float32(ROPE)))
    arrays["inv_freq"] = _np.tile(freq.astype(_np.float32), 4).reshape(P, 1)
    aps = {name: nc.dram_tensor(f"in_{name}", v.shape, _mybir.dt.from_np(v.dtype), kind="ExternalInput").ap()
           for name, v in arrays.items()}
    out = nc.dram_tensor("out", (1, S, D), F32, kind="ExternalOutput").ap()
    build(nc, aps, out)
    r = _run(nc, [{f"in_{name}": v for name, v in arrays.items()}], core_ids=[0])
    return r.results[0]["out"]
```

```python
from contextlib import ExitStack, nullcontext

import numpy as np

import concourse.bass as bass
from concourse import mybir

P = 128
S = 512
D = 1024
DT = D // P
EPS = 1e-6
POOL_WINDOWS = (2, 4, 8, 16)
PAD = 16
HEADS = 16
NOPE, ROPE, VD = 128, 64, 128
QK = NOPE + ROPE
Q_RANK, KV_RANK = 384, 256
ROPE_THETA = 10000.0
QK_SCALE = QK ** -0.5
ATT_GROUPS = 3
ATT_HEADS, ATT_DIM = 8, 64
ATT_WIDTH = ATT_HEADS * ATT_DIM
ATT_IN = ATT_GROUPS * 3 * ATT_WIDTH
CH = 64
PAIRS = D // P
RWKV_IN = 3 * D + 64 + 64 + 160
GATE0 = ATT_IN + RWKV_IN
GN_EPS = 64e-5
D_FF = 2816
FT = D_FF // P
DOWN_K = (8, 8, 6)
SCAN_SCALE = 2.0 ** -20
BIG = 1e30
ROUND = 1.5 * 2.0 ** 23
TWO_PI = (6.28125, 0.00193500518798828125, 3.0199159795074593e-07)
PI_IN = 3.14159250259399414

F32 = mybir.dt.float32
F32R = mybir.dt.float32r
BF16 = mybir.dt.bfloat16
I32 = mybir.dt.int32
ALU = mybir.AluOpType
ACT = mybir.ActivationFunctionType
AX = mybir.AxisListType
ds = bass.ds

VEC_ROWS = [("pool_norm", 8), ("pool_scale", 16), ("mla_norm", 8), ("mla_q_norm", 3), ("mla_kv_norm", 2),
            ("final_norm", 8), ("c_2", 8), ("b_ada_2", 48), ("norm1_w_2", 8), ("b_gate_2", 16),
            ("mu_shift_2", 27), ("w0_2", 8), ("a0_2", 8), ("k_k_2", 8), ("k_a_2", 8), ("r_k_2", 8),
            ("lnx_w_2", 8), ("lnx_b_2", 8), ("norm2_w_2", 8), ("conv_w_2", 132), ("conv_b_2", 44),
            ("norm_f_w_2", 8)]
VEC0 = {}
for _name, _rows in VEC_ROWS:
    VEC0[_name] = sum(r for n, r in VEC_ROWS[:len(VEC0)])
VEC_ALL = sum(r for _, r in VEC_ROWS)
VEC_TILES = -(-VEC_ALL // P)

STREAM = [("pool", 4, 6), ("pool_out", 2, 4), ("lat", 1, 4), ("mz", 4, 2), ("heads", 8, 2), ("mla_out", 2, 4),
          ("att", 9, 2), ("lora", 1, 2), ("rkv", PAIRS, 2), ("mix", 4, 4), ("wo", 2, 2), ("up", 11, 2),
          ("down", 2, 6)]
STRIP0 = {}
for _name, _n, _m in STREAM:
    STRIP0[_name] = sum(n * m for _, n, m in STREAM[:len(STRIP0)])
FILLS = {"pool": (12,) * 4, "pool_out": (2,) * 4, "lat": (2, 1, 2, 1), "mz": (4,) * 4, "heads": (16,) * 4,
         "mla_out": (2,) * 4, "att": (9,) * 4, "lora": (1, 0, 1, 1), "rkv": (8, 8, 8, 0), "mix": (8,) * 4,
         "wo": (2,) * 4, "up": (11,) * 4, "down": (2,) * 4}
FILL0 = {}
for _name, _n, _m in STREAM:
    FILL0[_name] = tuple(sum(FILLS[p][b] for p, _, _ in STREAM[:len(FILL0)]) for b in range(4))
ADA_W = 128
ADA_N = 6 * D // 8 // ADA_W
RAW_CREDIT = 2
SPLIT_CREDIT = 4


NORMS = [("n_pool", DT, True), ("n_mla", DT, True), ("n_q", 3, True), ("n_kv", 2, True), ("n_fin", DT, False),
         ("n_1", DT, True), ("n_2", DT, True), ("n_out", DT, False)]
NORM0 = {}
for _k, (_name, _, _) in enumerate(NORMS):
    _all, _split = sum(n for _, n, _ in NORMS[:_k]), sum(n for _, n, o in NORMS[:_k] if o)
    NORM0[_name] = {"sq": _all, "sum": _all, "hf": _all, "rms": _k, "hi": _split, "lo": _split}


def loaded_value(ph, i, j, m):
    before = STRIP0[ph] // 2 + j // 2 + 1
    if ph == "rkv" and j == 0:
        return (i * 2 + (before + 1)) * 16
    if j % 2 == 0 and STRIP0[ph] > STRIP0["rkv"]:
        before += PAIRS
    return (i * (m // 2) + before) * 16


def split_value(s):
    return RAW_CREDIT + s + 1


def done_value(s, half):
    return SPLIT_CREDIT + 2 * s + half + 1


def att_units(g):
    units = []
    for h in range(ATT_HEADS):
        if g == 0:
            units += [(h, [(0, 0), (1, 0), (1, 1)]), (h, [(2, 1), (2, 2), (3, 2), (3, 3)])]
        else:
            units.append((h, [(b, b) for b in range(4)]))
    return units


def att_rows(blocks):
    rows = []
    for n, (qb, kb) in enumerate(blocks):
        if rows and rows[-1][0] == qb:
            rows[-1] = (qb, rows[-1][1], rows[-1][2] + 1, rows[-1][3])
        else:
            rows.append((qb, kb, 1, n * P))
    return rows


def gram_list():
    return [(h, l, r) for l, r in (("b", "a"), ("a", "b")) for h in range(2)] + \
           [(h, l, r) for h in range(2) for l, r in (("k", "a"), ("b", "r"), ("k", "r"))]


INVERSE = [
    {"mm": [("DA", "D", "act", "N2"), ("D", "DA", "dve", "A2")]},
    {"mm": [("A2", "N2", "act", "N4"), ("N2", "A2", "act", "A4")]},
    {"mm": [("N4", "A4", "act", "A8"), ("A2", "U", "dve", "+U")]},
    {"mm": [("A4", "U", "dve", "+U")], "E": 16},
    {"mm": [("A8", "U", "dve", "+U")]},
    {"mm": [("U", "I", "act", "W"), ("E", "U", "act", "Z")]},
    {"mm": [("W", "Z", "dve", "+U"), ("Z", "W", "dve", "+W")], "E": 32},
    {"mm": [("E", "U", "act", "Z")]},
    {"mm": [("W", "Z", "dve", "+U"), ("Z", "W", "dve", "+W")], "E": 64},
    {"mm": [("E", "U", "act", "Z")]},
    {"mm": [("W", "Z", "dve", "+U")]},
]
INV_ACT = [sum(x[2] == "act" for st in INVERSE[:k] for x in st["mm"]) for k in range(len(INVERSE) + 1)]
INV_DVE = [1 + sum(x[2] == "dve" for st in INVERSE[:k] for x in st["mm"]) + sum("E" in st for st in INVERSE[:k])
           for k in range(len(INVERSE) + 1)]


def build(nc, a, out):
    with ExitStack() as ctx:
        def sb(name, shape, dt=F32, stack=None):
            return (stack or ctx).enter_context(nc.sbuf_tensor(name, shape, dt))

        sems = {}

        def sem(name):
            if name not in sems:
                sems[name] = ctx.enter_context(nc.semaphore(name))
            return sems[name]

        bank = [ctx.enter_context(nc.psum_tensor(f"bank{b}", [P, S], F32)) for b in range(8)]
        scratch = nc.dram_tensor("stat_scratch", [4, S * ATT_HEADS], F32, kind="Internal").ap()

        raw = [sb(f"raw{b}", [P, 2048]) for b in range(2)]
        whi = [sb(f"whi{b}", [P, 2048], F32R) for b in range(2)]
        wlo = [sb(f"wlo{b}", [P, 2048], F32R) for b in range(2)]
        xT = sb("xT", [P, DT * S])
        hbuf = sb("hbuf", [P, 2 * DT * S], F32R)
        sq = sb("sq", [P, 2 * S])
        hf = sb("hf", [P, 2 * S])
        inv = sb("inv", [P, S])
        vec = sb("vec", [P, VEC_ALL])
        ident = sb("ident", [P, P])
        ones = sb("ones", [P, P])
        same = {n: sb(f"same{n}", [P, P]) for n in (16, 32, 64)}
        upper1 = sb("upper1", [P, P])
        upper0 = sb("upper0", [P, P])
        lower1 = sb("lower1", [P, P])
        up16 = sb("up16", [P, P])
        low16 = sb("low16", [P, P])
        step_mask = {n: sb(f"step{n}", [P, P]) for n in (16, 32, 64)}
        ident_b = sb("ident_b", [P, P], BF16)
        neg_band = sb("neg_band", [P, 2 * P], BF16)
        neg_dil = sb("neg_dil", [P, P], BF16)
        ada = sb("ada", [P, 48])
        gain1 = sb("gain1", [P, DT])
        gain2 = sb("gain2", [P, DT])
        spare = sb("spare", [P, 1])
        eps_c = sb("eps_c", [P, 1])
        gneps_c = sb("gneps_c", [P, 1])
        one_minus_ka = sb("one_minus_ka", [P, DT])
        neg_causal = neg_band[:, P:2 * P]

        def tile(buf, i):
            return buf[:, i * S:(i + 1) * S]

        def dtile(buf, i):
            return buf[:, ds(i * S, S)]

        def col(name, i):
            return vec[:, VEC0[name] + i:VEC0[name] + i + 1]

        def dcol(name, i):
            return vec[:, ds(VEC0[name] + i, 1)]

        with ExitStack() as st:
            vecrow = sb("vecrow", [P, VEC_TILES * P], F32, st)
            xin = sb("xin", [P, 4 * D], F32, st)
            res4 = sb("res4", [P, 4], F32, st)
            tmp_mask = sb("tmp_mask", [P, P], F32, st)
        with ExitStack() as st:
            y1H = sb("y1H", [P, 16 * S], F32R, st)
            y1L = sb("y1L", [P, 16 * S], F32R, st)
            poolH = sb("poolH", [P, 4 * S], F32R, st)
            poolL = sb("poolL", [P, 4 * S], F32R, st)
            zp = sb("zp", [P, 4 * S], F32, st)
            upad = [sb(f"upad{b}", [P, PAD + S], F32, st) for b in range(2)]
            cinv = sb("cinv", [P, 4 * PAD], F32, st)
        with ExitStack() as st:
            zm = sb("zm", [P, 16 * S], F32, st)
            latH = sb("latH", [P, 5 * S], F32R, st)
            latL = sb("latL", [P, 5 * S], F32R, st)
            krope = sb("krope", [P, S], F32, st)
            cosT = sb("cosT", [P, S], F32, st)
            sinT = sb("sinT", [P, S], F32, st)
            with ExitStack() as st2:
                lat = sb("lat", [P, 5 * S], F32, st2)
                posi = sb("posi", [P, S], I32, st2)
                ang = sb("ang", [P, 3 * S], F32, st2)
                invf = sb("invf", [P, 1], F32, st2)
            with ExitStack() as st2:
                kT = sb("kT", [P, 2 * S], F32, st2)
                vN = hf
                qrope = inv
                qT = sb("qT", [P, 2 * S], F32, st2)
                prob = [sb(f"prob{b}", [P, S], F32, st2) for b in range(3)]
                probT = sb("probT", [P, 4 * S], F32, st2)
                adaw = [sb(f"adaw{b}", [P, DT * ADA_W], F32, st2) for b in range(2)]
                adaacc = sb("adaacc", [P, 6 * P], F32, st2)
                stat = sb("stat", [P, 9], F32, st2)
        with ExitStack() as st:
            y2L = sb("y2L", [P, 16 * S], F32R, st)
        y2H = hbuf
        with ExitStack() as st:
            at = sb("at", [P, 4 * S], F32, st)
            with ExitStack() as st2:
                aq = sb("aq", [P, 4 * S], F32, st2)
                ak = sb("ak", [P, 4 * S], F32, st2)
                av = sb("av", [P, 4 * ATT_HEADS * P], F32, st2)
                num = [sb(f"num{g}", [P, 4 * S], F32, st2) for g in range(3)]
                ap_ = [sb(f"ap{b}", [P, S], F32, st2) for b in range(2)]
                apT = [sb(f"apT{b}", [P, S], F32, st2) for b in range(2)]
                spread = [ap_[0], ap_[1], apT[0]]
                nmax = sb("nmax", [P, 3 * 32], F32, st2)
                den = sb("den", [P, 3 * 32], F32, st2)
                stq = sb("stq", [P, 2 * 32], F32, st2)
                fac = sb("fac", [P, 3 * 32], F32, st2)
                fac0 = sb("fac0", [P, 32], F32, st2)
                zden = sb("zden", [P, 32], F32, st2)
            with ExitStack() as st2:
                yr = sb("yr", [P, PAIRS * S], F32, st2)
                with ExitStack() as st3:
                    wlow = sb("wlow", [P, S], F32, st3)
                    glow = sb("glow", [P, 2 * S], F32, st3)
                    lw2 = sb("lw2", [P, P], F32, st3)
                    lg2 = sb("lg2", [P, 2 * P], F32, st3)
                    mid = sb("mid", [P, 4], F32, st3)
                    pcol = [sb(f"pcol{b}", [P, 16], F32, st3) for b in range(2)]
                    aT = [sb(f"aT{b}", [P, S], F32, st3) for b in range(2)]
                    rT = [sb(f"rT{b}", [P, S], F32, st3) for b in range(2)]
                    bonus = [sb(f"bonus{b}", [P, S], F32, st3) for b in range(2)]
                    vpad = [sb(f"vpad{b}", [P, 4 * 256], F32, st3) for b in range(2)]
                    bN = [sb(f"bN{b}", [P, S], F32, st3) for b in range(2)]
                    kN = [sb(f"kN{b}", [P, S], F32, st3) for b in range(2)]
                    fade = [sb(f"fade{b}", [P, 4], F32, st3) for b in range(2)]
                    bT = sb("bT", [P, S], F32, st3)
                    kkT = sb("kkT", [P, S], F32, st3)
                    vT = sb("vT", [P, S], F32, st3)
                    Gak = [sb(f"Gak{h}", [P, S], F32, st3) for h in range(2)]
                    Gqb = [sb(f"Gqb{h}", [P, S], F32, st3) for h in range(2)]
                    Gqk = [sb(f"Gqk{h}", [P, S], F32, st3) for h in range(2)]
                    sapad = sb("sapad", [P, 256], F32, st3)
                    rhs = sb("rhs", [P, P], F32, st3)
                    state = sb("state", [P, P], F32, st3)
                    with ExitStack() as st4:
                        zsh = [sb(f"zsh{b}", [P, 1 + S], F32, st4) for b in range(3)]
                        Rr = sb("Rr", [P, S], F32, st4)
                        Kr = sb("Kr", [P, S], F32, st4)
                        lwd = sb("lwd", [P, S], F32, st4)
                        aa = inv
                        epos, kk, cc = [z[:, 0:S] for z in zsh]
                    with ExitStack() as st4:
                        IA, IN4, IA4 = [[sb(f"{n}_{h}", [P, S], F32, st4) for h in range(2)]
                                        for n in ("IA", "IN4", "IA4")]
                    IA8, IE = [bT, kkT], [vT, inv]
                    IW = [tile(sq, h) for h in range(2)]
                    IU = [tile(hf, h) for h in range(2)]
        with ExitStack() as st:
            sb("under_at_and_yr", [P, (4 + PAIRS) * S], F32, st)
            atH = sb("atH", [P, 4 * S], F32R, st)
            atL = sb("atL", [P, 4 * S], F32R, st)
            rH = sb("rH", [P, PAIRS * S], F32R, st)
            rL = sb("rL", [P, PAIRS * S], F32R, st)
            mixL = sb("mixL", [P, DT * S], F32R, st)
        with ExitStack() as st:
            mixH = sb("mixH", [P, DT * S], F32R, st)
        with ExitStack() as st:
            fH = sb("fH", [P, FT * S], F32R, st)
            fL = sb("fL", [P, FT * S], F32R, st)
            cpad = [sb(f"cpad{b}", [P, 2 + S], F32, st) for b in range(2)]
        with ExitStack() as st:
            yout = [sb(f"yout{b}", [P, D], F32, st) for b in range(2)]
        V, A, G, M = nc.vector, nc.scalar, nc.gpsimd, nc.tensor
        products_done, raw_split = sem("products_done"), sem("raw_split")
        raw_loaded = [sem(f"raw_loaded{b}") for b in range(2)]
        evac = [sem(f"bank_taken{b}") for b in range(4)]
        hH = [hbuf[:, d * S:(d + 1) * S] for d in range(DT)]
        hL = [hbuf[:, (DT + d) * S:(DT + d + 1) * S] for d in range(DT)]
        f32 = lambda r: r.bitcast(F32)
        fill = lambda ph, b: FILL0[ph][b]

        def out_tile_taken(ph, t):
            b = (t // 2 % 2) * 2 + t % 2
            return evac[b], fill(ph, b) + t // 4 + 1

        w_in1 = a["pool_w_in"].rearrange("l (k p) n -> p (l k) n", p=P)
        w_grp = a["pool_w_group"].rearrange("l g (k p) n -> p (l g k) n", p=P)
        w_out1 = a["pool_w_out"].rearrange("l (k p) n -> p (l k) n", p=P)
        w_mla = a["mla_w_in"].rearrange("l (k p) n -> p (l k) n", p=P)
        w_q = a["mla_w_q_b"].rearrange("l (k p) n -> p (l k) n", p=P)
        w_kv = a["mla_w_kv_b"].rearrange("l (k p) n -> p (l k) n", p=P)
        w_out2 = a["mla_w_out"].rearrange("l (k p) n -> p (l k) n", p=P)
        w_ada = a["w_ada_2"].rearrange("l (k p) n -> p (l k) n", p=P)
        w_in2 = a["w_in_2"].rearrange("l (k p) n -> p (l k) n", p=P)
        w_ao = a["w_att_out_2"].rearrange("l (k p) n -> p (l k) n", p=P)
        w_ro = a["w_rwkv_out_2"].rearrange("l (k p) n -> p (l k) n", p=P)
        w_wo = a["w_o_2"].rearrange("l (k p) n -> p (l k) n", p=P)
        w_up = a["w_up_2"].rearrange("l (k p) n -> p (l k) n", p=P)
        w_dn = a["w_down_2"].rearrange("l (k p) n -> p (l k) n", p=P)
        LAT = ((0, 256), (256, 256), (512, 128), (640, 64))
        MZ0 = Q_RANK + KV_RANK + ROPE
        LORA0 = ATT_IN + 3 * D
        LORA = ((LORA0, 128), (LORA0 + 128, 160))

        def strip_source(ph, i, j):
            if ph == "pool":
                if j < 4:
                    return w_in1[:, :, ds(i * 512 + (j // 2) * 2 * D + (j % 2) * 256, 256)], 8, 256
                return w_grp[:, ds(i * 4, 4), (j - 4) * 256:(j - 3) * 256], 4, 256
            if ph in ("pool_out", "mla_out"):
                w = w_out1 if ph == "pool_out" else w_out2
                return w[:, (j % 2) * 8:(j % 2) * 8 + 8, ds(i * 512 + (j // 2) * 256, 256)], 8, 256
            if ph == "lat":
                return w_mla[:, :, LAT[j][0]:LAT[j][0] + LAT[j][1]], 8, LAT[j][1]
            if ph == "mz":
                return w_mla[:, :, ds(MZ0 + i * 512 + j * 256, 256)], 8, 256
            if ph == "heads":
                if j == 0:
                    return w_q[:, :, ds(i * 2 * QK, 2 * QK)], 3, 2 * QK
                return w_kv[:, :, ds(i * 512, 512)], 2, 512
            if ph == "att":
                return w_in2[:, :, ds(i * 512 + j * 256, 256)], 8, 256
            if ph == "lora":
                return w_in2[:, :, LORA[j][0]:LORA[j][0] + LORA[j][1]], 8, LORA[j][1]
            if ph == "rkv":
                if j == 0:
                    return None, 8, 256
                return w_in2[:, :, ds(i * P + (ATT_IN + 2 * D), P)], 8, P
            if ph == "mix":
                if j < 2:
                    return w_in2[:, :, ds(i * 256 + (GATE0 + j * D), 256)], 8, 256
                return (w_ao if j == 2 else w_ro)[:, :, ds(i * 256, 256)], (4 if j == 2 else 8), 256
            if ph == "wo":
                return w_wo[:, :, ds(i * 512 + j * 256, 256)], 8, 256
            if ph == "up":
                return w_up[:, :, ds(i * 256 + j * D_FF, 256)], 8, 256
            k0 = sum(DOWN_K[:j % 3])
            return w_dn[:, k0:k0 + DOWN_K[j % 3], ds(i * 512 + (j // 3) * 256, 256)], DOWN_K[j % 3], 256

        vec_src = {"conv_w_2": "l j (r c) -> (l j r) c", "r_k_2": "l (r h) e -> (l r) (h e)",
                   "final_norm": "(r c) -> r c", "norm_f_w_2": "(r c) -> r c"}
        vec_dmas = []
        for name, rows in VEC_ROWS:
            full = a[name]
            if name == "mu_shift_2":
                vec_dmas.append((VEC0[name] + 26, 1, 32, full[0:1, 26 * P:RWKV_IN]))
                full, rows = full[:, 0:26 * P], 26
            view = full.rearrange(vec_src[name], h=2) if name == "r_k_2" else \
                full.rearrange(vec_src.get(name, "l (r c) -> (l r) c"), c=P)
            r = 0
            while r < rows:
                n = min(rows - r, P - (VEC0[name] + r) % P)
                vec_dmas.append((VEC0[name] + r, n, P, view[r:r + n, :]))
                r += n
        VEC_DMAS = len(vec_dmas)

        block = ctx.enter_context(nc.Block())

        def phase_loop(eng, n):
            return eng.Fori(0, n) if n > 1 else nullcontext(0)

        @block.sync
        def _(sp):
            sp.dma_start(xin[:, :].rearrange("p (t d) -> p t d", t=4),
                         a["x"].rearrange("b (t p) d -> p (b t) d", p=P)).then_inc(sem("x_loaded"), 16)
            for ph, n, m in STREAM:
                if ph == "heads":
                    sp.wait_ge(sem("norm.lo"), NORM0["n_kv"]["lo"] + 2)
                    sp.wait_ge(sem("krope"), 1)
                def load_strips(i):
                    for j in range(m):
                        s = STRIP0[ph] + i * m + j
                        par = j % 2
                        src, K, W = strip_source(ph, i, j)
                        sp.wait_ge(raw_split, s + 1)
                        dst = raw[par][:, 0:K * W].rearrange("p (k n) -> p k n", k=K)
                        if ph == "rkv" and j == 0:
                            for t in range(2):
                                sp.dma_start(dst[:, :, t * P:(t + 1) * P],
                                             w_in2[:, :, ds(i * P + (ATT_IN + t * D), P)])\
                                    .then_inc(raw_loaded[par], 16)
                            continue
                        sp.dma_start(dst, src).then_inc(raw_loaded[par], 16)

                if ph == "mix":
                    for i in range(n):
                        load_strips(i)
                    continue
                with phase_loop(sp, n) as i:
                    load_strips(i)
                    if ph == "heads":
                        for q in range(ADA_N):
                            sp.wait_ge(sem("ada.acc"), i * ADA_N + q + 1)
                            sp.dma_start(adaw[q % 2][:, :].rearrange("p (k n) -> p k n", k=DT),
                                         w_ada[:, :, ds(i * 768 + q * ADA_W, ADA_W)])\
                                .then_inc(sem(f"ada.ld{q % 2}"), 16)
            for t in range(4):
                sp.wait_ge(sem("fin.out"), 2 * t + 2)
                sp.dma_start(out[0, t * P:(t + 1) * P, :], yout[t % 2][:, :]).then_inc(sem(f"out_stored{t % 2}"), 16)
            for b in range(2):
                sp.wait_ge(sem(f"out_stored{b}"), 32)

        @block.gpsimd
        def _(pool):
            G.memset(vecrow[:, :], 0.0).then_inc(sem("vecrow_zero"), 1)
            G.memset(ones[:, :], 1.0)
            G.memset(ident[:, :], 0.0)
            G.memset(upad[0][:, 0:PAD], 0.0)
            G.memset(upad[1][:, 0:PAD], 0.0)
            G.memset(eps_c[:, :], EPS)
            G.memset(gneps_c[:, :], GN_EPS)
            for n in (16, 32, 64):
                G.memset(same[n][:, :], 1.0)
            G.iota(cinv[:, :].rearrange("p (g t) -> p g t", g=4), [[0, 4], [1, PAD]], base=1, channel_multiplier=0,
                   allow_small_or_imprecise_dtypes=True)
            pool.drain()
            G.affine_select(out=ident[:, :], in_=ident[:, :], compare_op=ALU.not_equal, fill=1.0, base=0,
                            pattern=[[-1, P]], channel_multiplier=1)
            G.affine_select(out=upper0[:, :], in_=ones[:, :], compare_op=ALU.is_ge, fill=0.0, base=0,
                            pattern=[[1, P]], channel_multiplier=-1)
            G.affine_select(out=upper1[:, :], in_=ones[:, :], compare_op=ALU.is_gt, fill=0.0, base=0,
                            pattern=[[1, P]], channel_multiplier=-1)
            G.affine_select(out=lower1[:, :], in_=ones[:, :], compare_op=ALU.is_gt, fill=0.0, base=0,
                            pattern=[[-1, P]], channel_multiplier=1)
            for n in (16, 32, 64):
                v = same[n][:, :].rearrange("p (b c) -> p b c", c=n)
                G.affine_select(out=v, in_=v, compare_op=ALU.is_ge, fill=0.0, base=0,
                                pattern=[[-n, P // n], [0, n]], channel_multiplier=1)
                pool.drain()
                G.affine_select(out=v, in_=v, compare_op=ALU.is_ge, fill=0.0, base=n - 1,
                                pattern=[[n, P // n], [0, n]], channel_multiplier=-1)
            pool.drain()
            G.memset(res4[0:1, 0:1], 0.0).then_inc(raw_split, RAW_CREDIT)
            pool.drain()
            G.memset(res4[0:1, 0:1], 0.0).then_inc(products_done, SPLIT_CREDIT)
            for name, credit in (("ada.acc", 2), ("ada.col", 1), ("rk.g", 1), ("rk.y", 1), ("mx.lo2", 1),
                                 ("up.conv", 2)):
                pool.drain()
                G.memset(res4[0:1, 0:1], 0.0).then_inc(sem(name), credit)
            pool.drain()
            G.memset(res4[0:1, 0:1], 0.0).then_inc(sem("consts"), 1)
            def take_wait():
                G.tensor_tensor(spare[0:1, 0:1], ones[0:1, 0:1], ones[0:1, 0:1], ALU.mult)

            pool.wait_ge(sem("vec.ready"), 1)
            for ph, n, m in STREAM:
                with phase_loop(pool, n) as i:
                    for j in range(m):
                        s = STRIP0[ph] + i * m + j
                        par = j % 2
                        _, K, W = strip_source(ph, i, j)
                        pool.wait_ge(raw_loaded[par], loaded_value(ph, i, j, m))
                        pool.wait_ge(products_done, done_value(s, 1) - 4)
                        if n > 1:
                            take_wait()
                        r, h, l = raw[par][:, 0:K * W], whi[par][:, 0:K * W], wlo[par][:, 0:K * W]
                        if ph == "heads" and j == 0:
                            n = K * 2 * NOPE
                            r = r.rearrange("p (x c) -> p x c", c=QK)
                            parts = [(r[:, :, lo:hi], *[w[:, o:o + 2 * K * (hi - lo)]
                                                        .rearrange("p (x c) -> p x c", c=hi - lo) for w in (h, l)])
                                     for lo, hi, o in ((0, NOPE, 0), (NOPE, QK, n))]
                            for r_, h_, _ in parts:
                                G.tensor_scalar(h_, r_, 1.0, 1.0, ALU.mult, ALU.mult)
                            pool.drain()
                            for r_, h_, l_ in parts:
                                last = G.tensor_tensor(l_, r_, f32(h_), ALU.subtract)
                            last.then_inc(raw_split, 1)
                            continue
                        G.tensor_scalar(h, r, 1.0, 1.0, ALU.mult, ALU.mult)
                        pool.drain()
                        G.tensor_tensor(l, r, f32(h), ALU.subtract).then_inc(raw_split, 1)
                    if ph == "heads":
                        for q in range(ADA_N):
                            if q == 0:
                                pool.wait_ge(sem("ada.col"), i + 1)
                            pool.wait_ge(sem(f"ada.ld{q % 2}"), (i * (ADA_N // 2) + (q // 2 + 1)) * 16)
                            take_wait()
                            buf = adaw[q % 2]
                            for k in range(DT):
                                w = buf[:, k * ADA_W:(k + 1) * ADA_W]
                                G.tensor_scalar(w, w, col("c_2", k), 1.0, ALU.mult, ALU.mult)
                            for half in (4 * ADA_W, 2 * ADA_W, ADA_W):
                                pool.drain()
                                to = buf[:, 0:half] if half > ADA_W else adaacc[:, q * ADA_W:(q + 1) * ADA_W]
                                add = G.tensor_tensor(to, buf[:, 0:half], buf[:, half:2 * half], ALU.add)
                            add.then_inc(sem("ada.acc"), 1)
                            pool.drain()

        def act_norm(act, name, srcs, width, src_ready, outs):
            n = len(srcs)
            for d in range(n):
                src_ready(act, d)
                if d >= 2:
                    act.wait_ge(sem("norm.sum"), NORM0[name]["sum"] + d - 1)
                A.activation(tile(sq, d % 2), srcs[d], ACT.Square).then_inc(sem("norm.sq"), 1)
            act.wait_ge(sem("norm.sum"), NORM0[name]["sum"] + n)
            A.activation(inv[:, :], bank[7][:, :], ACT.Sqrt, scale=1.0 / width, bias=eps_c[:, 0:1])\
                .then_inc(sem("norm.rms"), 1)
            if outs:
                for d in range(n):
                    act.wait_ge(sem("norm.hf"), NORM0[name]["hf"] + d + 1)
                    A.copy(outs[d][0], tile(hf, d % 2)).then_inc(sem("norm.hi"), 1)

        def pe_norm(pe, name, n):
            for d in range(n):
                pe.wait_ge(sem("norm.sq"), NORM0[name]["sq"] + d + 1)
                M.matmul(bank[7][:, :], ones[:, :], tile(sq, d % 2), start=(d == 0), stop=(d == n - 1))\
                    .then_inc(sem("norm.sum"), 1)

        def dve_norm(dve, name, srcs, gains, outs, shifts=None):
            n = len(srcs)
            dve.wait_ge(sem("norm.rms"), NORM0[name]["rms"] + 1)
            V.reciprocal(inv[:, :], inv[:, :])
            dve.drain()
            if not outs:
                for d in range(n):
                    V.scalar_tensor_tensor(srcs[d], srcs[d], gains[d], inv[:, :], ALU.mult, ALU.mult)\
                        .then_inc(sem("norm.hf"), 1)
                return

            def normed(d):
                if d >= 2:
                    dve.wait_ge(sem("norm.hi"), NORM0[name]["hi"] + d - 1)
                if shifts is None:
                    V.scalar_tensor_tensor(tile(hf, d % 2), srcs[d], gains[d], inv[:, :], ALU.mult, ALU.mult)\
                        .then_inc(sem("norm.hf"), 1)
                else:
                    V.scalar_tensor_tensor(tile(hf, d % 2), srcs[d], gains[d], inv[:, :], ALU.mult, ALU.mult)
                    dve.drain()
                    V.tensor_scalar(tile(hf, d % 2), tile(hf, d % 2), shifts[d], None, ALU.add)\
                        .then_inc(sem("norm.hf"), 1)

            normed(0)
            for d in range(n):
                if d + 1 < n:
                    normed(d + 1)
                dve.drain()
                dve.wait_ge(sem("norm.hi"), NORM0[name]["hi"] + d + 1)
                V.tensor_tensor(outs[d][1], tile(hf, d % 2), f32(outs[d][0]), ALU.subtract)\
                    .then_inc(sem("norm.lo"), 1)
                dve.drain()

        xt = [tile(xT, d) for d in range(DT)]
        h_out = [(hH[d], hL[d]) for d in range(DT)]
        lat_t = [tile(lat, d) for d in range(5)]
        lat_out = [(tile(latH, d), tile(latL, d)) for d in range(5)]
        cols = lambda name, n: [col(name, d) for d in range(n)]

        @block.tensor
        def _(pe):
            def product(dst, slot, W, c0, cw, acts, first=True, last=True, ready=None, half_at=None):
                n = len(acts)
                for k in range(n):
                    wh = whi[slot][:, k * W + c0:k * W + c0 + cw]
                    wl = wlo[slot][:, k * W + c0:k * W + c0 + cw]
                    if ready is not None:
                        pe.wait_ge(ready[0], ready[1] + k)
                    M.matmul(dst, wh, acts[k][0], start=(first and k == 0), stop=False)
                    M.matmul(dst, wh, acts[k][1], start=False, stop=False)
                    mm = M.matmul(dst, wl, acts[k][0], start=False, stop=(last and k == n - 1))
                    if half_at is not None and k + 1 == half_at:
                        mm.then_inc(products_done, 1)
                return mm

            def strip_ready(s):
                pe.wait_ge(raw_split, split_value(s))

            def bank_free(ph, b, n):
                if isinstance(n, int) and fill(ph, b) + n == 0:
                    return
                pe.wait_ge(evac[b], fill(ph, b) + n)

            def two_tiles(ph, s, par, n, acts, ready=None):
                strip_ready(s)
                for j in range(2):
                    b = par * 2 + j
                    bank_free(ph, b, n)
                    product(bank[b][:, :], par, 256, j * P, P, acts, ready=ready if j == 0 else None)\
                        .then_inc(products_done, 1)

            def out_product(ph, acts, ready):
                pe.wait_ge(ready, 16)
                with pe.Fori(0, 2) as i:
                    for nn in range(2):
                        for half in range(2):
                            strip_ready(STRIP0[ph] + i * 4 + nn * 2 + half)
                            for j in range(2):
                                b = nn * 2 + j
                                if half == 0:
                                    bank_free(ph, b, i)
                                product(bank[b][:, :], half, 256, j * P, P, acts[half * 8:half * 8 + 8],
                                        first=(half == 0), last=(half == 1)).then_inc(products_done, 1)

            pe.wait_ge(sem("consts"), 1)
            pe.wait_ge(sem("vec_loaded"), 16 * VEC_DMAS)
            for t in range(VEC_TILES):
                mm = M.transpose(bank[4][:, t * P:(t + 1) * P], vecrow[:, t * P:(t + 1) * P], ident[:, :])
            mm.then_inc(sem("vec.t"), 1)
            pe.wait_ge(sem("x_loaded"), 16)
            for d in range(DT):
                if d >= 2:
                    pe.wait_ge(sem("xt.taken"), d - 1)
                for t in range(4):
                    mm = M.transpose(bank[5 + d % 2][:, t * P:(t + 1) * P],
                                     xin[:, t * D + d * P:t * D + (d + 1) * P], ident[:, :])
                mm.then_inc(sem("xt.t"), 1)

            pe_norm(pe, "n_pool", DT)
            pool_acts = [(tile(poolH, k), tile(poolL, k)) for k in range(4)]
            for g in range(4):
                s0 = STRIP0["pool"] + g * 6
                for j in range(4):
                    two_tiles("pool", s0 + j, j % 2, 3 * g + j // 2, h_out,
                              ready=(sem("norm.lo"), NORM0["n_pool"]["lo"] + 1) if g == 0 and j == 0 else None)
                for j in range(2):
                    two_tiles("pool", s0 + 4 + j, j, 3 * g + 2, pool_acts,
                              ready=(sem("pool.lo"), 4 * g + 1) if j == 0 else None)
            out_product("pool_out", [(tile(y1H, k), tile(y1L, k)) for k in range(16)], sem("pool.ylo"))

            pe_norm(pe, "n_mla", DT)
            for j in range(4):
                s, par, w = STRIP0["lat"] + j, j % 2, LAT[j][1]
                ready = (sem("norm.lo"), NORM0["n_mla"]["lo"] + 1) if j == 0 else None
                if w == 256:
                    two_tiles("lat", s, par, 0, h_out, ready=ready)
                    continue
                strip_ready(s)
                bank_free("lat", par * 2, 1)
                product(bank[par * 2][0:w, :], par, w, 0, w, h_out, half_at=1).then_inc(products_done, 1)
            two_tiles("mz", STRIP0["mz"], 0, 0, h_out)
            pe_norm(pe, "n_q", 3)
            pe_norm(pe, "n_kv", 2)
            two_tiles("mz", STRIP0["mz"] + 1, 1, 0, h_out)
            with pe.Fori(1, 4) as i:
                for j in range(2):
                    two_tiles("mz", STRIP0["mz"] + i * 2 + j, j, i, h_out)
            pe.wait_ge(sem("norm.lo"), NORM0["n_q"]["lo"] + 3)
            pe.wait_ge(sem("norm.lo"), NORM0["n_kv"]["lo"] + 2)
            pe.wait_ge(sem("krope"), 1)
            kv_acts, q_acts = lat_out[3:5], lat_out[0:3]
            score_bank, turn_bank, out_bank = (bank[4], bank[5], bank[0]), (bank[6], bank[1]), (bank[2], bank[7])
            with pe.Fori(0, 8) as i:
                sq_ = STRIP0["heads"] + i * 2
                strip_ready(sq_)
                for h in range(2):
                    bank_free("heads", h, i * 2)
                    mm = product(bank[h][:, :], 0, 2 * NOPE, h * NOPE, P, q_acts)
                mm.then_inc(products_done, 1)
                bank_free("heads", 2, i * 2)
                for k in range(3):
                    r0 = 3 * 2 * NOPE + k * 2 * ROPE
                    wr = [w[0][:, r0:r0 + 2 * ROPE] for w in (whi, wlo)]
                    M.matmul(bank[2][:, :], wr[0], q_acts[k][0], start=(k == 0), stop=False)
                    M.matmul(bank[2][:, :], wr[0], q_acts[k][1], start=False, stop=False)
                    mm = M.matmul(bank[2][:, :], wr[1], q_acts[k][0], start=False, stop=(k == 2))
                mm.then_inc(products_done, 1)
                strip_ready(sq_ + 1)
                for h, b, n in ((0, 3, i * 2), (1, 0, i * 2 + 1)):
                    bank_free("heads", b, n)
                    mm = product(bank[b][:, :], 1, 512, h * 256, P, kv_acts)
                mm.then_inc(products_done, 1)
                for b in (1, 2):
                    bank_free("heads", b, i * 2 + 1)
                    for t in range(2):
                        blk = (b - 1) * 2 + t
                        dst = bank[b][:, t * 256:(t + 1) * 256]
                        for k in range(2):
                            wv = [w[1][:, k * 512:(k + 1) * 512].rearrange("p (h c) -> p h c", h=2)[:, :, P:2 * P]
                                  for w in (whi, wlo)]
                            ah, al = [x[:, blk * P:(blk + 1) * P] for x in kv_acts[k]]
                            M.matmul(dst, ah, wv[0], start=(k == 0), stop=False)
                            M.matmul(dst, ah, wv[1], start=False, stop=False)
                            mm = M.matmul(dst, al, wv[0], start=False, stop=(k == 1))
                mm.then_inc(products_done, 1)
                pe.wait_ge(evac[3], fill("heads", 3) + i * 2 + 1)
                pe.wait_ge(evac[0], fill("heads", 0) + i * 2 + 2)
                pe.wait_ge(sem("qrope"), i + 1)

                def scores(u):
                    h, qb = u // 4, u % 4
                    w = (qb + 1) * P
                    if u >= 3:
                        pe.wait_ge(sem("m.exp"), i * 8 + u - 2)
                    dst = score_bank[u % 3]
                    M.matmul(dst[:, 0:w], qT[:, h * S + qb * P:h * S + (qb + 1) * P], kT[:, h * S:h * S + w],
                             start=True, stop=False)
                    M.matmul(dst[:, 0:w], qrope[h * 64:h * 64 + 64, qb * P:(qb + 1) * P],
                             krope[h * 64:h * 64 + 64, 0:w], start=False, stop=True)
                    M.matmul(dst[:, qb * P:w], ident_b[:, :], neg_causal, start=False, stop=True, skip_group_check=True)\
                        .then_inc(sem("m.s"), 1)

                def turned(u):
                    h, qb = u // 4, u % 4
                    pe.wait_ge(sem("m.p"), i * 8 + u + 1)
                    if u == 1:
                        pe.wait_ge(evac[1], fill("heads", 1) + i * 2 + 2)
                    if u >= 2:
                        pe.wait_ge(sem("m.te"), i * 8 + u - 1)
                    for kb in range(qb + 1):
                        mm = M.transpose(turn_bank[u % 2][:, kb * P:(kb + 1) * P], prob[u % 3][:, kb * P:(kb + 1) * P],
                                         ident[:, :])
                    mm.then_inc(sem("m.t"), 1)

                def values(h):
                    pe.wait_ge(sem("m.te"), i * 8 + 4 * h + 4)
                    if h == 0:
                        pe.wait_ge(evac[2], fill("heads", 2) + i * 2 + 2)
                    else:
                        pe.wait_ge(sem("m.y"), i * 2 + 1)
                    for kb in range(4):
                        mm = M.matmul(out_bank[h][:, kb * P:S], vN[:, kb * 256 + h * VD:kb * 256 + (h + 1) * VD],
                                      probT[:, kb * S + kb * P:(kb + 1) * S], start=(kb == 0), stop=(kb == 3))
                    mm.then_inc(sem("m.o"), 1)

                scores(0)
                scores(1)
                for u in range(8):
                    if u + 2 < 8:
                        scores(u + 2)
                    if u == 4:
                        values(0)
                    turned(u)
                pe.wait_ge(sem("ada.acc"), i * ADA_N + (ADA_N + 2))
                bank_free("heads", 3, i * 2 + 1)
                for t in range(6):
                    mm = M.matmul(bank[3][:, t:t + 1], adaacc[:, t * P:(t + 1) * P], ones[:, 0:1],
                                  start=True, stop=True)
                mm.then_inc(sem("ada.col"), 1)
                values(1)
            out_product("mla_out", [(y2H[:, k * S:(k + 1) * S], tile(y2L, k)) for k in range(16)], sem("m.lo"))

            pe_norm(pe, "n_fin", DT)
            pe_norm(pe, "n_1", DT)
            units_before = 0
            for g in range(3):
                sg = STRIP0["att"] + g * 6
                for kind in range(2):
                    for j in range(2):
                        two_tiles("att", sg + kind * 2 + j, j, 3 * g + kind, h_out,
                                  ready=(sem("norm.lo"), NORM0["n_1"]["lo"] + 1) if g == 0 and kind == 0 and j == 0 else None)
                for j in range(2):
                    strip_ready(sg + 4 + j)
                    for hv in range(2):
                        b = j * 2 + hv
                        bank_free("att", b, 3 * g + 2)
                        for t in range(2):
                            blk = hv * 2 + t
                            dst = bank[b][:, t * 256:(t + 1) * 256]
                            for k in range(DT):
                                if g == 0:
                                    ah, al = [x[:, blk * P:(blk + 1) * P] for x in h_out[k]]
                                else:
                                    ah, al = [x[:, blk:S:4] for x in h_out[k]]
                                wh, wl = whi[j][:, k * 256:(k + 1) * 256], wlo[j][:, k * 256:(k + 1) * 256]
                                M.matmul(dst, ah, wh, start=(k == 0), stop=False)
                                M.matmul(dst, ah, wl, start=False, stop=False)
                                mm = M.matmul(dst, al, wh, start=False, stop=(k == DT - 1))
                        mm.then_inc(products_done, 1)
                for b in range(4):
                    pe.wait_ge(evac[b], fill("att", b) + 3 * g + 3)
                pe.wait_ge(sem("att.vz"), 1)
                units = att_units(g)

                def scores(u):
                    h, blocks = units[u]
                    U = units_before + u
                    if U >= 2:
                        pe.wait_ge(sem("att.exp"), U - 1)
                    dst, rows = bank[4 + U % 2], slice((h % 2) * 64, (h % 2) * 64 + 64)
                    for qb, kb0, nk, c0 in att_rows(blocks):
                        w = nk * P
                        mask = neg_dil[:, :] if g == 2 else neg_band[:, (2 - nk) * P:2 * P]
                        base = (h // 2) * S
                        M.matmul(dst[:, c0:c0 + w], aq[rows, base + qb * P:base + (qb + 1) * P],
                                 ak[rows, base + kb0 * P:base + kb0 * P + w], start=True, stop=False)
                        mm = M.matmul(dst[:, c0:c0 + w], ident_b[:, :], mask, start=False, stop=True)
                    mm.then_inc(sem("att.s"), 1)

                def turned(u):
                    U = units_before + u
                    pe.wait_ge(sem("att.exp"), U + 1)
                    if U >= 1:
                        pe.wait_ge(sem("att.te"), U)
                    for n in range(len(units[u][1])):
                        mm = M.transpose(bank[6][:, n * P:(n + 1) * P], ap_[U % 2][:, n * P:(n + 1) * P],
                                         ident[:, :])
                    mm.then_inc(sem("att.t"), 1)

                def values(u):
                    h, blocks = units[u]
                    U = units_before + u
                    first = h % 2 == 0 and (u == 0 or units[u - 1][0] != h)
                    pe.wait_ge(sem("att.te"), U + 1)
                    if first and 4 * g + h // 2 > 0:
                        pe.wait_ge(sem("att.num"), 4 * g + h // 2)
                    for n, (qb, kb) in enumerate(blocks):
                        v0 = (kb * ATT_HEADS + h) * P
                        mm = M.matmul(bank[7][:, qb * P:(qb + 1) * P], av[:, v0:v0 + P],
                                      apT[U % 2][:, n * P:(n + 1) * P], start=(first and n == 0), stop=True,
                                      skip_group_check=True)
                    mm.then_inc(sem("att.pv"), 1)

                for u in range(len(units) + 2):
                    if u < len(units):
                        scores(u)
                    if 1 <= u <= len(units):
                        turned(u - 1)
                    if u >= 2:
                        values(u - 2)
                units_before += len(units)
            for pr in range(4):
                pe.wait_ge(sem("cmb.f"), (pr + 1) * 3)
                if pr >= 1:
                    pe.wait_ge(sem("cmb.used"), pr)
                for g in range(3):
                    for blk in range(4):
                        cs = slice(blk * P, (blk + 1) * P)
                        mm = M.transpose(bank[4 + g][:, cs], spread[g][:, cs], ident[:, :])
                mm.then_inc(sem("cmb.pe"), 1)

            strip_ready(STRIP0["lora"])
            bank_free("lora", 0, 0)
            product(bank[0][:, :], 0, P, 0, P, h_out, half_at=1).then_inc(products_done, 1)
            strip_ready(STRIP0["lora"] + 1)
            bank_free("lora", 2, 0)
            product(bank[2][:, :], 1, 160, 0, P, h_out).then_inc(products_done, 1)
            bank_free("lora", 3, 0)
            product(bank[3][0:32, :], 1, 160, P, 32, h_out).then_inc(products_done, 1)
            pe.wait_ge(sem("lora.act"), 2)
            pe.wait_ge(sem("rk.zero"), 1)

            def rkv_slice(p, n):
                z, k = divmod(n, DT)
                s0, slot, W, c0 = STRIP0["rkv"] + p * 2, z // 2, (256, 256, P)[z], z % 2 * P
                if k == 0:
                    if z != 1:
                        strip_ready(s0 + slot)
                    bank_free("rkv", z, p)
                wh, wl = [w[slot][:, k * W + c0:k * W + c0 + P] for w in (whi, wlo)]
                M.matmul(bank[z][:, :], wh, h_out[k][0], start=(k == 0), stop=False)
                M.matmul(bank[z][:, :], wh, h_out[k][1], start=False, stop=False)
                mm = M.matmul(bank[z][:, :], wl, h_out[k][0], start=False, stop=(k == DT - 1))
                if k == DT - 1 or (z == 2 and k == 0):
                    mm.then_inc(products_done, 1)

            def lora_products(p):
                pe.wait_ge(sem("lw.ld"), (p + 1) * 32)
                for b in range(2):
                    pe.wait_ge(evac[b], p + (fill("rkv", b) + 1))
                M.matmul(bank[0][:, :], lw2[0:64, :], wlow[0:64, :], start=True, stop=True)
                M.matmul(bank[1][:, :], lw2[64:128, :], wlow[64:128, :], start=True, stop=True)\
                    .then_inc(sem("rk.lora"), 1)

            def key_norms(p):
                pe.wait_ge(sem("rk.sq"), p + 1)
                M.matmul(bank[2][:, :], same[64][:, :], tile(sq, 0), start=True, stop=True)\
                    .then_inc(sem("rk.ss"), 1)

            def turn(b, x, signal):
                for c in range(4):
                    mm = M.transpose(bank[b][:, c * P:(c + 1) * P], x[:, c * P:(c + 1) * P], ident[:, :])
                mm.then_inc(sem(signal), 1)

            def turn_v(p):
                pe.wait_ge(sem("rk.sig"), p + 1)
                pe.wait_ge(sem("rk.v"), p + 1)
                turn(0, vT, "rk.tv")

            def turn_b(p):
                pe.wait_ge(sem("rk.ab"), p + 1)
                turn(1, bT, "rk.tb")

            def turn_k(p):
                pe.wait_ge(sem("rk.te"), p * 3 + 1)
                pe.wait_ge(sem("rk.kr"), p + 1)
                turn(0, kkT, "rk.tk")

            def bonus_sums(p):
                pe.wait_ge(sem("rk.nr"), p + 1)
                pe.wait_ge(sem("rk.bon"), p + 1)
                M.matmul(bank[2][:, :], same[64][:, :], Rr[:, :], start=True, stop=True)\
                    .then_inc(sem("rk.bs"), 1)

            def grams(p, par, follows):
                for q, (h, left, right) in enumerate(gram_list()):
                    if q == 1 and follows:
                        pe.wait_ge(sem("gn.s"), p)
                    if q >= 4:
                        pe.wait_ge(sem("rk.ge"), p * 10 + (q - 3))
                    L, R = [{"a": aT[par], "b": bT, "k": kkT, "r": rT[par]}[x] for x in (left, right)]
                    rows = slice(h * 64, h * 64 + 64)
                    for c in range(4):
                        mm = M.matmul(bank[4 + q % 4][:, c * P:(c + 1) * P], L[rows, c * P:(c + 1) * P],
                                      R[rows, c * P:(c + 1) * P], start=True, stop=True)
                    mm.then_inc(sem("rk.gram"), 1)
                pe.wait_ge(sem("rk.ge"), p * 10 + 10)

            def inverse(p, more):
                tiles = {"D": IN4, "N4": IN4, "Z": IN4, "DA": IA4, "A4": IA4, "N2": IA8, "A8": IA8,
                         "A2": IE, "E": IE, "U": IU, "W": IW}
                if more:
                    pe.wait_ge(sem("rk.te"), p * 3 + 3)
                    pe.wait_ge(sem("rk.bonus"), p + 1)
                done = 0
                for k, step in enumerate(INVERSE):
                    for h in range(2):
                        if INV_ACT[k]:
                            pe.wait_ge(sem(f"inv{h}.act"), p * INV_ACT[-1] + INV_ACT[k])
                        pe.wait_ge(sem(f"inv{h}.dve"), p * INV_DVE[-1] + INV_DVE[k])
                        for which, (left, right, _, _) in enumerate(step["mm"]):
                            for c in range(4):
                                cs = slice(c * P, (c + 1) * P)
                                dst = bank[4 + 2 * h + which][:, cs]
                                if right == "I":
                                    mm = M.transpose(dst, tiles[left][h][:, cs], ident[:, :])
                                else:
                                    mm = M.matmul(dst, tiles[left][h][:, cs], tiles[right][h][:, cs],
                                                  start=True, stop=True)
                        mm.then_inc(sem(f"inv{h}.pe"), 1)
                    if more:
                        upto = 24 * (k + 1) // len(INVERSE)
                        for n in range(done, upto):
                            rkv_slice(p + 1, n)
                        done = upto
                for h in range(2):
                    pe.wait_ge(sem(f"inv{h}.dve"), p * INV_DVE[-1] + INV_DVE[-1])

            def right_side(p, par, c):
                cs = slice(c * P, (c + 1) * P)
                if c > 0:
                    pe.wait_ge(sem("sq.st"), p * 3 + c)
                    M.matmul(bank[4][:, 0:P], aT[par][:, cs], state[:, :], start=True, stop=True)
                for h in range(2):
                    mm = M.matmul(bank[4][:, h * 64:h * 64 + 64], Gak[h][:, cs],
                                  vpad[par][:, c * 256 + h * 192:c * 256 + h * 192 + 64],
                                  start=(c == 0), stop=True, skip_group_check=True)
                mm.then_inc(sem("sq.r"), 1)
                if c > 0:
                    M.matmul(bank[7][:, cs], state[:, :], rT[par][:, cs], start=False, stop=True,
                             skip_group_check=True)
                for h in range(2):
                    M.matmul(bank[7][:, cs], vpad[par][:, c * 256 + h * P:c * 256 + (h + 1) * P], Gqk[h][:, cs],
                             start=(c == 0 and h == 0), stop=True, skip_group_check=True)

            def solution(p, c):
                cs = slice(c * P, (c + 1) * P)
                pe.wait_ge(sem("sq.re"), p * 4 + c + 1)
                for h in range(2):
                    mm = M.matmul(bank[5][:, h * 64:h * 64 + 64], IU[h][:, cs], rhs[:, h * 64:h * 64 + 64],
                                  start=True, stop=True)
                mm.then_inc(sem("sq.sa"), 1)

            def state_result(p, par, c):
                cs = slice(c * P, (c + 1) * P)
                pe.wait_ge(sem("sq.se"), p * 4 + c + 1)
                if c < 3:
                    M.matmul(bank[6][:, 0:64], bN[par][:, cs], sapad[:, 0:64], start=True, stop=True,
                             skip_group_check=True)
                    M.matmul(bank[6][:, 64:P], bN[par][:, cs], sapad[:, 192:256], start=False, stop=True,
                             skip_group_check=True)
                    for h in range(2):
                        mm = M.matmul(bank[6][:, h * 64:h * 64 + 64], kN[par][:, cs],
                                      vpad[par][:, c * 256 + h * 192:c * 256 + h * 192 + 64],
                                      start=False, stop=True, skip_group_check=True)
                    if c > 0:
                        mm = M.matmul(bank[6][:, 0:P], ident[:, :], state[:, :], start=False, stop=True,
                                      skip_group_check=True)
                    mm.then_inc(sem("sq.s"), 1)
                for h in range(2):
                    mm = M.matmul(bank[7][:, cs], sapad[:, h * P:(h + 1) * P], Gqb[h][:, cs], start=False,
                                  stop=True, skip_group_check=True)
                if c == 3:
                    mm.then_inc(sem("sq.y"), 1)

            def gate(p):
                pe.wait_ge(sem("lg.ld"), (p + 1) * 32)
                pe.wait_ge(sem("rk.y"), p + 1)
                M.matmul(bank[3][:, :], lg2[:, 0:P], tile(glow, 0), start=True, stop=False)
                M.matmul(bank[3][:, :], lg2[0:32, P:2 * P], glow[0:32, S:2 * S], start=False, stop=True)\
                    .then_inc(sem("rk.g"), 1)

            def means(p, par):
                pe.wait_ge(sem("gn.y"), p + 1)
                M.matmul(bank[4][:, :], same[64][:, :], aT[par][:, :], start=True, stop=True).then_inc(sem("gn.m"), 1)

            def variances(p, par):
                pe.wait_ge(sem("gn.q"), p + 1)
                M.matmul(bank[5][:, :], same[64][:, :], kN[par][:, :], start=True, stop=True).then_inc(sem("gn.v"), 1)

            def pair(p, par, follows, more):
                grams(p, par, follows)
                inverse(p, more)
                right_side(p, par, 0)
                if more:
                    lora_products(p + 1)
                solution(p, 0)
                state_result(p, par, 0)
                right_side(p, par, 1)
                if more:
                    key_norms(p + 1)
                solution(p, 1)
                state_result(p, par, 1)
                right_side(p, par, 2)
                if more:
                    turn_v(p + 1)
                solution(p, 2)
                state_result(p, par, 2)
                right_side(p, par, 3)
                solution(p, 3)
                state_result(p, par, 3)
                gate(p)
                means(p, par)
                if more:
                    turn_b(p + 1)
                variances(p, par)
                if more:
                    turn_k(p + 1)
                    bonus_sums(p + 1)

            for n in range(24):
                rkv_slice(0, n)
            lora_products(0)
            key_norms(0)
            turn_v(0)
            turn_b(0)
            turn_k(0)
            bonus_sums(0)
            pair(0, 0, False, True)
            with pe.Fori(0, (PAIRS - 2) // 2) as j:
                pair(j * 2 + 1, 1, True, True)
                pair(j * 2 + 2, 0, True, True)
            pair(PAIRS - 1, 1, True, False)

            at_acts = [(tile(atH, k), tile(atL, k)) for k in range(4)]
            r_acts = [(tile(rH, k), tile(rL, k)) for k in range(PAIRS)]
            mix_acts = [(tile(mixH, k), tile(mixL, k)) for k in range(DT)]
            pe.wait_ge(sem("rk.y"), 1 + PAIRS)
            with pe.Fori(0, 4) as i:
                s0 = STRIP0["mix"] + i * 4
                two_tiles("mix", s0, 0, i * 2, h_out)
                two_tiles("mix", s0 + 1, 1, i * 2, h_out)
                pe.wait_ge(sem("mx.lo"), 12)
                two_tiles("mix", s0 + 2, 0, i * 2 + 1, at_acts)
                two_tiles("mix", s0 + 3, 1, i * 2 + 1, r_acts)
            pe.wait_ge(sem("mx.lo2"), 1 + DT)
            with pe.Fori(0, 2) as i:
                for j in range(2):
                    two_tiles("wo", STRIP0["wo"] + i * 2 + j, j, i, mix_acts)

            pe_norm(pe, "n_2", DT)
            pe.wait_ge(sem("norm.lo"), NORM0["n_2"]["lo"] + DT)
            with pe.Fori(0, 11) as i:
                for j in range(2):
                    two_tiles("up", STRIP0["up"] + i * 2 + j, j, i, h_out)
            pe.wait_ge(sem("up.lo"), FT)
            with pe.Fori(0, 2) as i:
                for nn in range(2):
                    for kk_ in range(3):
                        j6 = nn * 3 + kk_
                        k0 = sum(DOWN_K[:kk_])
                        acts = [(tile(fH, k), tile(fL, k)) for k in range(k0, k0 + DOWN_K[kk_])]
                        strip_ready(STRIP0["down"] + i * 6 + j6)
                        for j in range(2):
                            b = nn * 2 + j
                            if kk_ == 0:
                                bank_free("down", b, i)
                            product(bank[b][:, :], j6 % 2, 256, j * P, P, acts, first=(kk_ == 0),
                                    last=(kk_ == 2)).then_inc(products_done, 1)
            pe_norm(pe, "n_out", DT)
            pe.wait_ge(sem("norm.hf"), NORM0["n_out"]["hf"] + DT)
            for q in range(8):
                t, half = q // 2, q % 2
                if q >= 2:
                    pe.wait_ge(sem("fin.out"), q - 1)
                for d in range(4):
                    mm = M.transpose(bank[4 + q % 2][:, d * P:(d + 1) * P],
                                     xT[:, (half * 4 + d) * S + t * P:(half * 4 + d) * S + (t + 1) * P], ident[:, :])
                mm.then_inc(sem("fin.t"), 1)

        @block.scalar
        def _(act):
            act.wait_ge(sem("vecrow_zero"), 1)
            for row, n, w, src in vec_dmas:
                c0 = row // P * P
                act.dma_start(vecrow[row % P:row % P + n, c0:c0 + w], src).then_inc(sem("vec_loaded"), 16)
            for d in range(DT):
                act.wait_ge(sem("xt.t"), d + 1)
                A.copy(xt[d], bank[5 + d % 2][:, :]).then_inc(sem("xt.taken"), 1)

            def product_ready(s, half):
                act.wait_ge(products_done, done_value(s, half))

            act.drain()
            act_norm(act, "n_pool", xt, D, lambda e, d: e.wait_ge(sem("xt.taken"), d + 1), h_out)
            for g in range(4):
                s0 = STRIP0["pool"] + 6 * g
                for t in range(4):
                    n = 4 * g + t
                    if n >= 2:
                        act.wait_ge(sem("pool.win"), n - 1)
                    product_ready(s0 + t // 2, t % 2)
                    A.copy(upad[n % 2][:, PAD:PAD + S], bank[t][:, :]).then_inc(evac[t], 1)
                for t in range(4):
                    if g >= 1:
                        act.wait_ge(evac[t], 3 * g)
                    product_ready(s0 + 2 + t // 2, t % 2)
                    A.activation(tile(zp, t), bank[t][:, :], ACT.Silu).then_inc(evac[t], 1)

            act_norm(act, "n_mla", xt, D, lambda e, d: e.wait_ge(*out_tile_taken("pool_out", d)), h_out)
            act.wait_ge(sem("norm.lo"), NORM0["n_mla"]["lo"] + DT)
            act.dma_start(posi[:, :], a["positions"][0:1, :].partition_broadcast(P)).then_inc(sem("pos_loaded"), 16)
            act.dma_start(invf[:, :], a["inv_freq"]).then_inc(sem("pos_loaded"), 16)
            s0 = STRIP0["lat"]
            for t, (s, half, b) in enumerate(((0, 0, 0), (0, 1, 1), (1, 0, 2), (1, 1, 3), (2, 1, 0))):
                product_ready(s0 + s, half)
                A.copy(lat_t[t], bank[b][:, :]).then_inc(evac[b], 1)
            act.wait_ge(sem("trig.r"), 1)
            A.activation(sinT[:, :], tile(ang, 0), ACT.Sin).then_inc(sem("trig.s"), 1)
            A.activation(tile(ang, 1), tile(ang, 0), ACT.Sin, scale=0.5).then_inc(sem("trig.s"), 1)
            act.drain()
            act_norm(act, "n_q", lat_t[0:3], Q_RANK, lambda e, d: None, lat_out[0:3])
            act.drain()
            act_norm(act, "n_kv", lat_t[3:5], KV_RANK, lambda e, d: None, lat_out[3:5])
            with act.Fori(0, 4) as i:
                for j in range(2):
                    for half in range(2):
                        product_ready(STRIP0["mz"] + i * 2 + j, half)
                        A.activation(dtile(zm, i * 4 + j * 2 + half), bank[j * 2 + half][:, :], ACT.Silu)\
                            .then_inc(evac[j * 2 + half], 1)
            act.wait_ge(sem("norm.lo"), NORM0["n_kv"]["lo"] + 2)
            act.wait_ge(sem("krope"), 1)
            score_bank, turn_bank = (bank[4], bank[5], bank[0]), (bank[6], bank[1])
            with act.Fori(0, 8) as i:
                sq_ = STRIP0["heads"] + i * 2
                product_ready(sq_, 0)
                for h in range(2):
                    A.copy(tile(qT, h), bank[h][:, :]).then_inc(evac[h], 1)
                product_ready(sq_ + 1, 0)
                for h, b in ((0, 3), (1, 0)):
                    A.activation(tile(kT, h), bank[b][:, :], ACT.Copy, scale=QK_SCALE).then_inc(evac[b], 1)
                product_ready(sq_ + 1, 1)
                for b in (1, 2):
                    A.copy(vN[:, (b - 1) * 512:b * 512], bank[b][:, :]).then_inc(evac[b], 1)

                def exponentials(u):
                    w, n = (u % 4 + 1) * P, u % 3
                    act.wait_ge(sem("m.max"), i * 8 + u + 1)
                    if u >= 3:
                        act.wait_ge(sem("m.t"), i * 8 + u - 2)
                    A.activation(prob[n][:, 0:w], score_bank[n][:, 0:w], ACT.Exp, bias=stat[:, n:n + 1],
                                 accum_out=stat[:, 3 + n:4 + n]).then_inc(sem("m.exp"), 1)

                def take_turned(u):
                    qb = u % 4
                    act.wait_ge(sem("m.t"), i * 8 + u + 1)
                    A.copy(probT[:, :].rearrange("p (k q) -> p k q", k=4)[:, 0:qb + 1, qb * P:(qb + 1) * P],
                           turn_bank[u % 2][:, 0:(qb + 1) * P].rearrange("p (k q) -> p k q", q=P))\
                        .then_inc(sem("m.te"), 1)

                def upper_part(h):
                    act.wait_ge(sem("m.y"), i * 2 + h + 1)
                    A.copy(dtile(y2H, i * 2 + h), dtile(zm, i * 2 + h)).then_inc(sem("m.hi"), 1)

                exponentials(0)
                exponentials(1)
                for u in range(8):
                    if u + 2 < 8:
                        exponentials(u + 2)
                    take_turned(u)
                    if u == 6:
                        upper_part(0)
                act.wait_ge(sem("ada.col"), i + 2)
                A.copy(ada[:, ds(i * 6, 6)], bank[3][:, 0:6]).then_inc(evac[3], 1)
                upper_part(1)

            act_norm(act, "n_fin", xt, D, lambda e, d: e.wait_ge(*out_tile_taken("mla_out", d)), None)
            act_norm(act, "n_1", xt, D, lambda e, d: e.wait_ge(sem("norm.hf"), NORM0["n_fin"]["hf"] + d + 1), h_out)
            act.wait_ge(sem("norm.lo"), NORM0["n_1"]["lo"] + DT)
            units_before = 0
            for g in range(3):
                sg = STRIP0["att"] + g * 6
                for kind, dst in ((0, aq), (1, ak)):
                    for t in range(4):
                        product_ready(sg + kind * 2 + t // 2, t % 2)
                        o, x = tile(dst, t), bank[t][:, :]
                        if g:
                            o, x = o.rearrange("p (b q) -> p b q", b=4), x.rearrange("p (q b) -> p b q", b=4)
                        A.activation(o, x, ACT.Copy, scale=ATT_DIM ** -0.5 if kind == 0 else 1.0)\
                            .then_inc(evac[t], 1)
                if g == 0:
                    act.wait_ge(sem("att.vz"), 1)
                av6 = av[:, :].rearrange("p (k r par c e) -> p k r par c e", k=4, r=4, par=2, c=2)
                for j in range(2):
                    for hv in range(2):
                        b = j * 2 + hv
                        product_ready(sg + 4 + j, hv)
                        x = bank[b][:, :].rearrange("p (k r par e) -> p k r par e", k=2, r=2, par=2)
                        for par in range(2):
                            cp = A.copy(av6[:, 2 * hv:2 * hv + 2, 2 * j:2 * j + 2, par, par, :], x[:, :, :, par, :])
                        cp.then_inc(evac[b], 1)
                units = att_units(g)

                def take_pair(u):
                    h = units[u][0]
                    act.wait_ge(sem("att.pv"), units_before + u + 1)
                    A.copy(tile(num[g], h // 2), bank[7][:, :]).then_inc(sem("att.num"), 1)

                def pair_ends(u):
                    return units[u][0] % 2 == 1 and (u + 1 == len(units) or units[u + 1][0] != units[u][0])

                for u in range(len(units) + 2):
                    if u < len(units):
                        h, blocks = units[u]
                        U = units_before + u
                        act.wait_ge(sem("att.max"), U + 1)
                        if U >= 2:
                            act.wait_ge(sem("att.t"), U - 1)
                        for qb, kb0, nk, c0 in att_rows(blocks):
                            n = g * 32 + qb * ATT_HEADS + h
                            ex = A.activation(ap_[U % 2][:, c0:c0 + nk * P], bank[4 + U % 2][:, c0:c0 + nk * P],
                                              ACT.Exp, bias=nmax[:, n:n + 1], accum_out=den[:, n:n + 1])
                        ex.then_inc(sem("att.exp"), 1)
                    if u >= 2 and pair_ends(u - 2):
                        take_pair(u - 2)
                units_before += len(units)
            act.wait_ge(sem("att.exp"), units_before)
            act.wait_ge(sem("att.max"), units_before)
            nat = "(B p h) -> p B h"
            for n, x in enumerate((nmax, den)):
                act.dma_start(scratch[n].rearrange(nat, p=P, h=ATT_HEADS),
                              x[:, 0:32].rearrange("p (B h) -> p B h", h=ATT_HEADS)).then_inc(sem("st.out"), 16)
            act.wait_ge(sem("st.out"), 32)
            for n in range(2):
                act.dma_start(stq[:, n * 32:n * 32 + 32], scratch[n].rearrange("(q c) -> q c", q=P))\
                    .then_inc(sem("st.in"), 16)
            act.wait_ge(sem("st.d"), 1)
            A.activation(fac[:, :], fac[:, :], ACT.Exp).then_inc(sem("st.e"), 1)
            act.wait_ge(sem("st.f"), 1)
            act.dma_start(scratch[2].rearrange("(q c) -> q c", q=P), fac[:, 0:32]).then_inc(sem("st.out"), 16)
            act.wait_ge(sem("st.out"), 48)
            act.dma_start(fac0[:, :].rearrange("p (B h) -> p B h", h=ATT_HEADS),
                          scratch[2].rearrange(nat, p=P, h=ATT_HEADS)).then_inc(sem("st.f0"), 16)
            act.wait_ge(sem("st.f0"), 16)
            act.wait_ge(sem("att.pv"), units_before)
            for pr in range(4):
                if pr >= 1:
                    act.wait_ge(sem("cmb.pe"), pr)
                for g in range(3):
                    f = (fac0 if g == 0 else fac[:, 32 * g:32 * g + 32])[:, :]
                    f = f.rearrange("p (k h) -> p k h", k=4)[:, :, 2 * pr:2 * pr + 2]
                    A.copy(spread[g][:, :].rearrange("p (k h e) -> p k h e", k=4, h=2),
                           f.unsqueeze(3).to_broadcast([P, 4, 2, 64])).then_inc(sem("cmb.f"), 1)

            act.wait_ge(sem("att.at"), 4)
            s0 = STRIP0["lora"]
            for z, s, half, b, rows in ((0, 0, 1, 0, P), (1, 1, 0, 2, P), (2, 1, 1, 3, 32)):
                product_ready(s0 + s, half)
                A.copy(zsh[z][0:rows, 1:S + 1], bank[b][0:rows, :]).then_inc(evac[b], 1)
            act.wait_ge(sem("lora.z"), 3)
            A.activation(wlow[0:64, :], wlow[0:64, :], ACT.Tanh).then_inc(sem("lora.act"), 1)
            A.activation(tile(glow, 0), tile(glow, 0), ACT.Sigmoid)
            A.activation(glow[0:32, S:2 * S], glow[0:32, S:2 * S], ACT.Sigmoid).then_inc(sem("lora.act"), 1)

            def load_lora(p):
                for dst, src in ((lw2[0:64, :], a["w2_2"][0, :, ds(p * P, P)]),
                                 (lw2[64:128, :], a["a2_2"][0, :, ds(p * P, P)])):
                    act.dma_start(dst, src).then_inc(sem("lw.ld"), 16)

            def load_gate(p):
                act.wait_ge(sem("rk.g"), p + 1)
                for dst, src in ((lg2[:, 0:P], a["g2_2"][0, 0:P, ds(p * P, P)]),
                                 (lg2[0:32, P:2 * P], a["g2_2"][0, P:160, ds(p * P, P)])):
                    act.dma_start(dst, src).then_inc(sem("lg.ld"), 16)

            def take_rkv(p):
                s0 = STRIP0["rkv"] + p * 2
                for z, s, half in ((1, 0, 1), (0, 0, 0), (2, 1, 1)):
                    product_ready(s0 + s, half)
                    A.copy(zsh[z][:, 1:S + 1], bank[z][:, :]).then_inc(evac[z], 1)

            def key_squares(p):
                act.wait_ge(sem("rk.kk"), p + 1)
                A.activation(tile(sq, 0), kk[:, :], ACT.Square).then_inc(sem("rk.sq"), 1)

            def sigmoids(p, par):
                act.wait_ge(sem("rk.lora"), p + 1)
                A.activation(lwd[:, :], bank[0][:, :], ACT.Sigmoid, bias=pcol[par][:, 3:4])
                A.activation(aa[:, :], bank[1][:, :], ACT.Sigmoid, bias=pcol[par][:, 4:5]).then_inc(sem("rk.sig"), 1)

            def take_v(p, par):
                act.wait_ge(sem("rk.tv"), p + 1)
                vp = vpad[par][:, :].rearrange("p (c x) -> p c x", c=4)
                vb = bank[0][:, :].rearrange("p (c h e) -> p c h e", c=4, h=2)
                A.copy(vp[:, :, 0:64], vb[:, :, 0, :])
                A.copy(vp[:, :, 192:256], vb[:, :, 1, :]).then_inc(sem("rk.te"), 1)

            def key_lengths(p):
                act.wait_ge(sem("rk.ss"), p + 1)
                A.activation(tile(sq, 1), bank[2][:, :], ACT.Sqrt).then_inc(sem("rk.nr"), 1)

            def decays(p, par):
                act.wait_ge(sem("rk.lp"), p + 1)
                A.activation(epos[:, :], cc[:, :], ACT.Exp)
                A.activation(fade[par][:, 0:3], fade[par][:, 0:3], ACT.Exp)
                A.activation(lwd[:, :], lwd[:, :], ACT.Exp)
                act.drain()
                A.activation(cc[:, :], cc[:, :], ACT.Exp, scale=-1.0).then_inc(sem("rk.ex"), 1)

            def take_b(p, par):
                act.wait_ge(sem("rk.tb"), p + 1)
                A.copy(bN[par][:, :], bank[1][:, :]).then_inc(sem("rk.te"), 1)

            def take_k(p, par):
                act.wait_ge(sem("rk.tk"), p + 1)
                A.copy(kN[par][:, :], bank[0][:, :]).then_inc(sem("rk.te"), 1)

            def take_inverse(p):
                goes = {"N2": IA8, "N4": IN4, "A4": IA4, "A8": IA8, "W": IW, "Z": IN4}
                for k, step in enumerate(INVERSE):
                    for h in range(2):
                        for which, (_, _, by, to) in enumerate(step["mm"]):
                            if by == "act":
                                act.wait_ge(sem(f"inv{h}.pe"), p * len(INVERSE) + k + 1)
                                A.copy(goes[to][h][:, :], bank[4 + 2 * h + which][:, :])\
                                    .then_inc(sem(f"inv{h}.act"), 1)

            def take_right_side(p, c):
                act.wait_ge(sem("sq.r"), p * 4 + c + 1)
                A.copy(rhs[:, :], bank[4][:, 0:P]).then_inc(sem("sq.re"), 1)

            def take_solution(p, c):
                act.wait_ge(sem("sq.sa"), p * 4 + c + 1)
                A.copy(sapad[:, 0:64], bank[5][:, 0:64])
                A.copy(sapad[:, 192:256], bank[5][:, 64:P]).then_inc(sem("sq.se"), 1)

            def take_state(p, par, c):
                act.wait_ge(sem("sq.s"), p * 3 + c + 1)
                A.activation(state[0:64, 0:64], bank[6][0:64, 0:64], ACT.Copy, scale=fade[par][0:64, c:c + 1])
                A.activation(state[64:P, 64:P], bank[6][64:P, 64:P], ACT.Copy, scale=fade[par][64:P, c:c + 1])\
                    .then_inc(sem("sq.st"), 1)

            def pair(p, par, more):
                nxt = 1 - par
                load_gate(p)
                if more:
                    load_lora(p + 1)
                take_inverse(p)
                take_right_side(p, 0)
                if more:
                    take_rkv(p + 1)
                take_solution(p, 0)
                take_state(p, par, 0)
                if more:
                    key_squares(p + 1)
                take_right_side(p, 1)
                take_solution(p, 1)
                if more:
                    sigmoids(p + 1, nxt)
                take_state(p, par, 1)
                take_right_side(p, 2)
                take_solution(p, 2)
                if more:
                    take_v(p + 1, nxt)
                take_state(p, par, 2)
                take_right_side(p, 3)
                take_solution(p, 3)
                if more:
                    key_lengths(p + 1)
                    decays(p + 1, nxt)
                act.wait_ge(sem("sq.y"), p + 1)
                A.activation(aT[par][:, :], bank[7][:, :], ACT.Copy, scale=SCAN_SCALE ** -2).then_inc(sem("gn.y"), 1)
                if more:
                    take_b(p + 1, nxt)
                act.wait_ge(sem("gn.c"), p + 1)
                A.activation(kN[par][:, :], rT[par][:, :], ACT.Square).then_inc(sem("gn.q"), 1)
                act.wait_ge(sem("gn.v"), p + 1)
                A.activation(bN[par][:, :], bank[5][:, :], ACT.Sqrt, scale=1.0 / 64, bias=gneps_c[:, 0:1])\
                    .then_inc(sem("gn.s"), 1)
                if more:
                    take_k(p + 1, nxt)

            load_lora(0)
            take_rkv(0)
            key_squares(0)
            sigmoids(0, 0)
            take_v(0, 0)
            key_lengths(0)
            decays(0, 0)
            take_b(0, 0)
            take_k(0, 0)
            pair(0, 0, True)
            with act.Fori(0, (PAIRS - 2) // 2) as j:
                pair(j * 2 + 1, 1, True)
                pair(j * 2 + 2, 0, True)
            pair(PAIRS - 1, 1, False)

            act.wait_ge(sem("rk.y"), 1 + PAIRS)
            act.wait_ge(sem("norm.lo"), NORM0["n_1"]["lo"] + DT)
            for k in range(12):
                src, dst = (tile(at, k), tile(atH, k)) if k < 4 else (tile(yr, k - 4), tile(rH, k - 4))
                A.copy(dst, src).then_inc(sem("mx.hi"), 1)
            with act.Fori(0, 4) as i:
                s0 = STRIP0["mix"] + i * 4
                for j, buf in enumerate((sq, hf)):
                    for half in range(2):
                        act.wait_ge(sem("mx.lo2"), i * 2 + 1)
                        product_ready(s0 + j, half)
                        A.activation(tile(buf, half), bank[2 * j + half][:, :], ACT.Sigmoid,
                                     bias=dcol("b_gate_2", i * 2 + (j * DT + half))).then_inc(evac[2 * j + half], 1)

            act_norm(act, "n_2", xt, D, lambda e, d: e.wait_ge(*out_tile_taken("wo", d)), h_out)
            act.wait_ge(sem("norm.lo"), NORM0["n_2"]["lo"] + DT)
            act.wait_ge(sem("up.zero"), 1)
            with act.Fori(0, 11) as i:
                s0 = STRIP0["up"] + i * 2
                for t in range(4):
                    act.wait_ge(sem("up.conv"), i * 4 + t + 1)
                    product_ready(s0 + t // 2, t % 2)
                    A.copy(cpad[t % 2][:, 2:2 + S], bank[t][:, :]).then_inc(evac[t], 1)
                    if t >= 2:
                        act.wait_ge(sem("up.conv"), i * 4 + t + 1)
                        A.activation(tile(sq, t - 2), tile(sq, t - 2), ACT.Silu).then_inc(sem("up.silu"), 1)
            act_norm(act, "n_out", xt, D, lambda e, d: e.wait_ge(*out_tile_taken("down", d)), None)
            for q in range(8):
                t, half = q // 2, q % 2
                act.wait_ge(sem("fin.t"), q + 1)
                if t >= 2:
                    act.wait_ge(sem(f"out_stored{t % 2}"), 16)
                A.copy(yout[t % 2][:, half * S:(half + 1) * S], bank[4 + q % 2][:, :]).then_inc(sem("fin.out"), 1)

        @block.vector
        def _(dve):
            def product_ready(s, half):
                dve.wait_ge(products_done, done_value(s, half))

            def split(hi, lo, x):
                V.tensor_copy(hi, x)
                dve.drain()
                return V.tensor_tensor(lo, x, f32(hi), ALU.subtract)

            dve.wait_ge(sem("consts"), 1)
            V.tensor_tensor(up16[:, :], upper1[:, :], same[16][:, :], ALU.mult)
            V.tensor_tensor(low16[:, :], lower1[:, :], same[16][:, :], ALU.mult)
            for n, wide in ((16, same[32]), (32, same[64]), (64, ones)):
                V.tensor_tensor(step_mask[n][:, :], wide[:, :], same[n][:, :], ALU.subtract)
            V.tensor_reduce(res4[:, :], ident[:, :].rearrange("p (k r) -> p r k", r=4), AX.X, ALU.add)
            V.tensor_tensor(tmp_mask[:, :], lower1[:, :], ident[:, :], ALU.add)
            V.tensor_copy(ident_b[:, :], ident[:, :])
            V.tensor_scalar(neg_band[:, P:2 * P], upper1[:, :], -BIG, None, ALU.mult)
            V.tensor_scalar(neg_band[:, 0:P], lower1[:, :], -BIG, None, ALU.mult)
            for g, w in enumerate(POOL_WINDOWS):
                V.tensor_scalar(cinv[:, g * PAD:(g + 1) * PAD], cinv[:, g * PAD:(g + 1) * PAD], float(w), None, ALU.min)
            dve.drain()
            V.reciprocal(cinv[:, :], cinv[:, :])
            for n in (16, 32, 64):
                V.tensor_tensor(step_mask[n][:, :], step_mask[n][:, :], lower1[:, :], ALU.mult)
            m4 = tmp_mask[:, :].rearrange("p (k r) -> p k r", r=4)
            V.tensor_tensor(m4, m4, res4[:, :].unsqueeze(1).to_broadcast([P, 32, 4]), ALU.mult)
            dve.drain()
            V.tensor_scalar(neg_dil[:, :], tmp_mask[:, :], BIG, -BIG, ALU.mult, ALU.add).then_inc(sem("masks"), 1)
            dve.wait_ge(sem("vec.t"), 1)
            V.tensor_copy(vec[:, :], bank[4][:, 0:VEC_ALL]).then_inc(sem("vec.ready"), 1)
            dve.drain()
            V.tensor_scalar(one_minus_ka[:, :], vec[:, VEC0["k_a_2"]:VEC0["k_a_2"] + DT], -1.0, 1.0, ALU.mult, ALU.add)

            dve_norm(dve, "n_pool", xt, cols("pool_norm", DT), h_out)
            dve.drain()
            W_ = PAD + S
            tmp = [sq[:, 0:W_], hf[:, 0:W_]]
            for g, w in enumerate(POOL_WINDOWS):
                s0 = STRIP0["pool"] + 6 * g
                for t in range(4):
                    u = upad[t % 2]
                    dve.wait_ge(evac[t], 3 * g + 1)
                    cur = u[:, :]
                    for l in range(g + 1):
                        sh, nxt = 1 << l, tmp[l % 2]
                        V.tensor_tensor(nxt[:, 2 * sh - 1:W_], cur[:, 2 * sh - 1:W_], cur[:, sh - 1:W_ - sh], ALU.add)
                        dve.drain()
                        cur = nxt
                    mean = tmp[(g + 1) % 2][:, PAD:W_]
                    V.scalar_tensor_tensor(mean, cur[:, PAD:W_], 1.0 / w, u[:, PAD:W_], ALU.mult, ALU.subtract)
                    V.tensor_tensor(inv[:, 0:PAD], cur[:, PAD:2 * PAD], cinv[:, g * PAD:(g + 1) * PAD], ALU.mult)
                    dve.drain()
                    V.tensor_tensor(mean[:, 0:PAD], inv[:, 0:PAD], u[:, PAD:2 * PAD], ALU.subtract)\
                        .then_inc(sem("pool.win"), 1)
                    dve.drain()
                    if g >= 1 and t == 0:
                        product_ready(s0 - 1, 1)
                    split(tile(poolH, t), tile(poolL, t), mean).then_inc(sem("pool.lo"), 1)
                    dve.drain()
                for t in range(4):
                    product_ready(s0 + 4 + t // 2, t % 2)
                    dve.wait_ge(evac[t], 3 * g + 2)
                    y = tmp[t % 2][:, 0:S]
                    V.scalar_tensor_tensor(y, bank[t][:, :], col("pool_scale", 4 * g + t), tile(zp, t),
                                           ALU.mult, ALU.mult).then_inc(evac[t], 1)
                    dve.drain()
                    split(tile(y1H, 4 * g + t), tile(y1L, 4 * g + t), y).then_inc(sem("pool.ylo"), 1)
                    dve.drain()

            def residual(ph):
                with dve.Fori(0, 2) as i:
                    for nn in range(2):
                        for j in range(2):
                            product_ready(STRIP0[ph] + i * 4 + nn * 2 + 1, j)
                            x = dtile(xT, i * 4 + nn * 2 + j)
                            V.tensor_tensor(x, bank[nn * 2 + j][:, :], x, ALU.add).then_inc(evac[nn * 2 + j], 1)

            residual("pool_out")

            dve.drain()
            dve_norm(dve, "n_mla", xt, cols("mla_norm", DT), h_out)
            dve.wait_ge(sem("pos_loaded"), 32)
            a0_, a1_, a2_ = [tile(ang, n) for n in range(3)]
            V.tensor_copy(a0_, posi[:, :])
            dve.drain()
            V.tensor_scalar(a0_, a0_, invf[:, 0:1], None, ALU.mult)
            dve.drain()
            V.tensor_scalar(a1_, a0_, 1.0 / (2.0 * np.pi), ROUND, ALU.mult, ALU.add)
            dve.drain()
            V.tensor_scalar(a1_, a1_, ROUND, None, ALU.subtract)
            for part in TWO_PI:
                dve.drain()
                V.scalar_tensor_tensor(a0_, a1_, -part, a0_, ALU.mult, ALU.add)
            dve.drain()
            V.tensor_scalar(a0_, a0_, PI_IN, -PI_IN, ALU.min, ALU.max).then_inc(sem("trig.r"), 1)
            dve.wait_ge(sem("trig.s"), 2)
            V.tensor_tensor(cosT[:, :], a1_, a1_, ALU.mult)
            V.tensor_scalar(sinT[0:32, :], sinT[0:32, :], -1.0, None, ALU.mult)
            V.tensor_scalar(sinT[64:96, :], sinT[64:96, :], -1.0, None, ALU.mult)
            dve.drain()
            V.tensor_scalar(cosT[:, :], cosT[:, :], -2.0, 1.0, ALU.mult, ALU.add)
            dve.drain()

            def rotate(x, t, turned, rows):
                V.tensor_tensor(t, x[0:rows, :], cosT[0:rows, :], ALU.mult)
                for q in range(0, rows, 32):
                    o = q ^ 32
                    last = V.tensor_tensor(turned[q:q + 32, :], x[o:o + 32, :], sinT[q:q + 32, :], ALU.mult)
                return last

            product_ready(STRIP0["lat"] + 3, 1)
            rotate(bank[2], a2_[0:64, :], a1_, 64).then_inc(evac[2], 1)
            dve.drain()
            V.tensor_tensor(a2_[0:64, :], a2_[0:64, :], a1_[0:64, :], ALU.add)
            dve.drain()
            V.tensor_scalar(krope[0:64, :], a2_[0:64, :], QK_SCALE, None, ALU.mult)
            V.tensor_scalar(krope[64:128, :], a2_[0:64, :], QK_SCALE, None, ALU.mult).then_inc(sem("krope"), 1)
            dve.drain()
            dve_norm(dve, "n_q", lat_t[0:3], cols("mla_q_norm", 3), lat_out[0:3])
            dve.drain()
            dve_norm(dve, "n_kv", lat_t[3:5], cols("mla_kv_norm", 2), lat_out[3:5])
            dve.drain()
            score_bank, out_bank = (bank[4], bank[5], bank[0]), (bank[2], bank[7])
            with dve.Fori(0, 8) as i:
                dve.drain()
                product_ready(STRIP0["heads"] + i * 2, 1)
                rotate(bank[2], tile(sq, 0), tile(sq, 1), P).then_inc(evac[2], 1)
                dve.drain()
                V.tensor_tensor(qrope[:, :], tile(sq, 0), tile(sq, 1), ALU.add).then_inc(sem("qrope"), 1)

                def maximum(u):
                    w, n = (u % 4 + 1) * P, u % 3
                    dve.wait_ge(sem("m.s"), i * 8 + u + 1)
                    V.tensor_reduce(stat[:, n:n + 1], score_bank[n][:, 0:w], AX.X, ALU.max, negate=True)\
                        .then_inc(sem("m.max"), 1)

                def divide(u):
                    w, n = (u % 4 + 1) * P, u % 3
                    dve.wait_ge(sem("m.exp"), i * 8 + u + 1)
                    V.reciprocal(stat[:, 6 + n:7 + n], stat[:, 3 + n:4 + n])
                    dve.drain()
                    V.tensor_scalar(prob[n][:, 0:w], prob[n][:, 0:w], stat[:, 6 + n:7 + n], None, ALU.mult)\
                        .then_inc(sem("m.p"), 1)

                def gated(h):
                    dve.wait_ge(sem("m.o"), i * 2 + h + 1)
                    z = dtile(zm, i * 2 + h)
                    V.tensor_tensor(z, out_bank[h][:, :], z, ALU.mult).then_inc(sem("m.y"), 1)

                def lower_part(h):
                    dve.wait_ge(sem("m.hi"), i * 2 + h + 1)
                    V.tensor_tensor(dtile(y2L, i * 2 + h), dtile(zm, i * 2 + h), f32(dtile(y2H, i * 2 + h)),
                                    ALU.subtract).then_inc(sem("m.lo"), 1)

                maximum(0)
                maximum(1)
                for u in range(8):
                    divide(u)
                    if u + 2 < 8:
                        maximum(u + 2)
                    if u == 5:
                        gated(0)
                lower_part(0)
                gated(1)
                dve.drain()
                lower_part(1)
            dve.drain()
            residual("mla_out")

            dve.wait_ge(evac[3], fill("heads", 3) + 16)
            V.tensor_tensor(ada[:, :], ada[:, :], vec[:, VEC0["b_ada_2"]:VEC0["b_ada_2"] + 48], ALU.add)
            dve.drain()
            for gain, name, c0 in ((gain1, "norm1_w_2", DT), (gain2, "norm2_w_2", 4 * DT)):
                V.scalar_tensor_tensor(gain[:, :], ada[:, c0:c0 + DT], 1.0, vec[:, VEC0[name]:VEC0[name] + DT],
                                       ALU.add, ALU.mult)
            dve.drain()
            dve_norm(dve, "n_fin", xt, cols("final_norm", DT), None)
            dve.drain()
            dve_norm(dve, "n_1", xt, [gain1[:, d:d + 1] for d in range(DT)], h_out,
                     [ada[:, d:d + 1] for d in range(DT)])
            dve.drain()
            V.memset(av[:, :], 0.0).then_inc(sem("att.vz"), 1)
            units_before = 0
            for g in range(3):
                units = att_units(g)

                def maxima(u):
                    h, blocks = units[u]
                    U = units_before + u
                    dve.wait_ge(sem("att.s"), U + 1)
                    rows = att_rows(blocks)
                    runs = [rows[:1], rows[1:]] if rows[0][2] != rows[-1][2] else [rows]
                    for run in runs:
                        qb, _, nk, c0 = run[0]
                        n = len(run)
                        x = bank[4 + U % 2][:, c0:c0 + n * nk * P].rearrange("p (n w) -> p n w", n=n)
                        m0 = g * 32 + qb * ATT_HEADS + h
                        last = V.tensor_reduce(nmax[:, m0:m0 + (n - 1) * ATT_HEADS + 1:ATT_HEADS], x, AX.X, ALU.max,
                                               negate=True)
                    last.then_inc(sem("att.max"), 1)

                def take_turned(u):
                    U = units_before + u
                    w = len(units[u][1]) * P
                    dve.wait_ge(sem("att.t"), U + 1)
                    if U >= 2:
                        dve.wait_ge(sem("att.pv"), U - 1)
                    V.tensor_copy(apT[U % 2][:, 0:w], bank[6][:, 0:w]).then_inc(sem("att.te"), 1)

                for u in range(len(units) + 1):
                    if u < len(units):
                        maxima(u)
                    if u >= 1:
                        take_turned(u - 1)
                units_before += len(units)
            dve.wait_ge(sem("st.in"), 32)
            negs = [stq[:, 0:32], nmax[:, 32:64], nmax[:, 64:96]]
            dens = [stq[:, 32:64], den[:, 32:64], den[:, 64:96]]
            facs = [fac[:, 32 * g:32 * g + 32] for g in range(3)]
            V.tensor_tensor(zden[:, :], negs[0], negs[1], ALU.min)
            dve.drain()
            V.tensor_tensor(zden[:, :], zden[:, :], negs[2], ALU.min)
            dve.drain()
            for g in range(3):
                last = V.tensor_tensor(facs[g], zden[:, :], negs[g], ALU.subtract)
            last.then_inc(sem("st.d"), 1)
            dve.wait_ge(sem("st.e"), 1)
            for g in range(3):
                V.tensor_tensor(dens[g], dens[g], facs[g], ALU.mult)
            dve.drain()
            V.tensor_tensor(zden[:, :], dens[0], dens[1], ALU.add)
            dve.drain()
            V.tensor_tensor(zden[:, :], zden[:, :], dens[2], ALU.add)
            dve.drain()
            V.reciprocal(zden[:, :], zden[:, :])
            dve.drain()
            for g in range(3):
                last = V.tensor_tensor(facs[g], facs[g], zden[:, :], ALU.mult)
            last.then_inc(sem("st.f"), 1)
            dve.wait_ge(sem("att.num"), 12)
            for pr in range(4):
                dve.wait_ge(sem("cmb.pe"), pr + 1)
                n_ = [tile(num[g], pr) for g in range(3)]
                for g in range(3):
                    last = V.tensor_tensor(n_[g], n_[g], bank[4 + g][:, :], ALU.mult)
                last.then_inc(sem("cmb.used"), 1)
                dve.drain()
                V.tensor_tensor(n_[1], n_[1], n_[2], ALU.add)
                dve.drain()
                V.tensor_tensor(tile(at, pr).rearrange("p (q b) -> p b q", b=4), n_[1].rearrange("p (b q) -> p b q", b=4),
                                n_[0].rearrange("p (q b) -> p b q", b=4), ALU.add).then_inc(sem("att.at"), 1)
            dve.drain()

            def shifted(z, mu, out_, rows=P):
                V.tensor_tensor(sq[0:rows, S:2 * S], z[0:rows, 0:S], z[0:rows, 1:S + 1], ALU.subtract)
                dve.drain()
                return V.scalar_tensor_tensor(out_, sq[0:rows, S:2 * S], mu, z[0:rows, 1:S + 1], ALU.mult, ALU.add)

            mu = VEC0["mu_shift_2"]
            dve.wait_ge(sem("cmb.pe"), 4)
            for z in range(3):
                V.memset(zsh[z][:, 0:1], 0.0)
            for b in range(2):
                V.memset(vpad[b][:, :], 0.0)
            V.memset(sapad[:, :], 0.0)
            V.memset(state[:, :], 0.0).then_inc(sem("rk.zero"), 1)
            dve.drain()
            for n, (z, b, out_, rows) in enumerate(((0, 0, wlow[:, :], P), (1, 2, tile(glow, 0), P),
                                                    (2, 3, glow[0:32, S:2 * S], 32))):
                dve.wait_ge(evac[b], fill("lora", b) + 1)
                shifted(zsh[z], vec[0:rows, mu + 24 + n:mu + 25 + n], out_, rows).then_inc(sem("lora.z"), 1)
                dve.drain()

            def masked(dst, x, mask):
                m = mask[:, :].unsqueeze(1).to_broadcast([P, 4, P])
                return V.tensor_tensor(dst[:, :].rearrange("p (c t) -> p c t", c=4),
                                       x.rearrange("p (c t) -> p c t", c=4), m, ALU.mult)

            def decayed_keys(p, par):
                pc = pcol[par]
                for z in range(3):
                    V.memset(zsh[z][:, 0:1], 0.0)
                V.tensor_copy(pc[:, 0:3], vec[:, mu:mu + 24].rearrange("p (j r) -> p j r", j=3)[:, :, ds(p, 1)])
                w0 = VEC0["w0_2"]
                V.tensor_copy(pc[:, 3:10], vec[:, w0:w0 + 56].rearrange("p (j r) -> p j r", j=7)[:, :, ds(p, 1)])
                V.tensor_copy(pc[:, 10:11], one_minus_ka[:, ds(p, 1)])
                dve.drain()
                for z, out_ in ((1, Kr), (0, Rr), (2, vT)):
                    dve.wait_ge(evac[z], p + (fill("rkv", z) + 1))
                    last = shifted(zsh[z], pc[:, z:z + 1], out_[:, :])
                    if z == 2:
                        last.then_inc(sem("rk.v"), 1)
                    dve.drain()
                    if z == 1:
                        V.tensor_scalar(kk[:, :], Kr[:, :], pc[:, 5:6], None, ALU.mult).then_inc(sem("rk.kk"), 1)
                dve.wait_ge(sem("rk.sig"), p + 1)
                V.tensor_scalar(lwd[:, :], lwd[:, :], -float(np.exp(-0.5)), None, ALU.mult)
                dve.drain()
                for c in range(4):
                    cs = slice(c * P, (c + 1) * P)
                    V.tensor_tensor_scan(cc[:, cs], ones[:, :], lwd[:, cs], 0.0, ALU.mult, ALU.add)
                dve.drain()
                c4 = cc[:, :].rearrange("p (c t) -> p c t", c=4)
                V.tensor_copy(mid[:, :], cc[:, CH - 1:S:P])
                dve.drain()
                V.tensor_tensor(c4, c4, mid[:, :].unsqueeze(2).to_broadcast([P, 4, P]), ALU.subtract)
                dve.drain()
                V.tensor_tensor(fade[par][:, 0:3], cc[:, P - 1:3 * P:P], mid[:, 1:4], ALU.add)
                V.tensor_tensor(lwd[:, :], cc[:, :], lwd[:, :], ALU.subtract).then_inc(sem("rk.lp"), 1)
                dve.wait_ge(sem("rk.nr"), p + 1)
                V.tensor_scalar(tile(sq, 1), tile(sq, 1), 1e-12, None, ALU.max)
                dve.drain()
                V.reciprocal(tile(sq, 1), tile(sq, 1))
                dve.drain()
                V.tensor_tensor(kk[:, :], kk[:, :], tile(sq, 1), ALU.mult)
                dve.drain()
                dve.wait_ge(sem("rk.ex"), p + 1)
                V.scalar_tensor_tensor(aT[par][:, :], kk[:, :], -1.0, lwd[:, :], ALU.mult, ALU.mult)
                V.tensor_tensor(bT[:, :], kk[:, :], aa[:, :], ALU.mult)
                dve.drain()
                V.tensor_tensor(bT[:, :], bT[:, :], cc[:, :], ALU.mult).then_inc(sem("rk.ab"), 1)

            def keys_and_bonus(p, par):
                pc = pcol[par]
                V.tensor_scalar(aa[:, :], aa[:, :], pc[:, 6:7], pc[:, 10:11], ALU.mult, ALU.add)
                dve.drain()
                V.tensor_tensor(Kr[:, :], Kr[:, :], aa[:, :], ALU.mult)
                dve.drain()
                V.scalar_tensor_tensor(kkT[:, :], Kr[:, :], SCAN_SCALE, cc[:, :], ALU.mult, ALU.mult)
                V.scalar_tensor_tensor(rT[par][:, :], Rr[:, :], SCAN_SCALE, epos[:, :], ALU.mult, ALU.mult)\
                    .then_inc(sem("rk.kr"), 1)
                dve.drain()
                V.scalar_tensor_tensor(Rr[:, :], Kr[:, :], pc[:, 7:8], Rr[:, :], ALU.mult, ALU.mult)\
                    .then_inc(sem("rk.bon"), 1)
                dve.wait_ge(sem("rk.bs"), p + 1)
                V.tensor_tensor(bonus[par][:, :], bank[2][:, :], vT[:, :], ALU.mult).then_inc(sem("rk.bonus"), 1)
                dve.drain()

            def finished(p, par, part):
                if part == 0:
                    dve.wait_ge(sem("gn.s"), p + 1)
                    V.reciprocal(bN[par][:, :], bN[par][:, :])
                elif part == 1:
                    V.scalar_tensor_tensor(aT[par][:, :], rT[par][:, :], pcol[par][:, 8:9], bN[par][:, :],
                                           ALU.mult, ALU.mult)
                elif part == 2:
                    V.scalar_tensor_tensor(aT[par][:, :], aT[par][:, :], pcol[par][:, 9:10], bonus[par][:, :],
                                           ALU.add, ALU.add)
                else:
                    dve.wait_ge(sem("rk.g"), p + 2)
                    V.tensor_tensor(dtile(yr, p), aT[par][:, :], bank[3][:, :], ALU.mult).then_inc(sem("rk.y"), 1)

            def pair(p, par, follows, more):
                for q, (h, left, right) in enumerate(gram_list()):
                    dve.wait_ge(sem("rk.gram"), p * 10 + q + 1)
                    x = bank[4 + q % 4][:, :]
                    if (left, right) == ("b", "a"):
                        last = masked(IN4[h], x, up16)
                    elif (left, right) == ("a", "b"):
                        masked(IA[h], x, lower1)
                        last = masked(IA4[h], x, low16)
                    elif right == "a":
                        last = masked(Gak[h], x, upper1)
                    else:
                        last = masked(Gqb[h] if left == "b" else Gqk[h], x, upper0)
                    last.then_inc(sem("rk.ge"), 1)
                    if follows and q % 2 == 1 and q < 8:
                        finished(p - 1, 1 - par, q // 2)
                        dve.drain()
                dve.drain()
                for h in range(2):
                    V.tensor_tensor(IU[h].rearrange("p (c t) -> p c t", c=4),
                                    IN4[h][:, :].rearrange("p (c t) -> p c t", c=4),
                                    ident[:, :].unsqueeze(1).to_broadcast([P, 4, P]), ALU.add)\
                        .then_inc(sem(f"inv{h}.dve"), 1)
                for k, step in enumerate(INVERSE):
                    for h in range(2):
                        waited = False
                        for which, (_, _, by, to) in enumerate(step["mm"]):
                            if by != "dve":
                                continue
                            if not waited:
                                dve.drain()
                                dve.wait_ge(sem(f"inv{h}.pe"), p * len(INVERSE) + k + 1)
                                waited = True
                            x = bank[4 + 2 * h + which][:, :]
                            if to == "A2":
                                last = V.tensor_copy(IE[h][:, :], x)
                            else:
                                dst = IU[h] if to == "+U" else IW[h]
                                last = V.tensor_tensor(dst, x, dst, ALU.add)
                            last.then_inc(sem(f"inv{h}.dve"), 1)
                        if "E" in step:
                            masked(IE[h], IA[h][:, :], step_mask[step["E"]]).then_inc(sem(f"inv{h}.dve"), 1)
                if more:
                    decayed_keys(p + 1, 1 - par)
                dve.wait_ge(sem("gn.m"), p + 1)
                V.scalar_tensor_tensor(rT[par][:, :], bank[4][:, :], -1.0 / 64, aT[par][:, :], ALU.mult, ALU.add)\
                    .then_inc(sem("gn.c"), 1)
                if more:
                    keys_and_bonus(p + 1, 1 - par)

            decayed_keys(0, 0)
            keys_and_bonus(0, 0)
            pair(0, 0, False, True)
            with dve.Fori(0, (PAIRS - 2) // 2) as j:
                pair(j * 2 + 1, 1, True, True)
                pair(j * 2 + 2, 0, True, True)
            pair(PAIRS - 1, 1, True, False)
            for part in range(4):
                dve.drain()
                finished(PAIRS - 1, 1, part)
            dve.drain()

            for k in range(12):
                src, hi, lo = (tile(at, k), tile(atH, k), tile(atL, k)) if k < 4 else \
                    (tile(yr, k - 4), tile(rH, k - 4), tile(rL, k - 4))
                dve.wait_ge(sem("mx.hi"), k + 1)
                V.tensor_tensor(lo, src, f32(hi), ALU.subtract).then_inc(sem("mx.lo"), 1)
            dve.drain()
            with dve.Fori(0, 4) as i:
                s0 = STRIP0["mix"] + i * 4
                for half in range(2):
                    dve.wait_ge(evac[half], fill("mix", half) + i * 2 + 1)
                    product_ready(s0 + 2, half)
                    V.tensor_tensor(tile(sq, half), bank[half][:, :], tile(sq, half), ALU.mult).then_inc(evac[half], 1)
                for half in range(2):
                    b = 2 + half
                    dve.wait_ge(evac[b], fill("mix", b) + i * 2 + 1)
                    product_ready(s0 + 3, half)
                    V.tensor_tensor(tile(hf, half), bank[b][:, :], tile(hf, half), ALU.mult).then_inc(evac[b], 1)
                    dve.drain()
                    V.tensor_tensor(tile(sq, half), tile(sq, half), tile(hf, half), ALU.add)
                    dve.drain()
                    split(dtile(mixH, i * 2 + half), dtile(mixL, i * 2 + half), tile(sq, half))\
                        .then_inc(sem("mx.lo2"), 1)

            with dve.Fori(0, 2) as i:
                for j in range(2):
                    for half in range(2):
                        product_ready(STRIP0["wo"] + i * 2 + j, half)
                        b, t = j * 2 + half, i * 4 + (j * 2 + half)
                        V.scalar_tensor_tensor(dtile(xT, t), bank[b][:, :], ada[:, ds(t + 2 * DT, 1)], dtile(xT, t),
                                               ALU.mult, ALU.add).then_inc(evac[b], 1)

            dve.drain()
            dve_norm(dve, "n_2", xt, [gain2[:, d:d + 1] for d in range(DT)], h_out,
                     [ada[:, 3 * DT + d:3 * DT + d + 1] for d in range(DT)])
            for b in range(2):
                last = V.memset(cpad[b][:, 0:2], 0.0)
            last.then_inc(sem("up.zero"), 1)
            dve.drain()
            cw, cb = VEC0["conv_w_2"], VEC0["conv_b_2"]
            with dve.Fori(0, 11) as i:
                for t in range(4):
                    n = i * 2 + (FT if t >= 2 else 0) + t % 2
                    u, acc = cpad[t % 2], tile(sq if t < 2 else hf, t % 2)
                    wt = [vec[:, ds(n + (cw + 2 * FT * j), 1)] for j in range(3)]
                    dve.wait_ge(evac[t], fill("up", t) + i + 1)
                    V.tensor_scalar(acc, u[:, 0:S], wt[0], vec[:, ds(n + cb, 1)], ALU.mult, ALU.add)
                    dve.drain()
                    V.scalar_tensor_tensor(acc, u[:, 1:S + 1], wt[1], acc, ALU.mult, ALU.add)
                    dve.drain()
                    V.scalar_tensor_tensor(acc, u[:, 2:S + 2], wt[2], acc, ALU.mult, ALU.add)\
                        .then_inc(sem("up.conv"), 1)
                    if t >= 2:
                        j = t - 2
                        dve.drain()
                        dve.wait_ge(sem("up.silu"), i * 2 + j + 1)
                        V.tensor_tensor(acc, acc, tile(sq, j), ALU.mult)
                        dve.drain()
                        split(dtile(fH, i * 2 + j), dtile(fL, i * 2 + j), acc).then_inc(sem("up.lo"), 1)
                dve.drain()
            with dve.Fori(0, 2) as i:
                for nn in range(2):
                    for half in range(2):
                        product_ready(STRIP0["down"] + i * 6 + nn * 3 + 2, half)
                        b, t = nn * 2 + half, i * 4 + (nn * 2 + half)
                        V.scalar_tensor_tensor(dtile(xT, t), bank[b][:, :], ada[:, ds(t + 5 * DT, 1)], dtile(xT, t),
                                               ALU.mult, ALU.add).then_inc(evac[b], 1)
            dve.drain()
            dve_norm(dve, "n_out", xt, cols("norm_f_w_2", DT), None)


_INS = ["x", "positions", "pool_norm", "pool_w_in", "pool_w_group", "pool_scale", "pool_w_out", "mla_norm", "mla_w_in",
        "mla_q_norm", "mla_w_q_b", "mla_kv_norm", "mla_w_kv_b", "mla_w_out", "final_norm", "c_2", "w_ada_2", "b_ada_2",
        "norm1_w_2", "w_in_2", "b_gate_2", "mu_shift_2", "w0_2", "w2_2", "a0_2", "a2_2", "g2_2", "k_k_2", "k_a_2",
        "r_k_2", "lnx_w_2", "lnx_b_2", "w_att_out_2", "w_rwkv_out_2", "w_o_2", "norm2_w_2", "w_up_2", "conv_w_2",
        "conv_b_2", "w_down_2", "norm_f_w_2"]


def kernel(**inputs):
    import numpy as _np
    import concourse.bacc as _bacc
    from concourse import mybir as _mybir
    from concourse.bass_utils import run_bass_kernel_spmd as _run

    nc = _bacc.Bacc("TRN2", target_bir_lowering=False, num_devices=1)
    arrays = {name: _np.ascontiguousarray(inputs[name]) for name in _INS}
    freq = 1.0 / (_np.float32(ROPE_THETA) ** (_np.arange(0, ROPE, 2, dtype=_np.float32) / _np.float32(ROPE)))
    arrays["inv_freq"] = _np.tile(freq.astype(_np.float32), 4).reshape(P, 1)
    aps = {name: nc.dram_tensor(f"in_{name}", v.shape, _mybir.dt.from_np(v.dtype), kind="ExternalInput").ap()
           for name, v in arrays.items()}
    out = nc.dram_tensor("out", (1, S, D), F32, kind="ExternalOutput").ap()
    build(nc, aps, out)
    r = _run(nc, [{f"in_{name}": v for name, v in arrays.items()}], core_ids=[0])
    return r.results[0]["out"]
```

```python
from contextlib import ExitStack, nullcontext

import numpy as np

import concourse.bass as bass
from concourse import mybir

P = 128
S = 512
D = 1024
DT = D // P
EPS = 1e-6
POOL_WINDOWS = (2, 4, 8, 16)
PAD = 16
HEADS = 16
NOPE, ROPE, VD = 128, 64, 128
QK = NOPE + ROPE
Q_RANK, KV_RANK = 384, 256
ROPE_THETA = 10000.0
QK_SCALE = QK ** -0.5
ATT_GROUPS = 3
ATT_HEADS, ATT_DIM = 8, 64
ATT_WIDTH = ATT_HEADS * ATT_DIM
ATT_IN = ATT_GROUPS * 3 * ATT_WIDTH
CH = 64
PAIRS = D // P
RWKV_IN = 3 * D + 64 + 64 + 160
GATE0 = ATT_IN + RWKV_IN
GN_EPS = 64e-5
D_FF = 2816
FT = D_FF // P
DOWN_K = (8, 8, 6)
SCAN_SCALE = 2.0 ** -20
BIG = 1e30
ROUND = 1.5 * 2.0 ** 23
TWO_PI = (6.28125, 0.00193500518798828125, 3.0199159795074593e-07)
PI_IN = 3.14159250259399414

F32 = mybir.dt.float32
F32R = mybir.dt.float32r
BF16 = mybir.dt.bfloat16
I32 = mybir.dt.int32
ALU = mybir.AluOpType
ACT = mybir.ActivationFunctionType
AX = mybir.AxisListType
ds = bass.ds

VEC_ROWS = [("pool_norm", 8), ("pool_scale", 16), ("mla_norm", 8), ("mla_q_norm", 3), ("mla_kv_norm", 2),
            ("final_norm", 8), ("c_2", 8), ("b_ada_2", 48), ("norm1_w_2", 8), ("b_gate_2", 16),
            ("mu_shift_2", 27), ("w0_2", 8), ("a0_2", 8), ("k_k_2", 8), ("k_a_2", 8), ("r_k_2", 8),
            ("lnx_w_2", 8), ("lnx_b_2", 8), ("norm2_w_2", 8), ("conv_w_2", 132), ("conv_b_2", 44),
            ("norm_f_w_2", 8)]
VEC0 = {}
for _name, _rows in VEC_ROWS:
    VEC0[_name] = sum(r for n, r in VEC_ROWS[:len(VEC0)])
VEC_ALL = sum(r for _, r in VEC_ROWS)
VEC_TILES = -(-VEC_ALL // P)

STREAM = [("pool", 4, 6), ("pool_out", 2, 4), ("lat", 1, 4), ("mz", 4, 2), ("heads", 8, 2), ("mla_out", 2, 4),
          ("att", 9, 2), ("lora", 1, 2), ("rkv", PAIRS, 2), ("mix", 4, 4), ("wo", 2, 2), ("up", 11, 2),
          ("down", 2, 6)]
STRIP0 = {}
for _name, _n, _m in STREAM:
    STRIP0[_name] = sum(n * m for _, n, m in STREAM[:len(STRIP0)])
FILLS = {"pool": (12,) * 4, "pool_out": (2,) * 4, "lat": (2, 1, 2, 1), "mz": (4,) * 4, "heads": (16,) * 4,
         "mla_out": (2,) * 4, "att": (9,) * 4, "lora": (1, 0, 1, 1), "rkv": (8, 8, 8, 0), "mix": (8,) * 4,
         "wo": (2,) * 4, "up": (11,) * 4, "down": (2,) * 4}
FILL0 = {}
for _name, _n, _m in STREAM:
    FILL0[_name] = tuple(sum(FILLS[p][b] for p, _, _ in STREAM[:len(FILL0)]) for b in range(4))
ADA_W = 128
ADA_N = 6 * D // 8 // ADA_W
RAW_CREDIT = 4
SPLIT_CREDIT = 4


NORM_COUNTS = ("sq", "sum", "rms", "hf", "lo")
NORMS = [("n_pool", DT, 1, 1, DT, DT), ("n_mla", DT, 1, 1, DT, DT), ("n_q", 3, 1, 1, 3, 3), ("n_kv", 2, 1, 1, 2, 2),
         ("n_fin", 2 * DT, 2, 1, 0, 0), ("n_1", 0, 0, 1, DT, DT), ("n_2", DT, 1, 1, DT, DT), ("n_out", DT, 1, 1, DT, 0)]
NORM0 = {row[0]: {c: sum(r[1 + n] for r in NORMS[:k]) for n, c in enumerate(NORM_COUNTS)}
         for k, row in enumerate(NORMS)}


def loaded_value(ph, i, j, m):
    before = STRIP0[ph] // 2 + j // 2 + 1
    if ph == "rkv" and j == 0:
        return (i * 2 + (before + 1)) * 16
    if j % 2 == 0 and STRIP0[ph] > STRIP0["rkv"]:
        before += PAIRS
    return (i * (m // 2) + before) * 16


def split_value(s, half):
    return RAW_CREDIT + 2 * s + half + 1


def first_half(K):
    return (K + 1) // 2


def done_value(s, half):
    return SPLIT_CREDIT + 2 * s + half + 1


def att_units(g):
    units = []
    for h in range(ATT_HEADS):
        if g == 0:
            units += [(h, [(0, 0), (1, 0), (1, 1)]), (h, [(2, 1), (2, 2), (3, 2), (3, 3)])]
        else:
            units.append((h, [(b, b) for b in range(4)]))
    return units


def att_rows(blocks):
    rows = []
    for n, (qb, kb) in enumerate(blocks):
        if rows and rows[-1][0] == qb:
            rows[-1] = (qb, rows[-1][1], rows[-1][2] + 1, rows[-1][3])
        else:
            rows.append((qb, kb, 1, n * P))
    return rows


def gram_list():
    return [(h, l, r) for l, r in (("b", "a"), ("k", "a"), ("b", "r"), ("a", "b"), ("k", "r")) for h in range(2)]


INVERSE = [
    {"mm": [("DA", "D", "act", "N2", None), ("D", "DA", "dve", "A2", None)]},
    {"mm": [("A2", "N2", "act", "N4", None), ("N2", "A2", "act", "A4", None)]},
    {"mm": [("N4", "A4", "act", "A8", None), ("A2", "U", "dve", "+U", None)]},
    {"mm": [("A4", "U", "dve", "+U", None)], "E": 16},
    {"mm": [("A8", "U", "dve", "+U", None)]},
    {"mm": [("U", "I", "act", "W", None), ("E", "U", "act", "Z", None)]},
    {"mm": [("W", "Z", "dve", "+U", (16, 1)), ("Z", "W", "dve", "+W", (16, 0))], "E": 32},
    {"mm": [("E", "U", "act", "Z", None)]},
    {"mm": [("W", "Z", "dve", "+U", (32, 1)), ("Z", "W", "dve", "+W", (32, 0))], "E": 64},
    {"mm": [("E", "U", "act", "Z", (64, 1))]},
    {"mm": [("W", "Z", "dve", "+U", (64, 1))]},
]


def columns(x, part):
    if part is None:
        return x
    return x.rearrange("p (x two n) -> p x two n", two=2, n=part[0])[:, :, part[1], :]


INV_ACT = [sum(x[2] == "act" for st in INVERSE[:k] for x in st["mm"]) for k in range(len(INVERSE) + 1)]
INV_DVE = [1 + sum(x[2] == "dve" for st in INVERSE[:k] for x in st["mm"]) + sum("E" in st for st in INVERSE[:k])
           for k in range(len(INVERSE) + 1)]


def build(nc, a, out):
    with ExitStack() as ctx:
        def sb(name, shape, dt=F32, stack=None):
            return (stack or ctx).enter_context(nc.sbuf_tensor(name, shape, dt))

        sems = {}

        def sem(name):
            if name not in sems:
                sems[name] = ctx.enter_context(nc.semaphore(name))
            return sems[name]

        bank = [ctx.enter_context(nc.psum_tensor(f"bank{b}", [P, S], F32)) for b in range(8)]
        scratch = nc.dram_tensor("stat_scratch", [4, S * ATT_HEADS], F32, kind="Internal").ap()

        raw = [sb(f"raw{b}", [P, 2048]) for b in range(2)]
        whi = [sb(f"whi{b}", [P, 2048], F32R) for b in range(2)]
        wlo = [sb(f"wlo{b}", [P, 2048], F32R) for b in range(2)]
        xT = sb("xT", [P, DT * S])
        hbuf = sb("hbuf", [P, 2 * DT * S], F32R)
        sq = sb("sq", [P, 2 * S])
        hf = sb("hf", [P, 2 * S])
        inv = sb("inv", [P, S])
        vec = sb("vec", [P, VEC_ALL])
        ident = sb("ident", [P, P])
        ones = sb("ones", [P, P])
        same = {n: sb(f"same{n}", [P, P]) for n in (16, 32, 64)}
        upper1 = sb("upper1", [P, P])
        upper0 = sb("upper0", [P, P])
        lower1 = sb("lower1", [P, P])
        up16 = sb("up16", [P, P])
        low16 = sb("low16", [P, P])
        step_mask = {n: sb(f"step{n}", [P, P]) for n in (16, 32, 64)}
        ident_b = sb("ident_b", [P, P], BF16)
        neg_band = sb("neg_band", [P, 2 * P], BF16)
        neg_dil = sb("neg_dil", [P, P], BF16)
        cinv = sb("cinv", [P, 4 * PAD])
        ada, gain1, gain2 = cinv[:, 0:48], cinv[:, 48:56], cinv[:, 56:64]
        spare = sb("spare", [P, 1])
        eps_c = sb("eps_c", [P, 1])
        rms4 = sb("rms4", [P, 4])
        ms4 = sb("ms4", [P, 4])
        gneps_c = sb("gneps_c", [P, 1])
        one_minus_mu = sb("one_minus_mu", [P, 27])
        one_minus_ka = sb("one_minus_ka", [P, DT])
        neg_causal = neg_band[:, P:2 * P]

        def tile(buf, i):
            return buf[:, i * S:(i + 1) * S]

        def dtile(buf, i):
            return buf[:, ds(i * S, S)]

        def col(name, i):
            return vec[:, VEC0[name] + i:VEC0[name] + i + 1]

        def dcol(name, i):
            return vec[:, ds(VEC0[name] + i, 1)]

        with ExitStack() as st:
            vecrow = sb("vecrow", [P, VEC_TILES * P], F32, st)
            xin = sb("xin", [P, 4 * D], F32, st)
            res4 = sb("res4", [P, 4], F32, st)
            tmp_mask = sb("tmp_mask", [P, P], F32, st)
        with ExitStack() as st:
            y1H = sb("y1H", [P, 16 * S], F32R, st)
            y1L = sb("y1L", [P, 16 * S], F32R, st)
            poolH = sb("poolH", [P, 4 * S], F32R, st)
            poolL = sb("poolL", [P, 4 * S], F32R, st)
            zp = sb("zp", [P, 4 * S], F32, st)
            upad = [sb(f"upad{b}", [P, PAD + S], F32, st) for b in range(2)]
        with ExitStack() as st:
            zm = sb("zm", [P, 16 * S], F32, st)
            latH = sb("latH", [P, 5 * S], F32R, st)
            latL = sb("latL", [P, 5 * S], F32R, st)
            krope = sb("krope", [P, S], F32, st)
            cosT = sb("cosT", [P, S], F32, st)
            sinT = sb("sinT", [P, S], F32, st)
            with ExitStack() as st2:
                lat = sb("lat", [P, 5 * S], F32, st2)
                posi = sb("posi", [P, S], I32, st2)
                ang = sb("ang", [P, 3 * S], F32, st2)
                invf = sb("invf", [P, 1], F32, st2)
            with ExitStack() as st2:
                kT = sb("kT", [P, 2 * S], F32, st2)
                vN = hf
                qrope = inv
                qT = sb("qT", [P, 2 * S], F32, st2)
                prob = [sb(f"prob{b}", [P, S], F32, st2) for b in range(3)]
                probT = sb("probT", [P, 4 * S], F32, st2)
                adaw = [sb(f"adaw{b}", [P, DT * ADA_W], F32, st2) for b in range(2)]
                adaw.append(raw[1][:, DT * ADA_W:2 * DT * ADA_W])
                adaacc = sb("adaacc", [P, 6 * P], F32, st2)
                stat = sb("stat", [P, 9], F32, st2)
        with ExitStack() as st:
            y2L = sb("y2L", [P, 16 * S], F32R, st)
        y2H = hbuf
        with ExitStack() as st:
            at = sb("at", [P, 4 * S], F32, st)
            with ExitStack() as st2:
                aq = sb("aq", [P, 4 * S], F32, st2)
                ak = sb("ak", [P, 4 * S], F32, st2)
                av = sb("av", [P, 4 * ATT_HEADS * P], F32, st2)
                num = [sb(f"num{g}", [P, 4 * S], F32, st2) for g in range(3)]
                ap_ = [sb(f"ap{b}", [P, S], F32, st2) for b in range(2)]
                apT = [sb(f"apT{b}", [P, S], F32, st2) for b in range(2)]
                spread = [ap_[0], ap_[1], apT[0]]
                nmax = sb("nmax", [P, 3 * 32], F32, st2)
                den = sb("den", [P, 3 * 32], F32, st2)
                stq = sb("stq", [P, 2 * 32], F32, st2)
                fac = sb("fac", [P, 3 * 32], F32, st2)
                fac0 = sb("fac0", [P, 32], F32, st2)
                zden = sb("zden", [P, 32], F32, st2)
            with ExitStack() as st2:
                yr = sb("yr", [P, PAIRS * S], F32, st2)
                with ExitStack() as st3:
                    wlow = sb("wlow", [P, S], F32, st3)
                    glow = sb("glow", [P, 2 * S], F32, st3)
                    lw2 = sb("lw2", [P, P], F32, st3)
                    lg2 = sb("lg2", [P, 2 * P], F32, st3)
                    mid = sb("mid", [P, 4], F32, st3)
                    pcol = [sb(f"pcol{b}", [P, 16], F32, st3) for b in range(2)]
                    aT = [sb(f"aT{b}", [P, S], F32, st3) for b in range(2)]
                    rT = [sb(f"rT{b}", [P, S], F32, st3) for b in range(2)]
                    bonus = [sb(f"bonus{b}", [P, S], F32, st3) for b in range(2)]
                    vpad = [sb(f"vpad{b}", [P, 4 * 256], F32, st3) for b in range(2)]
                    bN = [sb(f"bN{b}", [P, S], F32, st3) for b in range(2)]
                    kN = [sb(f"kN{b}", [P, S], F32, st3) for b in range(2)]
                    fade = [sb(f"fade{b}", [P, 4], F32, st3) for b in range(2)]
                    bT = sb("bT", [P, S], F32, st3)
                    kkT = sb("kkT", [P, S], F32, st3)
                    vT = sb("vT", [P, S], F32, st3)
                    Gak = [sb(f"Gak{h}", [P, S], F32, st3) for h in range(2)]
                    Gqb = [sb(f"Gqb{h}", [P, S], F32, st3) for h in range(2)]
                    Gqk = [sb(f"Gqk{h}", [P, S], F32, st3) for h in range(2)]
                    sapad = sb("sapad", [P, 256], F32, st3)
                    rhs = sb("rhs", [P, P], F32, st3)
                    state = sb("state", [P, P], F32, st3)
                    with ExitStack() as st4:
                        epos = sb("epos", [P, S], F32, st4)
                        kk = sb("kk", [P, S], F32, st4)
                        cc = sb("cc", [P, S], F32, st4)
                        Rr = sb("Rr", [P, S], F32, st4)
                        Kr = sb("Kr", [P, S], F32, st4)
                        lwd = sb("lwd", [P, S], F32, st4)
                        aa = inv
                    with ExitStack() as st4:
                        IA, IN4, IA4 = [[sb(f"{n}_{h}", [P, S], F32, st4) for h in range(2)]
                                        for n in ("IA", "IN4", "IA4")]
                    IA8, IE = [bT, kkT], [vT, inv]
                    IW = [tile(sq, h) for h in range(2)]
                    IU = [tile(hf, h) for h in range(2)]
        with ExitStack() as st:
            sb("under_at_and_yr", [P, (4 + PAIRS) * S], F32, st)
            atH = sb("atH", [P, 4 * S], F32R, st)
            atL = sb("atL", [P, 4 * S], F32R, st)
            rH = sb("rH", [P, PAIRS * S], F32R, st)
            rL = sb("rL", [P, PAIRS * S], F32R, st)
            mixL = sb("mixL", [P, DT * S], F32R, st)
        with ExitStack() as st:
            mixH = sb("mixH", [P, DT * S], F32R, st)
        with ExitStack() as st:
            fH = sb("fH", [P, FT * S], F32R, st)
            fL = sb("fL", [P, FT * S], F32R, st)
            cpad = [sb(f"cpad{b}", [P, 2 + S], F32, st) for b in range(2)]
        with ExitStack() as st:
            yout = [sb(f"yout{b}", [P, D], F32, st) for b in range(2)]
        V, A, G, M = nc.vector, nc.scalar, nc.gpsimd, nc.tensor
        products_done, raw_split = sem("products_done"), sem("raw_split")
        raw_loaded = [sem(f"raw_loaded{b}") for b in range(2)]
        evac = [sem(f"bank_taken{b}") for b in range(4)]
        hH = [hbuf[:, d * S:(d + 1) * S] for d in range(DT)]
        hL = [hbuf[:, (DT + d) * S:(DT + d + 1) * S] for d in range(DT)]
        f32 = lambda r: r.bitcast(F32)
        fill = lambda ph, b: FILL0[ph][b]

        def out_tile_taken(ph, t):
            b = (t // 2 % 2) * 2 + t % 2
            return evac[b], fill(ph, b) + t // 4 + 1

        w_in1 = a["pool_w_in"].rearrange("l (k p) n -> p (l k) n", p=P)
        w_grp = a["pool_w_group"].rearrange("l g (k p) n -> p (l g k) n", p=P)
        w_out1 = a["pool_w_out"].rearrange("l (k p) n -> p (l k) n", p=P)
        w_mla = a["mla_w_in"].rearrange("l (k p) n -> p (l k) n", p=P)
        w_q = a["mla_w_q_b"].rearrange("l (k p) n -> p (l k) n", p=P)
        w_kv = a["mla_w_kv_b"].rearrange("l (k p) n -> p (l k) n", p=P)
        w_out2 = a["mla_w_out"].rearrange("l (k p) n -> p (l k) n", p=P)
        w_ada = a["w_ada_2"].rearrange("l (k p) n -> p (l k) n", p=P)
        w_in2 = a["w_in_2"].rearrange("l (k p) n -> p (l k) n", p=P)
        w_ao = a["w_att_out_2"].rearrange("l (k p) n -> p (l k) n", p=P)
        w_ro = a["w_rwkv_out_2"].rearrange("l (k p) n -> p (l k) n", p=P)
        w_wo = a["w_o_2"].rearrange("l (k p) n -> p (l k) n", p=P)
        w_up = a["w_up_2"].rearrange("l (k p) n -> p (l k) n", p=P)
        w_dn = a["w_down_2"].rearrange("l (k p) n -> p (l k) n", p=P)
        LAT = ((0, 256), (256, 256), (512, 128), (640, 64))
        MZ0 = Q_RANK + KV_RANK + ROPE
        LORA0 = ATT_IN + 3 * D
        LORA = ((LORA0, 128), (LORA0 + 128, 160))

        def strip_source(ph, i, j):
            if ph == "pool":
                if j < 4:
                    return w_in1[:, :, ds(i * 512 + (j // 2) * 2 * D + (j % 2) * 256, 256)], 8, 256
                return w_grp[:, ds(i * 4, 4), (j - 4) * 256:(j - 3) * 256], 4, 256
            if ph in ("pool_out", "mla_out"):
                w = w_out1 if ph == "pool_out" else w_out2
                return w[:, (j % 2) * 8:(j % 2) * 8 + 8, ds(i * 512 + (j // 2) * 256, 256)], 8, 256
            if ph == "lat":
                return w_mla[:, :, LAT[j][0]:LAT[j][0] + LAT[j][1]], 8, LAT[j][1]
            if ph == "mz":
                return w_mla[:, :, ds(MZ0 + i * 512 + j * 256, 256)], 8, 256
            if ph == "heads":
                if j == 0:
                    return w_q[:, :, ds(i * 2 * QK, 2 * QK)], 3, 2 * QK
                return w_kv[:, :, ds(i * 512, 512)], 2, 512
            if ph == "att":
                return w_in2[:, :, ds(i * 512 + j * 256, 256)], 8, 256
            if ph == "lora":
                return w_in2[:, :, LORA[j][0]:LORA[j][0] + LORA[j][1]], 8, LORA[j][1]
            if ph == "rkv":
                if j == 0:
                    return None, 8, 256
                return w_in2[:, :, ds(i * P + (ATT_IN + 2 * D), P)], 8, P
            if ph == "mix":
                if j < 2:
                    return w_in2[:, :, ds(i * 256 + (GATE0 + j * D), 256)], 8, 256
                return (w_ao if j == 2 else w_ro)[:, :, ds(i * 256, 256)], (4 if j == 2 else 8), 256
            if ph == "wo":
                return w_wo[:, :, ds(i * 512 + j * 256, 256)], 8, 256
            if ph == "up":
                return w_up[:, :, ds(i * 256 + j * D_FF, 256)], 8, 256
            k0 = sum(DOWN_K[:j % 3])
            return w_dn[:, k0:k0 + DOWN_K[j % 3], ds(i * 512 + (j // 3) * 256, 256)], DOWN_K[j % 3], 256

        vec_src = {"conv_w_2": "l j (r c) -> (l j r) c", "r_k_2": "l (r h) e -> (l r) (h e)",
                   "final_norm": "(r c) -> r c", "norm_f_w_2": "(r c) -> r c"}
        vec_dmas = []
        for name, rows in VEC_ROWS:
            full = a[name]
            if name == "mu_shift_2":
                vec_dmas.append((VEC0[name] + 26, 1, 32, full[0:1, 26 * P:RWKV_IN]))
                full, rows = full[:, 0:26 * P], 26
            view = full.rearrange(vec_src[name], h=2) if name == "r_k_2" else \
                full.rearrange(vec_src.get(name, "l (r c) -> (l r) c"), c=P)
            r = 0
            while r < rows:
                n = min(rows - r, P - (VEC0[name] + r) % P)
                vec_dmas.append((VEC0[name] + r, n, P, view[r:r + n, :]))
                r += n
        VEC_DMAS = len(vec_dmas)

        block = ctx.enter_context(nc.Block())

        def phase_loop(eng, n):
            return eng.Fori(0, n) if n > 1 else nullcontext(0)

        @block.sync
        def _(sp):
            sp.dma_start(xin[:, :].rearrange("p (t d) -> p t d", t=4),
                         a["x"].rearrange("b (t p) d -> p (b t) d", p=P)).then_inc(sem("x_loaded"), 16)
            for ph, n, m in STREAM:
                if ph == "heads":
                    sp.wait_ge(sem("norm.lo"), NORM0["n_kv"]["lo"] + 2)
                    sp.wait_ge(sem("krope"), 1)
                if ph == "mla_out":
                    sp.wait_ge(sem("ada.acc"), 8 * ADA_N + 3)

                def load_strips(i):
                    for j in range(m):
                        s = STRIP0[ph] + i * m + j
                        par = j % 2
                        src, K, W = strip_source(ph, i, j)
                        sp.wait_ge(raw_split, 2 * s + 2)
                        dst = raw[par][:, 0:K * W].rearrange("p (k n) -> p k n", k=K)
                        if ph == "rkv" and j == 0:
                            for t in range(2):
                                sp.dma_start(dst[:, :, t * P:(t + 1) * P],
                                             w_in2[:, :, ds(i * P + (ATT_IN + t * D), P)])\
                                    .then_inc(raw_loaded[par], 16)
                            continue
                        sp.dma_start(dst, src).then_inc(raw_loaded[par], 16)

                if ph == "mix":
                    for i in range(n):
                        load_strips(i)
                    continue
                with phase_loop(sp, n) as i:
                    load_strips(i)
                    if ph == "heads":
                        for q in range(ADA_N):
                            sp.wait_ge(sem("ada.acc"), i * ADA_N + q + 1)
                            sp.dma_start(adaw[q % 3][:, :].rearrange("p (k n) -> p k n", k=DT),
                                         w_ada[:, :, ds(i * 768 + q * ADA_W, ADA_W)])\
                                .then_inc(sem(f"ada.ld{q % 3}"), 16)
            for t in range(4):
                sp.wait_ge(sem("fin.out"), 2 * t + 2)
                sp.dma_start(out[0, t * P:(t + 1) * P, :], yout[t % 2][:, :]).then_inc(sem(f"out_stored{t % 2}"), 16)
            for b in range(2):
                sp.wait_ge(sem(f"out_stored{b}"), 32)

        @block.gpsimd
        def _(pool):
            G.memset(vecrow[:, :], 0.0).then_inc(sem("vecrow_zero"), 1)
            G.memset(ones[:, :], 1.0)
            G.memset(ident[:, :], 0.0)
            G.memset(upad[0][:, 0:PAD], 0.0)
            G.memset(upad[1][:, 0:PAD], 0.0)
            G.memset(eps_c[:, :], EPS)
            G.memset(gneps_c[:, :], GN_EPS)
            for n in (16, 32, 64):
                G.memset(same[n][:, :], 1.0)
            G.iota(cinv[:, :].rearrange("p (g t) -> p g t", g=4), [[0, 4], [1, PAD]], base=1, channel_multiplier=0,
                   allow_small_or_imprecise_dtypes=True)
            pool.drain()
            G.affine_select(out=ident[:, :], in_=ident[:, :], compare_op=ALU.not_equal, fill=1.0, base=0,
                            pattern=[[-1, P]], channel_multiplier=1)
            G.affine_select(out=upper0[:, :], in_=ones[:, :], compare_op=ALU.is_ge, fill=0.0, base=0,
                            pattern=[[1, P]], channel_multiplier=-1)
            G.affine_select(out=upper1[:, :], in_=ones[:, :], compare_op=ALU.is_gt, fill=0.0, base=0,
                            pattern=[[1, P]], channel_multiplier=-1)
            G.affine_select(out=lower1[:, :], in_=ones[:, :], compare_op=ALU.is_gt, fill=0.0, base=0,
                            pattern=[[-1, P]], channel_multiplier=1)
            for n in (16, 32, 64):
                v = same[n][:, :].rearrange("p (b c) -> p b c", c=n)
                G.affine_select(out=v, in_=v, compare_op=ALU.is_ge, fill=0.0, base=0,
                                pattern=[[-n, P // n], [0, n]], channel_multiplier=1)
                pool.drain()
                G.affine_select(out=v, in_=v, compare_op=ALU.is_ge, fill=0.0, base=n - 1,
                                pattern=[[n, P // n], [0, n]], channel_multiplier=-1)
            pool.drain()
            G.memset(res4[0:1, 0:1], 0.0).then_inc(raw_split, RAW_CREDIT)
            pool.drain()
            G.memset(res4[0:1, 0:1], 0.0).then_inc(products_done, SPLIT_CREDIT)
            for name, credit in (("ada.acc", 3), ("ada.col", 1), ("rk.g", 1), ("rk.y", 1), ("mx.lo2", 1),
                                 ("up.conv", 2)):
                pool.drain()
                G.memset(res4[0:1, 0:1], 0.0).then_inc(sem(name), credit)
            pool.drain()
            G.memset(res4[0:1, 0:1], 0.0).then_inc(sem("consts"), 1)
            def take_wait():
                G.tensor_tensor(spare[0:1, 0:1], ones[0:1, 0:1], ones[0:1, 0:1], ALU.mult)

            for ph, n, m in STREAM:
                with phase_loop(pool, n) as i:
                    for j in range(m):
                        s = STRIP0[ph] + i * m + j
                        par = j % 2
                        _, K, W = strip_source(ph, i, j)
                        pool.wait_ge(raw_loaded[par], loaded_value(ph, i, j, m))
                        pool.wait_ge(products_done, done_value(s, 1) - 4)
                        if n > 1:
                            take_wait()
                        r, h, l = raw[par][:, 0:K * W], whi[par][:, 0:K * W], wlo[par][:, 0:K * W]
                        if ph == "heads" and j == 0:
                            nopes = K * 2 * NOPE
                            r = r.rearrange("p (x c) -> p x c", c=QK)
                            parts = [(r[:, :, lo:hi], *[w[:, o:o + 2 * K * (hi - lo)]
                                                        .rearrange("p (x c) -> p x c", c=hi - lo) for w in (h, l)])
                                     for lo, hi, o in ((0, NOPE, 0), (NOPE, QK, nopes))]
                        else:
                            mid = first_half(K) * W
                            parts = [[x[:, c] for x in (r, h, l)] for c in (slice(0, mid), slice(mid, K * W))]
                        for r_, h_, l_ in parts:
                            G.tensor_scalar(h_, r_, 1.0, 1.0, ALU.mult, ALU.mult)
                            pool.drain()
                            G.tensor_tensor(l_, r_, f32(h_), ALU.subtract).then_inc(raw_split, 1)
                    if ph == "heads":
                        for q in range(ADA_N):
                            if q == 0:
                                pool.wait_ge(sem("ada.col"), i + 1)
                            pool.wait_ge(sem("ada.c"), i * ADA_N + q + 1)
                            take_wait()
                            buf = adaw[q % 3]
                            for half in (4 * ADA_W, 2 * ADA_W, ADA_W):
                                pool.drain()
                                to = buf[:, 0:half] if half > ADA_W else adaacc[:, q * ADA_W:(q + 1) * ADA_W]
                                add = G.tensor_tensor(to, buf[:, 0:half], buf[:, half:2 * half], ALU.add)
                            add.then_inc(sem("ada.acc"), 1)
                            pool.drain()

        def act_squares(act, name, srcs, src_ready, gains=None):
            each = 2 if gains else 1
            for d, x in enumerate(srcs):
                src_ready(act, d)
                base = NORM0[name]["sq"] + each * d
                for n in range(each):
                    b = n if gains else d % 2
                    if d >= (1 if gains else 2):
                        act.wait_ge(sem("norm.acc"), base + n - 1)
                    A.activation(tile(sq, b), x, ACT.Square, scale=gains[d] if n else 1.0)\
                        .then_inc(sem("norm.sq"), 1)

        def act_rms(act, name, width, src=None):
            if name != "n_1":
                act.wait_ge(sem("norm.sum"), NORM0[name]["sum"] + 1)
            A.activation(rms4[:, :], bank[7][:, 0:4] if src is None else src, ACT.Sqrt, scale=1.0 / width, bias=eps_c[:, 0:1]).then_inc(sem("norm.rms"), 1)

        def act_upper(act, name, outs, shifts=None):
            for d, (hi, _) in enumerate(outs):
                act.wait_ge(sem("norm.hf"), NORM0[name]["hf"] + d + 1)
                if shifts is None:
                    cp = A.copy(hi, tile(hf, d % 2))
                else:
                    cp = A.activation(hi, tile(hf, d % 2), ACT.Identity, bias=shifts[d])
                cp.then_inc(sem("norm.hi"), 1)

        def act_norm(act, name, srcs, width, src_ready, outs, shifts=None):
            act_squares(act, name, srcs, src_ready)
            act_rms(act, name, width)
            act_upper(act, name, outs, shifts)

        def pe_norm(pe, name, n):
            pe.wait_ge(sem("norm.acc"), NORM0[name]["sq"] + n)
            token_sums(7, inv)
            if name != "n_fin":
                pe_factors(pe, name)

        def token_sums(b, x):
            for t in range(4):
                mm = M.matmul(bank[b][:, t:t + 1], x[:, t * P:(t + 1) * P], ones[:, 0:1], start=True, stop=True)
            mm.then_inc(sem("norm.sum"), 1)

        def pe_factors(pe, name):
            pe.wait_ge(sem("norm.diag"), norm_number(name) + 1)
            M.matmul(factor_bank(name)[:, :], ones[:, :], inv[:, :], start=True, stop=True)\
                .then_inc(sem("norm.factor"), 1)

        def norm_number(name):
            return [row[0] for row in NORMS].index(name)

        def factor_bank(name):
            return bank[6 if name == "n_1" else 7]

        def add_squares(dve, name, d, which=None):
            dve.wait_ge(sem("norm.sq"), NORM0[name]["sq"] + (d if which is None else 2 * d + which) + 1)
            acc, x = (tile(hf, 0) if which else inv[:, :]), tile(sq, d % 2 if which is None else which)
            dve.drain()
            add = V.tensor_tensor(acc, acc, x, ALU.add) if d else V.tensor_copy(acc, x)
            add.then_inc(sem("norm.acc"), 1)

        def dve_inverse(dve, name):
            dve.wait_ge(sem("norm.rms"), NORM0[name]["rms"] + 1)
            V.reciprocal(rms4[:, :], rms4[:, :])
            dve.drain()
            for t in range(4):
                diag = V.tensor_scalar(inv[:, t * P:(t + 1) * P], ident[:, :], rms4[:, t:t + 1], None, ALU.mult)
            diag.then_inc(sem("norm.diag"), 1)

        def over_rms(dve, name):
            dve.wait_ge(sem("norm.factor"), norm_number(name) + 1)

        def dve_split(dve, name, srcs, gains, outs, shifts=None):
            n = len(srcs)
            over_rms(dve, name)

            def normed(d):
                if d >= 2:
                    dve.wait_ge(sem("norm.hi"), NORM0[name]["lo"] + d - 1)
                V.scalar_tensor_tensor(tile(hf, d % 2), srcs[d], gains[d], factor_bank(name)[:, :], ALU.mult, ALU.mult)\
                    .then_inc(sem("norm.hf"), 1)

            normed(0)
            for d in range(n):
                if d + 1 < n:
                    normed(d + 1)
                dve.drain()
                dve.wait_ge(sem("norm.hi"), NORM0[name]["lo"] + d + 1)
                x, (hi, lo) = tile(hf, d % 2), outs[d]
                low = V.tensor_tensor(lo, x, f32(hi), ALU.subtract) if shifts is None else \
                    V.scalar_tensor_tensor(lo, x, shifts[d], f32(hi), ALU.add, ALU.subtract)
                low.then_inc(sem("norm.lo"), 1)
                dve.drain()

        def dve_norm(dve, name, srcs, gains, outs, shifts=None, added=False):
            if not added:
                for d in range(len(srcs)):
                    add_squares(dve, name, d)
            dve_inverse(dve, name)
            dve_split(dve, name, srcs, gains, outs, shifts)

        xt = [tile(xT, d) for d in range(DT)]
        h_out = [(hH[d], hL[d]) for d in range(DT)]
        lat_t = [tile(lat, d) for d in range(5)]
        lat_out = [(tile(latH, d), tile(latL, d)) for d in range(5)]
        cols = lambda name, n: [col(name, d) for d in range(n)]

        @block.tensor
        def _(pe):
            def strip_ready(s, half):
                pe.wait_ge(raw_split, split_value(s, half))

            def product(dst, slot, W, c0, cw, acts, first=True, last=True, half_at=None, strip=None):
                n = len(acts)
                for k in range(n):
                    if strip is not None and k in (0, first_half(n)):
                        strip_ready(strip, int(k > 0))
                    wh = whi[slot][:, k * W + c0:k * W + c0 + cw]
                    wl = wlo[slot][:, k * W + c0:k * W + c0 + cw]
                    M.matmul(dst, wh, acts[k][0], start=(first and k == 0), stop=False)
                    M.matmul(dst, wh, acts[k][1], start=False, stop=False)
                    mm = M.matmul(dst, wl, acts[k][0], start=False, stop=(last and k == n - 1))
                    if half_at is not None and k + 1 == half_at:
                        mm.then_inc(products_done, 1)
                return mm

            def bank_free(ph, b, n):
                if isinstance(n, int) and fill(ph, b) + n == 0:
                    return
                pe.wait_ge(evac[b], fill(ph, b) + n)

            def two_tiles(ph, s, par, n, acts, ready=None):
                if ready is not None:
                    for j in range(2):
                        bank_free(ph, par * 2 + j, n)
                    for k in range(len(acts)):
                        if k in (0, first_half(len(acts))):
                            strip_ready(s, int(k > 0))
                        pe.wait_ge(ready[0], ready[1] + k)
                        for j in range(2):
                            dst, c0 = bank[par * 2 + j][:, :], k * 256 + j * P
                            wh, wl = whi[par][:, c0:c0 + P], wlo[par][:, c0:c0 + P]
                            M.matmul(dst, wh, acts[k][0], start=(k == 0), stop=False)
                            M.matmul(dst, wh, acts[k][1], start=False, stop=False)
                            mm = M.matmul(dst, wl, acts[k][0], start=False, stop=(k == len(acts) - 1))
                            if k == len(acts) - 1:
                                mm.then_inc(products_done, 1)
                    return
                for j in range(2):
                    b = par * 2 + j
                    bank_free(ph, b, n)
                    product(bank[b][:, :], par, 256, j * P, P, acts, strip=s if j == 0 else None)\
                        .then_inc(products_done, 1)

            def out_product(ph, acts, ready):
                pe.wait_ge(ready, 16)
                with pe.Fori(0, 2) as i:
                    for nn in range(2):
                        for half in range(2):
                            s = STRIP0[ph] + i * 4 + nn * 2 + half
                            for j in range(2):
                                b = nn * 2 + j
                                if half == 0:
                                    bank_free(ph, b, i)
                                product(bank[b][:, :], half, 256, j * P, P, acts[half * 8:half * 8 + 8],
                                        first=(half == 0), last=(half == 1), strip=s if j == 0 else None)\
                                    .then_inc(products_done, 1)

            pe.wait_ge(sem("consts"), 1)
            pe.wait_ge(sem("x_loaded"), 16)
            for d in range(DT):
                if d >= 2:
                    pe.wait_ge(sem("xt.taken"), d - 1)
                for t in range(4):
                    mm = M.transpose(bank[5 + d % 2][:, t * P:(t + 1) * P],
                                     xin[:, t * D + d * P:t * D + (d + 1) * P], ident[:, :])
                mm.then_inc(sem("xt.t"), 1)
            pe.wait_ge(sem("vec_loaded"), 16 * VEC_DMAS)
            for t in range(VEC_TILES):
                mm = M.transpose(bank[4][:, t * P:(t + 1) * P], vecrow[:, t * P:(t + 1) * P], ident[:, :])
            mm.then_inc(sem("vec.t"), 1)

            pe_norm(pe, "n_pool", DT)
            pool_acts = [(tile(poolH, k), tile(poolL, k)) for k in range(4)]
            for g in range(4):
                s0 = STRIP0["pool"] + g * 6
                for j in range(4):
                    two_tiles("pool", s0 + j, j % 2, 3 * g + j // 2, h_out,
                              ready=(sem("norm.lo"), NORM0["n_pool"]["lo"] + 1) if g == 0 and j == 0 else None)
                for j in range(2):
                    two_tiles("pool", s0 + 4 + j, j, 3 * g + 2, pool_acts,
                              ready=(sem("pool.lo"), 4 * g + 1) if j == 0 else None)
            out_product("pool_out", [(tile(y1H, k), tile(y1L, k)) for k in range(16)], sem("pool.ylo"))

            pe_norm(pe, "n_mla", DT)
            for j in range(4):
                s, par, w = STRIP0["lat"] + j, j % 2, LAT[j][1]
                ready = (sem("norm.lo"), NORM0["n_mla"]["lo"] + 1) if j == 0 else None
                if w == 256:
                    two_tiles("lat", s, par, 0, h_out, ready=ready)
                    continue
                bank_free("lat", par * 2, 1)
                product(bank[par * 2][0:w, :], par, w, 0, w, h_out, half_at=1, strip=s).then_inc(products_done, 1)
            two_tiles("mz", STRIP0["mz"], 0, 0, h_out)
            pe_norm(pe, "n_q", 3)
            two_tiles("mz", STRIP0["mz"] + 1, 1, 0, h_out)
            pe_norm(pe, "n_kv", 2)
            with pe.Fori(1, 4) as i:
                for j in range(2):
                    two_tiles("mz", STRIP0["mz"] + i * 2 + j, j, i, h_out)
            pe.wait_ge(sem("norm.lo"), NORM0["n_q"]["lo"] + 3)
            pe.wait_ge(sem("norm.lo"), NORM0["n_kv"]["lo"] + 2)
            pe.wait_ge(sem("krope"), 1)
            kv_acts, q_acts = lat_out[3:5], lat_out[0:3]
            score_bank, turn_bank, out_bank = (bank[4], bank[5], bank[0]), (bank[6], bank[1]), (bank[2], bank[7])
            with pe.Fori(0, 8) as i:
                sq_ = STRIP0["heads"] + i * 2
                strip_ready(sq_, 0)
                for h in range(2):
                    bank_free("heads", h, i * 2)
                    mm = product(bank[h][:, :], 0, 2 * NOPE, h * NOPE, P, q_acts)
                mm.then_inc(products_done, 1)
                bank_free("heads", 2, i * 2)
                strip_ready(sq_, 1)
                for k in range(3):
                    r0 = 3 * 2 * NOPE + k * 2 * ROPE
                    wr = [w[0][:, r0:r0 + 2 * ROPE] for w in (whi, wlo)]
                    M.matmul(bank[2][:, :], wr[0], q_acts[k][0], start=(k == 0), stop=False)
                    M.matmul(bank[2][:, :], wr[0], q_acts[k][1], start=False, stop=False)
                    mm = M.matmul(bank[2][:, :], wr[1], q_acts[k][0], start=False, stop=(k == 2))
                mm.then_inc(products_done, 1)
                for h, b, n in ((0, 3, i * 2), (1, 0, i * 2 + 1)):
                    bank_free("heads", b, n)
                    mm = product(bank[b][:, :], 1, 512, h * 256, P, kv_acts, strip=sq_ + 1 if h == 0 else None)
                mm.then_inc(products_done, 1)
                for b in (1, 2):
                    bank_free("heads", b, i * 2 + 1)
                    for t in range(2):
                        blk = (b - 1) * 2 + t
                        dst = bank[b][:, t * 256:(t + 1) * 256]
                        for k in range(2):
                            wv = [w[1][:, k * 512:(k + 1) * 512].rearrange("p (h c) -> p h c", h=2)[:, :, P:2 * P]
                                  for w in (whi, wlo)]
                            ah, al = [x[:, blk * P:(blk + 1) * P] for x in kv_acts[k]]
                            M.matmul(dst, ah, wv[0], start=(k == 0), stop=False)
                            M.matmul(dst, ah, wv[1], start=False, stop=False)
                            mm = M.matmul(dst, al, wv[0], start=False, stop=(k == 1))
                mm.then_inc(products_done, 1)
                pe.wait_ge(evac[3], fill("heads", 3) + i * 2 + 1)
                pe.wait_ge(evac[0], fill("heads", 0) + i * 2 + 2)
                pe.wait_ge(sem("qrope"), i + 1)

                def scores(u):
                    h, qb = u // 4, u % 4
                    w = (qb + 1) * P
                    if u >= 3:
                        pe.wait_ge(sem("m.exp"), i * 8 + u - 2)
                    dst = score_bank[u % 3]
                    M.matmul(dst[:, 0:w], qT[:, h * S + qb * P:h * S + (qb + 1) * P], kT[:, h * S:h * S + w],
                             start=True, stop=False)
                    M.matmul(dst[:, 0:w], qrope[h * 64:h * 64 + 64, qb * P:(qb + 1) * P],
                             krope[h * 64:h * 64 + 64, 0:w], start=False, stop=True)
                    M.matmul(dst[:, qb * P:w], ident_b[:, :], neg_causal, start=False, stop=True, skip_group_check=True)\
                        .then_inc(sem("m.s"), 1)

                def turned(u):
                    h, qb = u // 4, u % 4
                    pe.wait_ge(sem("m.p"), i * 8 + u + 1)
                    if u == 1:
                        pe.wait_ge(evac[1], fill("heads", 1) + i * 2 + 2)
                    if u >= 2:
                        pe.wait_ge(sem("m.te"), i * 8 + u - 1)
                    for kb in range(qb + 1):
                        mm = M.transpose(turn_bank[u % 2][:, kb * P:(kb + 1) * P], prob[u % 3][:, kb * P:(kb + 1) * P],
                                         ident[:, :])
                    mm.then_inc(sem("m.t"), 1)

                def values(h):
                    pe.wait_ge(sem("m.te"), i * 8 + 4 * h + 4)
                    if h == 0:
                        pe.wait_ge(evac[2], fill("heads", 2) + i * 2 + 2)
                    else:
                        pe.wait_ge(sem("m.y"), i * 2 + 1)
                    for kb in range(4):
                        mm = M.matmul(out_bank[h][:, kb * P:S], vN[:, kb * 256 + h * VD:kb * 256 + (h + 1) * VD],
                                      probT[:, kb * S + kb * P:(kb + 1) * S], start=(kb == 0), stop=(kb == 3))
                    mm.then_inc(sem("m.o"), 1)

                scores(0)
                scores(1)
                for u in range(8):
                    if u + 2 < 8:
                        scores(u + 2)
                    if u == 4:
                        values(0)
                    turned(u)
                values(1)
                pe.wait_ge(sem("ada.acc"), i * ADA_N + (ADA_N + 3))
                bank_free("heads", 3, i * 2 + 1)
                for t in range(6):
                    mm = M.matmul(bank[3][:, t:t + 1], adaacc[:, t * P:(t + 1) * P], ones[:, 0:1],
                                  start=True, stop=True)
                mm.then_inc(sem("ada.col"), 1)
            out_product("mla_out", [(y2H[:, k * S:(k + 1) * S], tile(y2L, k)) for k in range(16)], sem("m.lo"))

            pe_norm(pe, "n_fin", 2 * DT)
            token_sums(6, hf)
            pe_factors(pe, "n_fin")
            pe_factors(pe, "n_1")
            units_before = 0
            for g in range(3):
                sg = STRIP0["att"] + g * 6
                for kind in range(2):
                    for j in range(2):
                        two_tiles("att", sg + kind * 2 + j, j, 3 * g + kind, h_out,
                                  ready=(sem("norm.lo"), NORM0["n_1"]["lo"] + 1) if g == 0 and kind == 0 and j == 0 else None)
                for j in range(2):
                    strip_ready(sg + 4 + j, 1)
                    for hv in range(2):
                        b = j * 2 + hv
                        bank_free("att", b, 3 * g + 2)
                        for t in range(2):
                            blk = hv * 2 + t
                            dst = bank[b][:, t * 256:(t + 1) * 256]
                            for k in range(DT):
                                if g == 0:
                                    ah, al = [x[:, blk * P:(blk + 1) * P] for x in h_out[k]]
                                else:
                                    ah, al = [x[:, blk:S:4] for x in h_out[k]]
                                wh, wl = whi[j][:, k * 256:(k + 1) * 256], wlo[j][:, k * 256:(k + 1) * 256]
                                M.matmul(dst, ah, wh, start=(k == 0), stop=False)
                                M.matmul(dst, ah, wl, start=False, stop=False)
                                mm = M.matmul(dst, al, wh, start=False, stop=(k == DT - 1))
                        mm.then_inc(products_done, 1)
                for b in range(4):
                    pe.wait_ge(evac[b], fill("att", b) + 3 * g + 3)
                pe.wait_ge(sem("att.vz"), 1)
                units = att_units(g)

                def scores(u):
                    h, blocks = units[u]
                    U = units_before + u
                    if U >= 2:
                        pe.wait_ge(sem("att.exp"), U - 1)
                    dst, rows = bank[4 + U % 2], slice((h % 2) * 64, (h % 2) * 64 + 64)
                    for qb, kb0, nk, c0 in att_rows(blocks):
                        w = nk * P
                        mask = neg_dil[:, :] if g == 2 else neg_band[:, (2 - nk) * P:2 * P]
                        base = (h // 2) * S
                        M.matmul(dst[:, c0:c0 + w], aq[rows, base + qb * P:base + (qb + 1) * P],
                                 ak[rows, base + kb0 * P:base + kb0 * P + w], start=True, stop=False)
                        mm = M.matmul(dst[:, c0:c0 + w], ident_b[:, :], mask, start=False, stop=True)
                    mm.then_inc(sem("att.s"), 1)

                def turned(u):
                    U = units_before + u
                    pe.wait_ge(sem("att.exp"), U + 1)
                    if U >= 1:
                        pe.wait_ge(sem("att.te"), U)
                    for n in range(len(units[u][1])):
                        mm = M.transpose(bank[6][:, n * P:(n + 1) * P], ap_[U % 2][:, n * P:(n + 1) * P],
                                         ident[:, :])
                    mm.then_inc(sem("att.t"), 1)

                def values(u):
                    h, blocks = units[u]
                    U = units_before + u
                    first = h % 2 == 0 and (u == 0 or units[u - 1][0] != h)
                    pe.wait_ge(sem("att.te"), U + 1)
                    if first and 4 * g + h // 2 > 0:
                        pe.wait_ge(sem("att.num"), 4 * g + h // 2)
                    for n, (qb, kb) in enumerate(blocks):
                        v0 = (kb * ATT_HEADS + h) * P
                        mm = M.matmul(bank[7][:, qb * P:(qb + 1) * P], av[:, v0:v0 + P],
                                      apT[U % 2][:, n * P:(n + 1) * P], start=(first and n == 0), stop=True,
                                      skip_group_check=True)
                    mm.then_inc(sem("att.pv"), 1)

                for u in range(len(units) + 2):
                    if u < len(units):
                        scores(u)
                    if 1 <= u <= len(units):
                        turned(u - 1)
                    if u >= 2:
                        values(u - 2)
                units_before += len(units)
            bank_free("lora", 0, 0)
            product(bank[0][:, :], 0, P, 0, P, h_out, half_at=1, strip=STRIP0["lora"])\
                .then_inc(products_done, 1)
            bank_free("lora", 2, 0)
            product(bank[2][:, :], 1, 160, 0, P, h_out, strip=STRIP0["lora"] + 1).then_inc(products_done, 1)
            bank_free("lora", 3, 0)
            product(bank[3][0:32, :], 1, 160, P, 32, h_out).then_inc(products_done, 1)
            def rkv_slice(p, n):
                z, k = divmod(n, DT)
                s0, slot, W, c0 = STRIP0["rkv"] + p * 2, z // 2, (256, 256, P)[z], z % 2 * P
                if k == 0:
                    bank_free("rkv", z, p)
                if z != 1 and k in (0, first_half(DT)):
                    strip_ready(s0 + slot, int(k > 0))
                wh, wl = [w[slot][:, k * W + c0:k * W + c0 + P] for w in (whi, wlo)]
                M.matmul(bank[z][:, :], wh, h_out[k][0], start=(k == 0), stop=False)
                M.matmul(bank[z][:, :], wh, h_out[k][1], start=False, stop=False)
                mm = M.matmul(bank[z][:, :], wl, h_out[k][0], start=False, stop=(k == DT - 1))
                if k == DT - 1 or (z == 2 and k == 0):
                    mm.then_inc(products_done, 1)

            for pr in range(4):
                for n in range(pr * 6, pr * 6 + 6):
                    rkv_slice(0, n)
                pe.wait_ge(sem("cmb.f"), (pr + 1) * 3)
                if pr >= 1:
                    pe.wait_ge(sem("cmb.used"), pr)
                for g in range(3):
                    for blk in range(4):
                        cs = slice(blk * P, (blk + 1) * P)
                        mm = M.transpose(bank[4 + g][:, cs], spread[g][:, cs], ident[:, :])
                mm.then_inc(sem("cmb.pe"), 1)

            pe.wait_ge(sem("lora.act"), 2)

            def lora_products(p):
                pe.wait_ge(sem("lw.ld"), (p + 1) * 32)
                for b in range(2):
                    pe.wait_ge(evac[b], p + (fill("rkv", b) + 1))
                M.matmul(bank[0][:, :], lw2[0:64, :], wlow[0:64, :], start=True, stop=True)
                M.matmul(bank[1][:, :], lw2[64:128, :], wlow[64:128, :], start=True, stop=True)\
                    .then_inc(sem("rk.lora"), 1)

            def key_norms(p):
                pe.wait_ge(sem("rk.sq"), p + 1)
                pe.wait_ge(evac[2], p + (fill("rkv", 2) + 1))
                M.matmul(bank[2][:, :], same[64][:, :], tile(sq, 0), start=True, stop=True)\
                    .then_inc(sem("rk.ss"), 1)

            def turn(b, x, signal):
                for c in range(4):
                    mm = M.transpose(bank[b][:, c * P:(c + 1) * P], x[:, c * P:(c + 1) * P], ident[:, :])
                mm.then_inc(sem(signal), 1)

            def turn_v(p):
                pe.wait_ge(sem("rk.sig"), p + 1)
                pe.wait_ge(evac[2], p + (fill("rkv", 2) + 1))
                turn(0, vT, "rk.tv")

            def turn_b(p):
                pe.wait_ge(sem("rk.ab"), p + 1)
                turn(1, bT, "rk.tb")

            def turn_k(p):
                pe.wait_ge(sem("rk.te"), p * 3 + 1)
                pe.wait_ge(sem("rk.kr"), p + 1)
                turn(0, kkT, "rk.tk")

            def bonus_sums(p):
                pe.wait_ge(sem("rk.nr"), p + 1)
                pe.wait_ge(sem("rk.bon"), p + 1)
                M.matmul(bank[2][:, :], same[64][:, :], Rr[:, :], start=True, stop=True)\
                    .then_inc(sem("rk.bs"), 1)

            def grams(p, par, follows):
                if follows:
                    pe.wait_ge(sem("gn.s"), p)
                for q in range(0, 10, 2):
                    if q >= 4:
                        pe.wait_ge(sem("rk.ge"), p * 10 + (q - 2))
                    _, left, right = gram_list()[q]
                    L, R = [{"a": aT[par], "b": bT, "k": kkT, "r": rT[par]}[x] for x in (left, right)]
                    for c in range(4):
                        cs = slice(c * P, (c + 1) * P)
                        for h in range(2):
                            rows = slice(h * 64, h * 64 + 64)
                            mm = M.matmul(bank[4 + (q + h) % 4][:, cs], L[rows, cs], R[rows, cs],
                                          start=True, stop=True)
                    mm.then_inc(sem("rk.gram"), 2)

            def inverse(p, more):
                tiles = {"D": IN4, "N4": IN4, "Z": IN4, "DA": IA4, "A4": IA4, "N2": IA8, "A8": IA8,
                         "A2": IE, "E": IE, "U": IU, "W": IW}
                if more:
                    pe.wait_ge(sem("rk.te"), p * 3 + 3)
                    pe.wait_ge(sem("rk.bonus"), p + 1)
                done = 4 if more else 0
                for n in range(done):
                    rkv_slice(p + 1, n)
                pe.wait_ge(sem("rk.ge"), p * 10 + 10)
                for k, step in enumerate(INVERSE):
                    for h in range(2):
                        if INV_ACT[k]:
                            pe.wait_ge(sem(f"inv{h}.act"), p * INV_ACT[-1] + INV_ACT[k])
                        pe.wait_ge(sem(f"inv{h}.dve"), p * INV_DVE[-1] + INV_DVE[k])
                        for which, (left, right, _, _, part) in enumerate(step["mm"]):
                            for c in range(4):
                                cs = slice(c * P, (c + 1) * P)
                                dst = columns(bank[4 + 2 * h + which][:, cs], part)
                                if right == "I":
                                    mm = M.transpose(dst, tiles[left][h][:, cs], ident[:, :])
                                else:
                                    mm = M.matmul(dst, tiles[left][h][:, cs], columns(tiles[right][h][:, cs], part),
                                                  start=True, stop=True)
                        mm.then_inc(sem(f"inv{h}.pe"), 1)
                    if more:
                        upto = 4 + 20 * (k + 1) // len(INVERSE)
                        for n in range(done, upto):
                            rkv_slice(p + 1, n)
                        done = upto
                for h in range(2):
                    pe.wait_ge(sem(f"inv{h}.dve"), p * INV_DVE[-1] + INV_DVE[-1])

            def right_side(p, par, c):
                cs = slice(c * P, (c + 1) * P)
                if c > 0:
                    pe.wait_ge(sem("sq.st"), p * 3 + c)
                    M.matmul(bank[4][:, 0:P], aT[par][:, cs], state[:, :], start=True, stop=True)
                for h in range(2):
                    mm = M.matmul(bank[4][:, h * 64:h * 64 + 64], Gak[h][:, cs],
                                  vpad[par][:, c * 256 + h * 192:c * 256 + h * 192 + 64],
                                  start=(c == 0), stop=True, skip_group_check=True)
                mm.then_inc(sem("sq.r"), 1)
                if c > 0:
                    M.matmul(bank[7][:, cs], state[:, :], rT[par][:, cs], start=False, stop=True,
                             skip_group_check=True)
                for h in range(2):
                    M.matmul(bank[7][:, cs], vpad[par][:, c * 256 + h * P:c * 256 + (h + 1) * P], Gqk[h][:, cs],
                             start=(c == 0 and h == 0), stop=True, skip_group_check=True)

            def solution(p, c):
                cs = slice(c * P, (c + 1) * P)
                pe.wait_ge(sem("sq.re"), p * 4 + c + 1)
                for h in range(2):
                    mm = M.matmul(bank[5][:, h * 64:h * 64 + 64], IU[h][:, cs], rhs[:, h * 64:h * 64 + 64],
                                  start=True, stop=True)
                mm.then_inc(sem("sq.sa"), 1)

            def state_result(p, par, c):
                cs = slice(c * P, (c + 1) * P)
                pe.wait_ge(sem("sq.se"), p * 4 + c + 1)
                if c < 3:
                    M.matmul(bank[6][:, 0:64], bN[par][:, cs], sapad[:, 0:64], start=True, stop=True,
                             skip_group_check=True)
                    M.matmul(bank[6][:, 64:P], bN[par][:, cs], sapad[:, 192:256], start=False, stop=True,
                             skip_group_check=True)
                    for h in range(2):
                        mm = M.matmul(bank[6][:, h * 64:h * 64 + 64], kN[par][:, cs],
                                      vpad[par][:, c * 256 + h * 192:c * 256 + h * 192 + 64],
                                      start=False, stop=True, skip_group_check=True)
                    if c > 0:
                        mm = M.matmul(bank[6][:, 0:P], ident[:, :], state[:, :], start=False, stop=True,
                                      skip_group_check=True)
                    mm.then_inc(sem("sq.s"), 1)
                for h in range(2):
                    mm = M.matmul(bank[7][:, cs], sapad[:, h * P:(h + 1) * P], Gqb[h][:, cs], start=False,
                                  stop=True, skip_group_check=True)
                if c == 3:
                    mm.then_inc(sem("sq.y"), 1)

            def gate(p):
                pe.wait_ge(sem("lg.ld"), (p + 1) * 32)
                pe.wait_ge(sem("rk.y"), p + 1)
                M.matmul(bank[3][:, :], lg2[:, 0:P], tile(glow, 0), start=True, stop=False)
                M.matmul(bank[3][:, :], lg2[0:32, P:2 * P], glow[0:32, S:2 * S], start=False, stop=True)\
                    .then_inc(sem("rk.g"), 1)

            def means(p, par):
                pe.wait_ge(sem("gn.y"), p + 1)
                M.matmul(bank[4][:, :], same[64][:, :], aT[par][:, :], start=True, stop=True).then_inc(sem("gn.m"), 1)

            def variances(p, par):
                pe.wait_ge(sem("gn.q"), p + 1)
                M.matmul(bank[5][:, :], same[64][:, :], kN[par][:, :], start=True, stop=True).then_inc(sem("gn.v"), 1)

            def pair(p, par, follows, more):
                grams(p, par, follows)
                inverse(p, more)
                right_side(p, par, 0)
                solution(p, 0)
                state_result(p, par, 0)
                if more:
                    lora_products(p + 1)
                right_side(p, par, 1)
                if more:
                    key_norms(p + 1)
                solution(p, 1)
                state_result(p, par, 1)
                right_side(p, par, 2)
                if more:
                    turn_v(p + 1)
                solution(p, 2)
                state_result(p, par, 2)
                right_side(p, par, 3)
                solution(p, 3)
                state_result(p, par, 3)
                means(p, par)
                gate(p)
                if more:
                    turn_b(p + 1)
                variances(p, par)
                if more:
                    turn_k(p + 1)
                    bonus_sums(p + 1)

            lora_products(0)
            key_norms(0)
            turn_v(0)
            turn_b(0)
            turn_k(0)
            bonus_sums(0)
            pe.wait_ge(sem("rk.zero"), 1)
            pair(0, 0, False, True)
            with pe.Fori(0, (PAIRS - 2) // 2) as j:
                pair(j * 2 + 1, 1, True, True)
                pair(j * 2 + 2, 0, True, True)
            pair(PAIRS - 1, 1, True, False)

            at_acts = [(tile(atH, k), tile(atL, k)) for k in range(4)]
            r_acts = [(tile(rH, k), tile(rL, k)) for k in range(PAIRS)]
            mix_acts = [(tile(mixH, k), tile(mixL, k)) for k in range(DT)]
            with pe.Fori(0, 4) as i:
                s0 = STRIP0["mix"] + i * 4
                two_tiles("mix", s0, 0, i * 2, h_out)
                pe.wait_ge(sem("rk.y"), 1 + PAIRS)
                two_tiles("mix", s0 + 1, 1, i * 2, h_out)
                pe.wait_ge(sem("mx.lo"), 12)
                two_tiles("mix", s0 + 2, 0, i * 2 + 1, at_acts)
                two_tiles("mix", s0 + 3, 1, i * 2 + 1, r_acts)
            pe.wait_ge(sem("mx.lo2"), 1 + DT)
            with pe.Fori(0, 2) as i:
                for j in range(2):
                    two_tiles("wo", STRIP0["wo"] + i * 2 + j, j, i, mix_acts)

            pe_norm(pe, "n_2", DT)
            with pe.Fori(0, 11) as i:
                for j in range(2):
                    two_tiles("up", STRIP0["up"] + i * 2 + j, j, i, h_out,
                              ready=(sem("norm.lo"), NORM0["n_2"]["lo"] + 1) if j == 0 else None)
            pe.wait_ge(sem("up.lo"), FT)
            with pe.Fori(0, 2) as i:
                for nn in range(2):
                    for kk_ in range(3):
                        j6 = nn * 3 + kk_
                        k0 = sum(DOWN_K[:kk_])
                        acts = [(tile(fH, k), tile(fL, k)) for k in range(k0, k0 + DOWN_K[kk_])]
                        for j in range(2):
                            b = nn * 2 + j
                            if kk_ == 0:
                                bank_free("down", b, i)
                            product(bank[b][:, :], j6 % 2, 256, j * P, P, acts, first=(kk_ == 0),
                                    last=(kk_ == 2), strip=STRIP0["down"] + i * 6 + j6 if j == 0 else None)\
                                .then_inc(products_done, 1)
            pe_norm(pe, "n_out", DT)
            for q in range(8):
                t, half = q // 2, q % 2
                if q >= 2:
                    pe.wait_ge(sem("fin.out"), q - 1)
                for d in range(4):
                    if q < 2:
                        pe.wait_ge(sem("norm.hf"), NORM0["n_out"]["hf"] + half * 4 + d + 1)
                    mm = M.transpose(bank[4 + q % 2][:, d * P:(d + 1) * P],
                                     xT[:, (half * 4 + d) * S + t * P:(half * 4 + d) * S + (t + 1) * P], ident[:, :])
                mm.then_inc(sem("fin.t"), 1)

        @block.scalar
        def _(act):
            act.wait_ge(sem("vecrow_zero"), 1)
            for row, n, w, src in vec_dmas:
                c0 = row // P * P
                act.dma_start(vecrow[row % P:row % P + n, c0:c0 + w], src).then_inc(sem("vec_loaded"), 16)

            def product_ready(s, half):
                act.wait_ge(products_done, done_value(s, half))

            act_norm(act, "n_pool", xt, D, lambda e, d: e.wait_ge(sem("xt.taken"), d + 1), h_out)
            for g in range(4):
                s0 = STRIP0["pool"] + 6 * g
                for t in range(4):
                    n = 4 * g + t
                    if n >= 2:
                        act.wait_ge(sem("pool.win"), n - 1)
                    product_ready(s0 + t // 2, t % 2)
                    A.copy(upad[n % 2][:, PAD:PAD + S], bank[t][:, :]).then_inc(evac[t], 1)
                for t in range(4):
                    if g >= 1:
                        act.wait_ge(evac[t], 3 * g)
                    product_ready(s0 + 2 + t // 2, t % 2)
                    A.activation(tile(zp, t), bank[t][:, :], ACT.Silu).then_inc(evac[t], 1)

            act_norm(act, "n_mla", xt, D, lambda e, d: e.wait_ge(*out_tile_taken("pool_out", d)), h_out)
            act.wait_ge(sem("norm.lo"), NORM0["n_mla"]["lo"] + DT)
            act.dma_start(posi[:, :], a["positions"][0:1, :].partition_broadcast(P)).then_inc(sem("pos_loaded"), 16)
            act.dma_start(invf[:, :], a["inv_freq"]).then_inc(sem("pos_loaded"), 16)
            s0 = STRIP0["lat"]
            for t, (s, half, b) in enumerate(((0, 0, 0), (0, 1, 1), (1, 0, 2), (1, 1, 3), (2, 1, 0))):
                product_ready(s0 + s, half)
                A.copy(lat_t[t], bank[b][:, :]).then_inc(evac[b], 1)
            act.wait_ge(sem("trig.r"), 1)
            A.activation(sinT[:, :], tile(ang, 0), ACT.Sin).then_inc(sem("trig.s"), 1)
            A.activation(tile(ang, 1), tile(ang, 0), ACT.Sin, scale=0.5).then_inc(sem("trig.s"), 1)
            act.drain()
            act_norm(act, "n_q", lat_t[0:3], Q_RANK, lambda e, d: None, lat_out[0:3])
            act.drain()

            def take_z(i, j):
                for half in range(2):
                    product_ready(STRIP0["mz"] + i * 2 + j, half)
                    A.activation(dtile(zm, i * 4 + j * 2 + half), bank[j * 2 + half][:, :], ACT.Silu)\
                        .then_inc(evac[j * 2 + half], 1)

            act_squares(act, "n_kv", lat_t[3:5], lambda e, d: None)
            take_z(0, 0)
            act_rms(act, "n_kv", KV_RANK)
            act_upper(act, "n_kv", lat_out[3:5])
            take_z(0, 1)
            with act.Fori(1, 4) as i:
                for j in range(2):
                    take_z(i, j)
            act.wait_ge(sem("norm.lo"), NORM0["n_kv"]["lo"] + 2)
            act.wait_ge(sem("krope"), 1)
            score_bank, turn_bank = (bank[4], bank[5], bank[0]), (bank[6], bank[1])
            with act.Fori(0, 8) as i:
                sq_ = STRIP0["heads"] + i * 2
                product_ready(sq_, 0)
                for h in range(2):
                    A.copy(tile(qT, h), bank[h][:, :]).then_inc(evac[h], 1)
                product_ready(sq_ + 1, 0)
                for h, b in ((0, 3), (1, 0)):
                    A.activation(tile(kT, h), bank[b][:, :], ACT.Copy, scale=QK_SCALE).then_inc(evac[b], 1)
                product_ready(sq_ + 1, 1)
                for b in (1, 2):
                    A.copy(vN[:, (b - 1) * 512:b * 512], bank[b][:, :]).then_inc(evac[b], 1)

                def exponentials(u):
                    w, n = (u % 4 + 1) * P, u % 3
                    act.wait_ge(sem("m.max"), i * 8 + u + 1)
                    if u >= 3:
                        act.wait_ge(sem("m.t"), i * 8 + u - 2)
                    A.activation(prob[n][:, 0:w], score_bank[n][:, 0:w], ACT.Exp, bias=stat[:, n:n + 1],
                                 accum_out=stat[:, 3 + n:4 + n]).then_inc(sem("m.exp"), 1)

                def take_turned(u):
                    qb = u % 4
                    act.wait_ge(sem("m.t"), i * 8 + u + 1)
                    A.copy(probT[:, :].rearrange("p (k q) -> p k q", k=4)[:, 0:qb + 1, qb * P:(qb + 1) * P],
                           turn_bank[u % 2][:, 0:(qb + 1) * P].rearrange("p (k q) -> p k q", q=P))\
                        .then_inc(sem("m.te"), 1)

                def upper_part(h):
                    act.wait_ge(sem("m.y"), i * 2 + h + 1)
                    A.copy(dtile(y2H, i * 2 + h), dtile(zm, i * 2 + h)).then_inc(sem("m.hi"), 1)

                exponentials(0)
                exponentials(1)
                for u in range(8):
                    if u + 2 < 8:
                        exponentials(u + 2)
                    take_turned(u)
                    if u == 6:
                        upper_part(0)
                upper_part(1)
                act.wait_ge(sem("ada.col"), i + 2)
                A.copy(ada[:, ds(i * 6, 6)], bank[3][:, 0:6]).then_inc(evac[3], 1)

            act_squares(act, "n_fin", xt, lambda e, d: e.wait_ge(*out_tile_taken("mla_out", d)),
                        cols("final_norm", DT))
            act_rms(act, "n_fin", D)
            act.wait_ge(sem("fin.ms"), 1)
            act_rms(act, "n_1", D, ms4[:, :])
            act_upper(act, "n_1", h_out, [ada[:, d:d + 1] for d in range(DT)])
            act.wait_ge(sem("norm.lo"), NORM0["n_1"]["lo"] + DT)
            units_before = 0
            for g in range(3):
                sg = STRIP0["att"] + g * 6
                for kind, dst in ((0, aq), (1, ak)):
                    for t in range(4):
                        product_ready(sg + kind * 2 + t // 2, t % 2)
                        o, x = tile(dst, t), bank[t][:, :]
                        if g:
                            o, x = o.rearrange("p (b q) -> p b q", b=4), x.rearrange("p (q b) -> p b q", b=4)
                        A.activation(o, x, ACT.Copy, scale=ATT_DIM ** -0.5 if kind == 0 else 1.0)\
                            .then_inc(evac[t], 1)
                if g == 0:
                    act.wait_ge(sem("att.vz"), 1)
                av6 = av[:, :].rearrange("p (k r par c e) -> p k r par c e", k=4, r=4, par=2, c=2)
                for j in range(2):
                    for hv in range(2):
                        b = j * 2 + hv
                        product_ready(sg + 4 + j, hv)
                        x = bank[b][:, :].rearrange("p (k r par e) -> p k r par e", k=2, r=2, par=2)
                        for par in range(2):
                            cp = A.copy(av6[:, 2 * hv:2 * hv + 2, 2 * j:2 * j + 2, par, par, :], x[:, :, :, par, :])
                        cp.then_inc(evac[b], 1)
                units = att_units(g)

                def take_pair(u):
                    h = units[u][0]
                    act.wait_ge(sem("att.pv"), units_before + u + 1)
                    A.copy(tile(num[g], h // 2), bank[7][:, :]).then_inc(sem("att.num"), 1)

                def pair_ends(u):
                    return units[u][0] % 2 == 1 and (u + 1 == len(units) or units[u + 1][0] != units[u][0])

                for u in range(len(units) + 2):
                    if u < len(units):
                        h, blocks = units[u]
                        U = units_before + u
                        act.wait_ge(sem("att.max"), U + 1)
                        if U >= 2:
                            act.wait_ge(sem("att.t"), U - 1)
                        for qb, kb0, nk, c0 in att_rows(blocks):
                            n = g * 32 + qb * ATT_HEADS + h
                            ex = A.activation(ap_[U % 2][:, c0:c0 + nk * P], bank[4 + U % 2][:, c0:c0 + nk * P],
                                              ACT.Exp, bias=nmax[:, n:n + 1], accum_out=den[:, n:n + 1])
                        ex.then_inc(sem("att.exp"), 1)
                    if u >= 2 and pair_ends(u - 2):
                        take_pair(u - 2)
                units_before += len(units)
            act.wait_ge(sem("att.exp"), units_before)
            act.wait_ge(sem("att.max"), units_before)
            nat = "(B p h) -> p B h"
            for n, x in enumerate((nmax, den)):
                act.dma_start(scratch[n].rearrange(nat, p=P, h=ATT_HEADS),
                              x[:, 0:32].rearrange("p (B h) -> p B h", h=ATT_HEADS)).then_inc(sem("st.out"), 16)
            act.wait_ge(sem("st.out"), 32)
            for n in range(2):
                act.dma_start(stq[:, n * 32:n * 32 + 32], scratch[n].rearrange("(q c) -> q c", q=P))\
                    .then_inc(sem("st.in"), 16)
            act.wait_ge(sem("st.d"), 1)
            A.activation(fac[:, :], fac[:, :], ACT.Exp).then_inc(sem("st.e"), 1)
            act.wait_ge(sem("st.f"), 1)
            act.dma_start(scratch[2].rearrange("(q c) -> q c", q=P), fac[:, 0:32]).then_inc(sem("st.out"), 16)
            act.wait_ge(sem("st.out"), 48)
            act.dma_start(fac0[:, :].rearrange("p (B h) -> p B h", h=ATT_HEADS),
                          scratch[2].rearrange(nat, p=P, h=ATT_HEADS)).then_inc(sem("st.f0"), 16)
            act.wait_ge(sem("st.f0"), 16)
            act.wait_ge(sem("att.pv"), units_before)
            for pr in range(4):
                if pr >= 1:
                    act.wait_ge(sem("cmb.pe"), pr)
                for g in range(3):
                    f = (fac0 if g == 0 else fac[:, 32 * g:32 * g + 32])[:, :]
                    f = f.rearrange("p (k h) -> p k h", k=4)[:, :, 2 * pr:2 * pr + 2]
                    A.copy(spread[g][:, :].rearrange("p (k h e) -> p k h e", k=4, h=2),
                           f.unsqueeze(3).to_broadcast([P, 4, 2, 64])).then_inc(sem("cmb.f"), 1)

            for b in (0, 2, 3):
                act.wait_ge(evac[b], fill("lora", b) + 1)
            A.activation(wlow[0:64, :], wlow[0:64, :], ACT.Tanh).then_inc(sem("lora.act"), 1)
            A.activation(tile(glow, 0), tile(glow, 0), ACT.Sigmoid)
            A.activation(glow[0:32, S:2 * S], glow[0:32, S:2 * S], ACT.Sigmoid).then_inc(sem("lora.act"), 1)

            def load_lora(p):
                for dst, src in ((lw2[0:64, :], a["w2_2"][0, :, ds(p * P, P)]),
                                 (lw2[64:128, :], a["a2_2"][0, :, ds(p * P, P)])):
                    act.dma_start(dst, src).then_inc(sem("lw.ld"), 16)

            def load_gate(p):
                act.wait_ge(sem("rk.g"), p + 1)
                for dst, src in ((lg2[:, 0:P], a["g2_2"][0, 0:P, ds(p * P, P)]),
                                 (lg2[0:32, P:2 * P], a["g2_2"][0, P:160, ds(p * P, P)])):
                    act.dma_start(dst, src).then_inc(sem("lg.ld"), 16)

            def key_squares(p):
                act.wait_ge(sem("rk.kk"), p + 1)
                A.activation(tile(sq, 0), kk[:, :], ACT.Square).then_inc(sem("rk.sq"), 1)

            def sigmoids(p, par):
                act.wait_ge(sem("rk.lora"), p + 1)
                A.activation(lwd[:, :], bank[0][:, :], ACT.Sigmoid, bias=pcol[par][:, 3:4])
                A.activation(aa[:, :], bank[1][:, :], ACT.Sigmoid, bias=pcol[par][:, 4:5]).then_inc(sem("rk.sig"), 1)

            def take_v(p, par):
                act.wait_ge(sem("rk.tv"), p + 1)
                vp = vpad[par][:, :].rearrange("p (c x) -> p c x", c=4)
                vb = bank[0][:, :].rearrange("p (c h e) -> p c h e", c=4, h=2)
                A.copy(vp[:, :, 0:64], vb[:, :, 0, :])
                A.copy(vp[:, :, 192:256], vb[:, :, 1, :]).then_inc(sem("rk.te"), 1)

            def key_lengths(p):
                act.wait_ge(sem("rk.ss"), p + 1)
                A.activation(tile(sq, 1), bank[2][:, :], ACT.Sqrt).then_inc(sem("rk.nr"), 1)

            def decays(p, par, part):
                if part == 0:
                    act.wait_ge(sem("rk.lp"), p + 1)
                    A.activation(epos[:, :], cc[:, :], ACT.Exp)
                elif part == 1:
                    A.activation(fade[par][:, 0:3], fade[par][:, 0:3], ACT.Exp)
                    A.activation(lwd[:, :], lwd[:, :], ACT.Exp)
                    act.drain()
                else:
                    A.activation(cc[:, :], cc[:, :], ACT.Exp, scale=-1.0).then_inc(sem("rk.ex"), 1)

            def take_b(p, par):
                act.wait_ge(sem("rk.tb"), p + 1)
                A.copy(bN[par][:, :], bank[1][:, :]).then_inc(sem("rk.te"), 1)

            def take_k(p, par):
                act.wait_ge(sem("rk.tk"), p + 1)
                A.copy(kN[par][:, :], bank[0][:, :]).then_inc(sem("rk.te"), 1)

            def take_inverse(p):
                goes = {"N2": IA8, "N4": IN4, "A4": IA4, "A8": IA8, "W": IW, "Z": IN4}
                for k, step in enumerate(INVERSE):
                    for h in range(2):
                        for which, (_, _, by, to, part) in enumerate(step["mm"]):
                            if by == "act":
                                act.wait_ge(sem(f"inv{h}.pe"), p * len(INVERSE) + k + 1)
                                A.copy(columns(goes[to][h][:, :], part), columns(bank[4 + 2 * h + which][:, :], part))\
                                    .then_inc(sem(f"inv{h}.act"), 1)

            def take_right_side(p, c):
                act.wait_ge(sem("sq.r"), p * 4 + c + 1)
                A.copy(rhs[:, :], bank[4][:, 0:P]).then_inc(sem("sq.re"), 1)

            def take_solution(p, c):
                act.wait_ge(sem("sq.sa"), p * 4 + c + 1)
                A.copy(sapad[:, 0:64], bank[5][:, 0:64])
                A.copy(sapad[:, 192:256], bank[5][:, 64:P]).then_inc(sem("sq.se"), 1)

            def take_state(p, par, c):
                act.wait_ge(sem("sq.s"), p * 3 + c + 1)
                A.activation(state[0:64, 0:64], bank[6][0:64, 0:64], ACT.Copy, scale=fade[par][0:64, c:c + 1])
                A.activation(state[64:P, 64:P], bank[6][64:P, 64:P], ACT.Copy, scale=fade[par][64:P, c:c + 1])\
                    .then_inc(sem("sq.st"), 1)

            def pair(p, par, more):
                nxt = 1 - par
                load_gate(p)
                if more:
                    load_lora(p + 1)
                take_inverse(p)
                take_right_side(p, 0)
                take_solution(p, 0)
                take_state(p, par, 0)
                if more:
                    key_squares(p + 1)
                    sigmoids(p + 1, nxt)
                take_right_side(p, 1)
                take_solution(p, 1)
                take_state(p, par, 1)
                if more:
                    key_lengths(p + 1)
                take_right_side(p, 2)
                take_solution(p, 2)
                if more:
                    take_v(p + 1, nxt)
                    decays(p + 1, nxt, 0)
                take_state(p, par, 2)
                if more:
                    decays(p + 1, nxt, 1)
                take_right_side(p, 3)
                take_solution(p, 3)
                if more:
                    decays(p + 1, nxt, 2)
                act.wait_ge(sem("sq.y"), p + 1)
                A.activation(aT[par][:, :], bank[7][:, :], ACT.Copy, scale=SCAN_SCALE ** -2).then_inc(sem("gn.y"), 1)
                if more:
                    take_b(p + 1, nxt)
                act.wait_ge(sem("gn.c"), p + 1)
                A.activation(kN[par][:, :], rT[par][:, :], ACT.Square).then_inc(sem("gn.q"), 1)
                act.wait_ge(sem("gn.v"), p + 1)
                A.activation(bN[par][:, :], bank[5][:, :], ACT.Sqrt, scale=1.0 / 64, bias=gneps_c[:, 0:1])\
                    .then_inc(sem("gn.s"), 1)
                if more:
                    take_k(p + 1, nxt)

            act.wait_ge(sem("att.at"), 4)
            load_lora(0)
            key_squares(0)
            sigmoids(0, 0)
            key_lengths(0)
            act.wait_ge(sem("rk.zero"), 1)
            take_v(0, 0)
            for part in range(3):
                decays(0, 0, part)
            take_b(0, 0)
            take_k(0, 0)
            pair(0, 0, True)
            with act.Fori(0, (PAIRS - 2) // 2) as j:
                pair(j * 2 + 1, 1, True)
                pair(j * 2 + 2, 0, True)
            pair(PAIRS - 1, 1, False)

            act.wait_ge(sem("rk.y"), 1 + PAIRS)
            act.wait_ge(sem("norm.lo"), NORM0["n_1"]["lo"] + DT)
            for k in range(12):
                src, dst = (tile(at, k), tile(atH, k)) if k < 4 else (tile(yr, k - 4), tile(rH, k - 4))
                A.copy(dst, src).then_inc(sem("mx.hi"), 1)
            with act.Fori(0, 4) as i:
                s0 = STRIP0["mix"] + i * 4
                for j, buf in enumerate((sq, hf)):
                    for half in range(2):
                        act.wait_ge(sem("mx.lo2"), i * 2 + 1)
                        product_ready(s0 + j, half)
                        A.activation(tile(buf, half), bank[2 * j + half][:, :], ACT.Sigmoid,
                                     bias=dcol("b_gate_2", i * 2 + (j * DT + half))).then_inc(evac[2 * j + half], 1)

            act_norm(act, "n_2", xt, D, lambda e, d: e.wait_ge(*out_tile_taken("wo", d)), h_out,
                     [ada[:, 3 * DT + d:3 * DT + d + 1] for d in range(DT)])
            act.wait_ge(sem("norm.lo"), NORM0["n_2"]["lo"] + DT)
            act.wait_ge(sem("up.zero"), 1)
            with act.Fori(0, 11) as i:
                s0 = STRIP0["up"] + i * 2
                for t in range(4):
                    act.wait_ge(sem("up.conv"), i * 4 + t + 1)
                    product_ready(s0 + t // 2, t % 2)
                    A.copy(cpad[t % 2][:, 2:2 + S], bank[t][:, :]).then_inc(evac[t], 1)
                    if t >= 2:
                        act.wait_ge(sem("up.conv"), i * 4 + t + 1)
                        A.activation(tile(sq, t - 2), tile(sq, t - 2), ACT.Silu).then_inc(sem("up.silu"), 1)
            act_norm(act, "n_out", xt, D, lambda e, d: e.wait_ge(*out_tile_taken("down", d)), [])
            for q in range(8):
                t, half = q // 2, q % 2
                act.wait_ge(sem("fin.t"), q + 1)
                if t >= 2:
                    act.wait_ge(sem(f"out_stored{t % 2}"), 16)
                A.copy(yout[t % 2][:, half * S:(half + 1) * S], bank[4 + q % 2][:, :]).then_inc(sem("fin.out"), 1)

        @block.vector
        def _(dve):
            def product_ready(s, half):
                dve.wait_ge(products_done, done_value(s, half))

            def split(hi, lo, x):
                V.tensor_copy(hi, x)
                dve.drain()
                return V.tensor_tensor(lo, x, f32(hi), ALU.subtract)

            dve.wait_ge(sem("consts"), 1)
            V.tensor_tensor(up16[:, :], upper1[:, :], same[16][:, :], ALU.mult)
            V.tensor_tensor(low16[:, :], lower1[:, :], same[16][:, :], ALU.mult)
            for n, wide in ((16, same[32]), (32, same[64]), (64, ones)):
                V.tensor_tensor(step_mask[n][:, :], wide[:, :], same[n][:, :], ALU.subtract)
            V.tensor_reduce(res4[:, :], ident[:, :].rearrange("p (k r) -> p r k", r=4), AX.X, ALU.add)
            V.tensor_tensor(tmp_mask[:, :], lower1[:, :], ident[:, :], ALU.add)
            V.tensor_copy(ident_b[:, :], ident[:, :])
            V.tensor_scalar(neg_band[:, P:2 * P], upper1[:, :], -BIG, None, ALU.mult)
            V.tensor_scalar(neg_band[:, 0:P], lower1[:, :], -BIG, None, ALU.mult)
            for g, w in enumerate(POOL_WINDOWS):
                V.tensor_scalar(cinv[:, g * PAD:(g + 1) * PAD], cinv[:, g * PAD:(g + 1) * PAD], float(w), None, ALU.min)
            dve.drain()
            V.reciprocal(cinv[:, :], cinv[:, :])
            for n in (16, 32, 64):
                V.tensor_tensor(step_mask[n][:, :], step_mask[n][:, :], lower1[:, :], ALU.mult)
            m4 = tmp_mask[:, :].rearrange("p (k r) -> p k r", r=4)
            V.tensor_tensor(m4, m4, res4[:, :].unsqueeze(1).to_broadcast([P, 32, 4]), ALU.mult)
            dve.drain()
            V.tensor_scalar(neg_dil[:, :], tmp_mask[:, :], BIG, -BIG, ALU.mult, ALU.add)
            for d in range(DT):
                dve.wait_ge(sem("xt.t"), d + 1)
                V.tensor_copy(xt[d], bank[5 + d % 2][:, :]).then_inc(sem("xt.taken"), 1)
            for d in range(DT):
                add_squares(dve, "n_pool", d)
            dve.wait_ge(sem("vec.t"), 1)
            V.tensor_copy(vec[:, :], bank[4][:, 0:VEC_ALL])
            dve.drain()
            m0 = VEC0["mu_shift_2"]
            V.tensor_scalar(one_minus_mu[:, :], vec[:, m0:m0 + 27], -1.0, 1.0, ALU.mult, ALU.add)
            V.tensor_scalar(one_minus_ka[:, :], vec[:, VEC0["k_a_2"]:VEC0["k_a_2"] + DT], -1.0, 1.0, ALU.mult, ALU.add)

            dve.drain()
            dve_norm(dve, "n_pool", xt, cols("pool_norm", DT), h_out, added=True)
            dve.drain()
            W_ = PAD + S
            tmp = [sq[:, 0:W_], hf[:, 0:W_]]
            for g, w in enumerate(POOL_WINDOWS):
                s0 = STRIP0["pool"] + 6 * g
                for t in range(4):
                    u = upad[t % 2]
                    dve.wait_ge(evac[t], 3 * g + 1)
                    cur = u[:, :]
                    for l in range(g + 1):
                        sh, nxt = 1 << l, tmp[l % 2]
                        V.tensor_tensor(nxt[:, 2 * sh - 1:W_], cur[:, 2 * sh - 1:W_], cur[:, sh - 1:W_ - sh], ALU.add)
                        dve.drain()
                        cur = nxt
                    mean = tmp[(g + 1) % 2][:, PAD:W_]
                    V.scalar_tensor_tensor(mean, cur[:, PAD:W_], 1.0 / w, u[:, PAD:W_], ALU.mult, ALU.subtract)
                    V.tensor_tensor(inv[:, 0:PAD], cur[:, PAD:2 * PAD], cinv[:, g * PAD:(g + 1) * PAD], ALU.mult)
                    dve.drain()
                    V.tensor_tensor(mean[:, 0:PAD], inv[:, 0:PAD], u[:, PAD:2 * PAD], ALU.subtract)\
                        .then_inc(sem("pool.win"), 1)
                    dve.drain()
                    if g >= 1 and t == 0:
                        product_ready(s0 - 1, 1)
                    split(tile(poolH, t), tile(poolL, t), mean).then_inc(sem("pool.lo"), 1)
                    dve.drain()
                for t in range(4):
                    product_ready(s0 + 4 + t // 2, t % 2)
                    dve.wait_ge(evac[t], 3 * g + 2)
                    y = tmp[t % 2][:, 0:S]
                    V.scalar_tensor_tensor(y, bank[t][:, :], col("pool_scale", 4 * g + t), tile(zp, t),
                                           ALU.mult, ALU.mult).then_inc(evac[t], 1)
                    dve.drain()
                    split(tile(y1H, 4 * g + t), tile(y1L, 4 * g + t), y).then_inc(sem("pool.ylo"), 1)
                    dve.drain()

            def residual(ph, strips, last, name, gate=None, squares=(None,)):
                for t in range(DT):
                    product_ready(STRIP0[ph] + t // 4 * 2 * strips + t // 2 % 2 * strips + last, t % 2)
                    b = t // 2 % 2 * 2 + t % 2
                    add = V.tensor_tensor(xt[t], bank[b][:, :], xt[t], ALU.add) if gate is None else \
                        V.scalar_tensor_tensor(xt[t], bank[b][:, :], ada[:, gate + t:gate + t + 1], xt[t],
                                               ALU.mult, ALU.add)
                    add.then_inc(evac[b], 1)
                    for d in [t - 1] * (t > 0) + [t] * (t == DT - 1):
                        for which in squares:
                            add_squares(dve, name, d, which)

            residual("pool_out", 2, 1, "n_mla")

            dve.drain()
            dve_norm(dve, "n_mla", xt, cols("mla_norm", DT), h_out, added=True)
            dve.wait_ge(sem("pos_loaded"), 32)
            a0_, a1_, a2_ = [tile(ang, n) for n in range(3)]
            V.tensor_copy(a0_, posi[:, :])
            dve.drain()
            V.tensor_scalar(a0_, a0_, invf[:, 0:1], None, ALU.mult)
            dve.drain()
            V.tensor_scalar(a1_, a0_, 1.0 / (2.0 * np.pi), ROUND, ALU.mult, ALU.add)
            dve.drain()
            V.tensor_scalar(a1_, a1_, ROUND, None, ALU.subtract)
            for part in TWO_PI:
                dve.drain()
                V.scalar_tensor_tensor(a0_, a1_, -part, a0_, ALU.mult, ALU.add)
            dve.drain()
            V.tensor_scalar(a0_, a0_, PI_IN, -PI_IN, ALU.min, ALU.max).then_inc(sem("trig.r"), 1)
            dve.wait_ge(sem("trig.s"), 2)
            V.tensor_tensor(cosT[:, :], a1_, a1_, ALU.mult)
            V.tensor_scalar(sinT[0:32, :], sinT[0:32, :], -1.0, None, ALU.mult)
            V.tensor_scalar(sinT[64:96, :], sinT[64:96, :], -1.0, None, ALU.mult)
            dve.drain()
            V.tensor_scalar(cosT[:, :], cosT[:, :], -2.0, 1.0, ALU.mult, ALU.add)
            dve.drain()

            def rotate(x, t, turned, rows):
                V.tensor_tensor(t, x[0:rows, :], cosT[0:rows, :], ALU.mult)
                for q in range(0, rows, 32):
                    o = q ^ 32
                    last = V.tensor_tensor(turned[q:q + 32, :], x[o:o + 32, :], sinT[q:q + 32, :], ALU.mult)
                return last

            product_ready(STRIP0["lat"] + 3, 1)
            rotate(bank[2], a2_[0:64, :], a1_, 64).then_inc(evac[2], 1)
            dve.drain()
            V.tensor_tensor(a2_[0:64, :], a2_[0:64, :], a1_[0:64, :], ALU.add)
            dve.drain()
            V.tensor_scalar(krope[0:64, :], a2_[0:64, :], QK_SCALE, None, ALU.mult)
            V.tensor_scalar(krope[64:128, :], a2_[0:64, :], QK_SCALE, None, ALU.mult).then_inc(sem("krope"), 1)
            dve.drain()
            dve_norm(dve, "n_q", lat_t[0:3], cols("mla_q_norm", 3), lat_out[0:3])
            dve.drain()
            dve_norm(dve, "n_kv", lat_t[3:5], cols("mla_kv_norm", 2), lat_out[3:5])
            dve.drain()
            score_bank, out_bank = (bank[4], bank[5], bank[0]), (bank[2], bank[7])
            with dve.Fori(0, 8) as i:
                def times_c(q):
                    dve.wait_ge(sem(f"ada.ld{q % 3}"), (i * (ADA_N // 3) + (q // 3 + 1)) * 16)
                    w = adaw[q % 3][:, 0:DT * ADA_W].rearrange("p (k n) -> p k n", k=DT)
                    c_cols = vec[:, VEC0["c_2"]:VEC0["c_2"] + DT].unsqueeze(2).to_broadcast([P, DT, ADA_W])
                    V.tensor_tensor(w, w, c_cols, ALU.mult).then_inc(sem("ada.c"), 1)

                times_c(0)
                times_c(1)
                times_c(2)
                dve.drain()
                product_ready(STRIP0["heads"] + i * 2, 1)
                rotate(bank[2], tile(sq, 0), tile(sq, 1), P).then_inc(evac[2], 1)
                dve.drain()
                V.tensor_tensor(qrope[:, :], tile(sq, 0), tile(sq, 1), ALU.add).then_inc(sem("qrope"), 1)

                def maximum(u):
                    w, n = (u % 4 + 1) * P, u % 3
                    dve.wait_ge(sem("m.s"), i * 8 + u + 1)
                    V.tensor_reduce(stat[:, n:n + 1], score_bank[n][:, 0:w], AX.X, ALU.max, negate=True)\
                        .then_inc(sem("m.max"), 1)

                def divide(u):
                    w, n = (u % 4 + 1) * P, u % 3
                    dve.wait_ge(sem("m.exp"), i * 8 + u + 1)
                    V.reciprocal(stat[:, 6 + n:7 + n], stat[:, 3 + n:4 + n])
                    dve.drain()
                    V.tensor_scalar(prob[n][:, 0:w], prob[n][:, 0:w], stat[:, 6 + n:7 + n], None, ALU.mult)\
                        .then_inc(sem("m.p"), 1)

                def gated(h):
                    dve.wait_ge(sem("m.o"), i * 2 + h + 1)
                    z = dtile(zm, i * 2 + h)
                    V.tensor_tensor(z, out_bank[h][:, :], z, ALU.mult).then_inc(sem("m.y"), 1)

                def lower_part(h):
                    dve.wait_ge(sem("m.hi"), i * 2 + h + 1)
                    V.tensor_tensor(dtile(y2L, i * 2 + h), dtile(zm, i * 2 + h), f32(dtile(y2H, i * 2 + h)),
                                    ALU.subtract).then_inc(sem("m.lo"), 1)

                maximum(0)
                maximum(1)
                for u in range(8):
                    if u != 6:
                        divide(u)
                    if u == 4:
                        times_c(3)
                        times_c(4)
                    if u == 5:
                        times_c(5)
                        divide(6)
                    if u + 2 < 8:
                        maximum(u + 2)
                    if u == 5:
                        gated(0)
                lower_part(0)
                gated(1)
                dve.drain()
                lower_part(1)
            dve.drain()
            dve.wait_ge(evac[3], fill("heads", 3) + 16)
            V.tensor_tensor(ada[:, :], ada[:, :], vec[:, VEC0["b_ada_2"]:VEC0["b_ada_2"] + 48], ALU.add)
            dve.drain()
            for gain, name, c0 in ((gain1, "norm1_w_2", DT), (gain2, "norm2_w_2", 4 * DT)):
                V.scalar_tensor_tensor(gain[:, :], ada[:, c0:c0 + DT], 1.0, vec[:, VEC0[name]:VEC0[name] + DT],
                                       ALU.add, ALU.mult)
            dve.drain()
            residual("mla_out", 2, 1, "n_fin", squares=(0, 1))
            dve_inverse(dve, "n_fin")
            dve.wait_ge(sem("norm.sum"), NORM0["n_fin"]["sum"] + 2)
            V.tensor_tensor(ms4[:, :], bank[6][:, 0:4], rms4[:, :], ALU.mult)
            dve.drain()
            V.tensor_tensor(ms4[:, :], ms4[:, :], rms4[:, :], ALU.mult).then_inc(sem("fin.ms"), 1)
            over_rms(dve, "n_fin")
            for d in range(DT):
                V.scalar_tensor_tensor(xt[d], xt[d], col("final_norm", d), bank[7][:, :], ALU.mult, ALU.mult)
            dve_inverse(dve, "n_1")
            dve.drain()
            dve_split(dve, "n_1", xt, [gain1[:, d:d + 1] for d in range(DT)], h_out,
                      [ada[:, d:d + 1] for d in range(DT)])
            dve.drain()
            V.memset(av[:, :], 0.0).then_inc(sem("att.vz"), 1)
            units_before = 0
            for g in range(3):
                units = att_units(g)

                def maxima(u):
                    h, blocks = units[u]
                    U = units_before + u
                    dve.wait_ge(sem("att.s"), U + 1)
                    rows = att_rows(blocks)
                    runs = [rows[:1], rows[1:]] if rows[0][2] != rows[-1][2] else [rows]
                    for run in runs:
                        qb, _, nk, c0 = run[0]
                        n = len(run)
                        x = bank[4 + U % 2][:, c0:c0 + n * nk * P].rearrange("p (n w) -> p n w", n=n)
                        m0 = g * 32 + qb * ATT_HEADS + h
                        last = V.tensor_reduce(nmax[:, m0:m0 + (n - 1) * ATT_HEADS + 1:ATT_HEADS], x, AX.X, ALU.max,
                                               negate=True)
                    last.then_inc(sem("att.max"), 1)

                def take_turned(u):
                    U = units_before + u
                    w = len(units[u][1]) * P
                    dve.wait_ge(sem("att.t"), U + 1)
                    if U >= 2:
                        dve.wait_ge(sem("att.pv"), U - 1)
                    V.tensor_copy(apT[U % 2][:, 0:w], bank[6][:, 0:w]).then_inc(sem("att.te"), 1)

                for u in range(len(units) + 1):
                    if u < len(units):
                        maxima(u)
                    if u >= 1:
                        take_turned(u - 1)
                units_before += len(units)
            dve.wait_ge(sem("st.in"), 32)
            negs = [stq[:, 0:32], nmax[:, 32:64], nmax[:, 64:96]]
            dens = [stq[:, 32:64], den[:, 32:64], den[:, 64:96]]
            facs = [fac[:, 32 * g:32 * g + 32] for g in range(3)]
            V.tensor_tensor(zden[:, :], negs[0], negs[1], ALU.min)
            dve.drain()
            V.tensor_tensor(zden[:, :], zden[:, :], negs[2], ALU.min)
            dve.drain()
            for g in range(3):
                last = V.tensor_tensor(facs[g], zden[:, :], negs[g], ALU.subtract)
            last.then_inc(sem("st.d"), 1)
            dve.wait_ge(sem("st.e"), 1)
            for g in range(3):
                V.tensor_tensor(dens[g], dens[g], facs[g], ALU.mult)
            dve.drain()
            V.tensor_tensor(zden[:, :], dens[0], dens[1], ALU.add)
            dve.drain()
            V.tensor_tensor(zden[:, :], zden[:, :], dens[2], ALU.add)
            dve.drain()
            V.reciprocal(zden[:, :], zden[:, :])
            dve.drain()
            for g in range(3):
                last = V.tensor_tensor(facs[g], facs[g], zden[:, :], ALU.mult)
            last.then_inc(sem("st.f"), 1)
            def shifted(z, mu_c, rest, out_, rows=P):
                V.tensor_scalar(out_, z[0:rows, :], rest, None, ALU.mult)
                dve.drain()
                return V.scalar_tensor_tensor(out_[:, 1:S], z[0:rows, 0:S - 1], mu_c, out_[:, 1:S], ALU.mult, ALU.add)

            mu = VEC0["mu_shift_2"]
            for n, (b, half, out_, rows) in enumerate(((0, (0, 1), wlow[:, :], P), (2, (1, 0), tile(glow, 0), P),
                                                       (3, (1, 1), glow[0:32, S:2 * S], 32))):
                product_ready(STRIP0["lora"] + half[0], half[1])
                shifted(bank[b], vec[0:rows, mu + 24 + n:mu + 25 + n], one_minus_mu[0:rows, 24 + n:25 + n], out_, rows).then_inc(evac[b], 1)
                dve.drain()

            dve.wait_ge(sem("att.num"), 12)
            for pr in range(4):
                dve.wait_ge(sem("cmb.pe"), pr + 1)
                n_ = [tile(num[g], pr) for g in range(3)]
                for g in range(3):
                    last = V.tensor_tensor(n_[g], n_[g], bank[4 + g][:, :], ALU.mult)
                last.then_inc(sem("cmb.used"), 1)
                dve.drain()
                V.tensor_tensor(n_[1], n_[1], n_[2], ALU.add)
                dve.drain()
                V.tensor_tensor(tile(at, pr).rearrange("p (q b) -> p b q", b=4), n_[1].rearrange("p (b q) -> p b q", b=4),
                                n_[0].rearrange("p (q b) -> p b q", b=4), ALU.add).then_inc(sem("att.at"), 1)
            dve.drain()

            def masked(dst, x, mask):
                m = mask[:, :].unsqueeze(1).to_broadcast([P, 4, P])
                return V.tensor_tensor(dst[:, :].rearrange("p (c t) -> p c t", c=4),
                                       x.rearrange("p (c t) -> p c t", c=4), m, ALU.mult)

            def decayed_keys(p, par, first=False):
                pc = pcol[par]
                V.tensor_copy(pc[:, 0:3], vec[:, mu:mu + 24].rearrange("p (j r) -> p j r", j=3)[:, :, ds(p, 1)])
                w0 = VEC0["w0_2"]
                V.tensor_copy(pc[:, 3:10], vec[:, w0:w0 + 56].rearrange("p (j r) -> p j r", j=7)[:, :, ds(p, 1)])
                V.tensor_copy(pc[:, 10:11], one_minus_ka[:, ds(p, 1)])
                V.tensor_copy(pc[:, 11:14], one_minus_mu[:, 0:24].rearrange("p (j r) -> p j r", j=3)[:, :, ds(p, 1)])
                dve.drain()
                s0 = STRIP0["rkv"] + p * 2
                for z, s, half, out_ in ((1, 0, 1, Kr), (0, 0, 0, Rr), (2, 1, 1, vT)):
                    product_ready(s0 + s, half)
                    shifted(bank[z], pc[:, z:z + 1], pc[:, 11 + z:12 + z], out_[:, :]).then_inc(evac[z], 1)
                    dve.drain()
                    if z == 1:
                        V.tensor_scalar(kk[:, :], Kr[:, :], pc[:, 5:6], None, ALU.mult).then_inc(sem("rk.kk"), 1)
                if first:
                    dve.wait_ge(sem("cmb.pe"), 4)
                    for b in range(2):
                        V.memset(vpad[b][:, :], 0.0)
                    V.memset(sapad[:, :], 0.0)
                    V.memset(state[:, :], 0.0).then_inc(sem("rk.zero"), 1)
                    dve.drain()
                dve.wait_ge(sem("rk.sig"), p + 1)
                V.tensor_scalar(lwd[:, :], lwd[:, :], -float(np.exp(-0.5)), None, ALU.mult)
                dve.drain()
                for c in range(4):
                    cs = slice(c * P, (c + 1) * P)
                    V.tensor_tensor_scan(cc[:, cs], ones[:, :], lwd[:, cs], 0.0, ALU.mult, ALU.add)
                dve.drain()
                c4 = cc[:, :].rearrange("p (c t) -> p c t", c=4)
                V.tensor_copy(mid[:, :], cc[:, CH - 1:S:P])
                dve.drain()
                V.tensor_tensor(c4, c4, mid[:, :].unsqueeze(2).to_broadcast([P, 4, P]), ALU.subtract)
                dve.drain()
                V.tensor_tensor(fade[par][:, 0:3], cc[:, P - 1:3 * P:P], mid[:, 1:4], ALU.add)
                V.tensor_tensor(lwd[:, :], cc[:, :], lwd[:, :], ALU.subtract).then_inc(sem("rk.lp"), 1)
                dve.wait_ge(sem("rk.nr"), p + 1)
                V.tensor_scalar(tile(sq, 1), tile(sq, 1), 1e-12, None, ALU.max)
                dve.drain()
                V.reciprocal(tile(sq, 1), tile(sq, 1))
                dve.drain()
                V.tensor_tensor(kk[:, :], kk[:, :], tile(sq, 1), ALU.mult)
                dve.drain()
                dve.wait_ge(sem("rk.ex"), p + 1)
                V.scalar_tensor_tensor(aT[par][:, :], kk[:, :], -1.0, lwd[:, :], ALU.mult, ALU.mult)
                V.tensor_tensor(bT[:, :], kk[:, :], aa[:, :], ALU.mult)
                dve.drain()
                V.tensor_tensor(bT[:, :], bT[:, :], cc[:, :], ALU.mult).then_inc(sem("rk.ab"), 1)

            def keys_and_bonus(p, par):
                pc = pcol[par]
                V.tensor_scalar(aa[:, :], aa[:, :], pc[:, 6:7], pc[:, 10:11], ALU.mult, ALU.add)
                dve.drain()
                V.tensor_tensor(Kr[:, :], Kr[:, :], aa[:, :], ALU.mult)
                dve.drain()
                V.scalar_tensor_tensor(kkT[:, :], Kr[:, :], SCAN_SCALE, cc[:, :], ALU.mult, ALU.mult)
                V.scalar_tensor_tensor(rT[par][:, :], Rr[:, :], SCAN_SCALE, epos[:, :], ALU.mult, ALU.mult)\
                    .then_inc(sem("rk.kr"), 1)
                dve.drain()
                V.scalar_tensor_tensor(Rr[:, :], Kr[:, :], pc[:, 7:8], Rr[:, :], ALU.mult, ALU.mult)\
                    .then_inc(sem("rk.bon"), 1)
                dve.wait_ge(sem("rk.bs"), p + 1)
                V.tensor_tensor(bonus[par][:, :], bank[2][:, :], vT[:, :], ALU.mult).then_inc(sem("rk.bonus"), 1)
                dve.drain()

            def finished(p, par, part):
                if part == 0:
                    dve.wait_ge(sem("gn.s"), p + 1)
                    V.reciprocal(bN[par][:, :], bN[par][:, :])
                elif part == 1:
                    V.scalar_tensor_tensor(aT[par][:, :], rT[par][:, :], pcol[par][:, 8:9], bN[par][:, :],
                                           ALU.mult, ALU.mult)
                elif part == 2:
                    V.scalar_tensor_tensor(aT[par][:, :], aT[par][:, :], pcol[par][:, 9:10], bonus[par][:, :],
                                           ALU.add, ALU.add)
                else:
                    dve.wait_ge(sem("rk.g"), p + 2)
                    V.tensor_tensor(dtile(yr, p), aT[par][:, :], bank[3][:, :], ALU.mult).then_inc(sem("rk.y"), 1)

            def pair(p, par, follows, more):
                for q, (h, left, right) in enumerate(gram_list()):
                    dve.wait_ge(sem("rk.gram"), p * 10 + q + 1)
                    x = bank[4 + q % 4][:, :]
                    if (left, right) == ("b", "a"):
                        last = masked(IN4[h], x, up16)
                    elif (left, right) == ("a", "b"):
                        masked(IA[h], x, lower1)
                        last = masked(IA4[h], x, low16)
                    elif right == "a":
                        last = masked(Gak[h], x, upper1)
                    else:
                        last = masked(Gqb[h] if left == "b" else Gqk[h], x, upper0)
                    last.then_inc(sem("rk.ge"), 1)
                dve.drain()
                for h in range(2):
                    V.tensor_tensor(IU[h].rearrange("p (c t) -> p c t", c=4),
                                    IN4[h][:, :].rearrange("p (c t) -> p c t", c=4),
                                    ident[:, :].unsqueeze(1).to_broadcast([P, 4, P]), ALU.add)\
                        .then_inc(sem(f"inv{h}.dve"), 1)
                for k, step in enumerate(INVERSE):
                    for h in range(2):
                        waited = False
                        for which, (_, _, by, to, part) in enumerate(step["mm"]):
                            if by != "dve":
                                continue
                            if not waited:
                                dve.drain()
                                dve.wait_ge(sem(f"inv{h}.pe"), p * len(INVERSE) + k + 1)
                                waited = True
                            x = columns(bank[4 + 2 * h + which][:, :], part)
                            if to == "A2":
                                last = V.tensor_copy(IE[h][:, :], x)
                            else:
                                dst = columns(IU[h] if to == "+U" else IW[h], part)
                                last = V.tensor_tensor(dst, x, dst, ALU.add)
                            last.then_inc(sem(f"inv{h}.dve"), 1)
                        if "E" in step:
                            masked(IE[h], IA[h][:, :], step_mask[step["E"]]).then_inc(sem(f"inv{h}.dve"), 1)
                    if follows and k in (1, 5, 7):
                        for part in {1: (0,), 5: (1, 2), 7: (3,)}[k]:
                            finished(p - 1, 1 - par, part)
                            dve.drain()
                if more:
                    decayed_keys(p + 1, 1 - par)
                dve.wait_ge(sem("gn.m"), p + 1)
                V.scalar_tensor_tensor(rT[par][:, :], bank[4][:, :], -1.0 / 64, aT[par][:, :], ALU.mult, ALU.add)\
                    .then_inc(sem("gn.c"), 1)
                if more:
                    keys_and_bonus(p + 1, 1 - par)

            decayed_keys(0, 0, first=True)
            keys_and_bonus(0, 0)
            pair(0, 0, False, True)
            with dve.Fori(0, (PAIRS - 2) // 2) as j:
                pair(j * 2 + 1, 1, True, True)
                pair(j * 2 + 2, 0, True, True)
            pair(PAIRS - 1, 1, True, False)
            for part in range(4):
                dve.drain()
                finished(PAIRS - 1, 1, part)
            dve.drain()

            for k in range(12):
                src, hi, lo = (tile(at, k), tile(atH, k), tile(atL, k)) if k < 4 else \
                    (tile(yr, k - 4), tile(rH, k - 4), tile(rL, k - 4))
                dve.wait_ge(sem("mx.hi"), k + 1)
                V.tensor_tensor(lo, src, f32(hi), ALU.subtract).then_inc(sem("mx.lo"), 1)
            dve.drain()
            with dve.Fori(0, 4) as i:
                s0 = STRIP0["mix"] + i * 4
                for half in range(2):
                    dve.wait_ge(evac[half], fill("mix", half) + i * 2 + 1)
                    product_ready(s0 + 2, half)
                    V.tensor_tensor(tile(sq, half), bank[half][:, :], tile(sq, half), ALU.mult).then_inc(evac[half], 1)
                for half in range(2):
                    b = 2 + half
                    dve.wait_ge(evac[b], fill("mix", b) + i * 2 + 1)
                    product_ready(s0 + 3, half)
                    V.tensor_tensor(tile(hf, half), bank[b][:, :], tile(hf, half), ALU.mult).then_inc(evac[b], 1)
                    dve.drain()
                    V.tensor_tensor(tile(sq, half), tile(sq, half), tile(hf, half), ALU.add)
                    dve.drain()
                    split(dtile(mixH, i * 2 + half), dtile(mixL, i * 2 + half), tile(sq, half))\
                        .then_inc(sem("mx.lo2"), 1)

            residual("wo", 1, 0, "n_2", 2 * DT)

            dve.drain()
            dve_norm(dve, "n_2", xt, [gain2[:, d:d + 1] for d in range(DT)], h_out,
                     [ada[:, 3 * DT + d:3 * DT + d + 1] for d in range(DT)], added=True)
            for b in range(2):
                last = V.memset(cpad[b][:, 0:2], 0.0)
            last.then_inc(sem("up.zero"), 1)
            dve.drain()
            cw, cb = VEC0["conv_w_2"], VEC0["conv_b_2"]
            with dve.Fori(0, 11) as i:
                for t in range(4):
                    n = i * 2 + (FT if t >= 2 else 0) + t % 2
                    u, acc = cpad[t % 2], tile(sq if t < 2 else hf, t % 2)
                    wt = [vec[:, ds(n + (cw + 2 * FT * j), 1)] for j in range(3)]
                    dve.wait_ge(evac[t], fill("up", t) + i + 1)
                    V.tensor_scalar(acc, u[:, 0:S], wt[0], vec[:, ds(n + cb, 1)], ALU.mult, ALU.add)
                    dve.drain()
                    V.scalar_tensor_tensor(acc, u[:, 1:S + 1], wt[1], acc, ALU.mult, ALU.add)
                    dve.drain()
                    V.scalar_tensor_tensor(acc, u[:, 2:S + 2], wt[2], acc, ALU.mult, ALU.add)\
                        .then_inc(sem("up.conv"), 1)
                    if t >= 2:
                        j = t - 2
                        dve.drain()
                        dve.wait_ge(sem("up.silu"), i * 2 + j + 1)
                        V.tensor_tensor(acc, acc, tile(sq, j), ALU.mult)
                        dve.drain()
                        split(dtile(fH, i * 2 + j), dtile(fL, i * 2 + j), acc).then_inc(sem("up.lo"), 1)
                dve.drain()
            residual("down", 3, 2, "n_out", 5 * DT)
            dve_inverse(dve, "n_out")
            over_rms(dve, "n_out")
            for d in range(DT):
                V.scalar_tensor_tensor(xt[d], xt[d], col("norm_f_w_2", d), bank[7][:, :], ALU.mult, ALU.mult)\
                    .then_inc(sem("norm.hf"), 1)


_INS = ["x", "positions", "pool_norm", "pool_w_in", "pool_w_group", "pool_scale", "pool_w_out", "mla_norm", "mla_w_in",
        "mla_q_norm", "mla_w_q_b", "mla_kv_norm", "mla_w_kv_b", "mla_w_out", "final_norm", "c_2", "w_ada_2", "b_ada_2",
        "norm1_w_2", "w_in_2", "b_gate_2", "mu_shift_2", "w0_2", "w2_2", "a0_2", "a2_2", "g2_2", "k_k_2", "k_a_2",
        "r_k_2", "lnx_w_2", "lnx_b_2", "w_att_out_2", "w_rwkv_out_2", "w_o_2", "norm2_w_2", "w_up_2", "conv_w_2",
        "conv_b_2", "w_down_2", "norm_f_w_2"]


def kernel(**inputs):
    import numpy as _np
    import concourse.bacc as _bacc
    from concourse import mybir as _mybir
    from concourse.bass_utils import run_bass_kernel_spmd as _run

    nc = _bacc.Bacc("TRN2", target_bir_lowering=False, num_devices=1)
    arrays = {name: _np.ascontiguousarray(inputs[name]) for name in _INS}
    freq = 1.0 / (_np.float32(ROPE_THETA) ** (_np.arange(0, ROPE, 2, dtype=_np.float32) / _np.float32(ROPE)))
    arrays["inv_freq"] = _np.tile(freq.astype(_np.float32), 4).reshape(P, 1)
    aps = {name: nc.dram_tensor(f"in_{name}", v.shape, _mybir.dt.from_np(v.dtype), kind="ExternalInput").ap()
           for name, v in arrays.items()}
    out = nc.dram_tensor("out", (1, S, D), F32, kind="ExternalOutput").ap()
    build(nc, aps, out)
    r = _run(nc, [{f"in_{name}": v for name, v in arrays.items()}], core_ids=[0])
    return r.results[0]["out"]
```
